# Optimizing a Trainium2 kernel written in Bass

```python
import jax
import jax.numpy as jnp
from jax import lax
import numpy as np

D_MODEL = 1024
BATCH = 1
SEQ = 256
DEPTH = 2
DEC_BATCH = 8
DEC_SEQ = 1
PAST_LEN = 256
PAGE_SIZE = 128

N_EVEN = (DEPTH + 1) // 2
N_ODD = DEPTH // 2

CONV_CH = D_MODEL // 2
CONV_W = 31
SB_HEADS = 8
SB_HEAD_DIM = 64
SB_WIDTH = SB_HEADS * SB_HEAD_DIM
EVEN_IN = 2 * CONV_CH + 3 * SB_WIDTH
EVEN_MIX = CONV_CH + SB_WIDTH
Q_BLOCK = 128
SB_BIAS_INIT = -6.0

RET_HEADS = 8
RET_DK = D_MODEL // RET_HEADS
RET_DV = 2 * RET_DK
RET_QK = RET_HEADS * RET_DK
RET_V = RET_HEADS * RET_DV
ODD_IN = 2 * RET_QK + 2 * RET_V
RET_CHUNK = 128
ROPE_BASE = 10000.0

D_FF = 2816
N_EXPERTS = 8
TOP_K = 2
D_FF_EXPERT = 3584
EPS = 1e-6

kernel_name = 'conv_stickbreak_retention_moe_decoder_step'

def rmsnorm(x, g):
    xf = x.astype(jnp.float32)
    y = xf * lax.rsqrt(jnp.mean(xf * xf, axis=-1, keepdims=True) + EPS)
    return (y * g.astype(jnp.float32)).astype(x.dtype)

def layernorm(x, g, b):
    xf = x.astype(jnp.float32)
    mu = jnp.mean(xf, axis=-1, keepdims=True)
    var = jnp.mean(jnp.square(xf - mu), axis=-1, keepdims=True)
    y = (xf - mu) * lax.rsqrt(var + EPS) * g.astype(jnp.float32) + b.astype(jnp.float32)
    return y.astype(x.dtype)

def swiglu(h, w_gate, w_up, w_down):
    return (jax.nn.silu(h @ w_gate) * (h @ w_up)) @ w_down

def moe_swiglu(h, router_w, w_gate, w_up, w_down):
    logits = (h @ router_w).astype(jnp.float32)
    top_val, top_idx = lax.top_k(logits, TOP_K)
    gates = jax.nn.softmax(top_val, axis=-1)
    combine = jnp.sum(jax.nn.one_hot(top_idx, N_EXPERTS, dtype=jnp.float32) * gates[..., None], axis=-2)
    combine = combine.astype(h.dtype)
    y = jnp.zeros_like(h)
    for e in range(N_EXPERTS):
        y = y + combine[..., e:e + 1] * swiglu(h, w_gate[e], w_up[e], w_down[e])
    return y

def causal_depthwise_conv(u, buf, w, b):
    full = jnp.concatenate([buf.astype(u.dtype), u], axis=1)
    out = lax.conv_general_dilated(full, w[:, None, :].astype(u.dtype), window_strides=(1,), padding='VALID',
                                   dimension_numbers=('NWC', 'WIO', 'NWC'), feature_group_count=u.shape[-1])
    return out + b, full[:, -(CONV_W - 1):]

def stick_breaking_block(q, k, v, q_pos, bias):
    z = jnp.einsum('bqhd,bkhd->bhqk', q, k, preferred_element_type=jnp.float32) * (SB_HEAD_DIM ** -0.5)
    z = z + bias.astype(jnp.float32)[None, :, None, None]
    k_pos = jnp.arange(k.shape[1], dtype=jnp.int32)
    mask = k_pos[None, :] < q_pos[:, None]
    log_keep = jnp.where(mask, jax.nn.log_sigmoid(-z), 0.0)
    suffix = lax.cumsum(log_keep, axis=3, reverse=True)
    log_a = jax.nn.log_sigmoid(z) + (suffix - log_keep)
    a = jnp.where(mask, jnp.exp(log_a), 0.0)
    return jnp.einsum('bhqk,bkhd->bqhd', a.astype(v.dtype), v)

def stick_breaking_prompt(q, k, v, bias):
    b, s, h, d = q.shape
    nb = s // Q_BLOCK
    qb = q.reshape(b, nb, Q_BLOCK, h, d).transpose(1, 0, 2, 3, 4)
    pos = jnp.arange(s, dtype=jnp.int32).reshape(nb, Q_BLOCK)
    out = lax.map(lambda args: stick_breaking_block(args[0], k, v, args[1], bias), (qb, pos))
    return out.transpose(1, 0, 2, 3, 4).reshape(b, s, h, d)

def conv_sb_mixer(h, w_in, conv_w, conv_b, ln_g, ln_b, q_g, k_g, sb_bias, w_out, conv_buf, k_past, v_past):
    b, t, _ = h.shape
    a, gate, q, k, v = jnp.split(h @ w_in, [CONV_CH, 2 * CONV_CH, 2 * CONV_CH + SB_WIDTH,
                                            2 * CONV_CH + 2 * SB_WIDTH], axis=-1)
    u = a * jax.nn.sigmoid(gate)
    c, new_buf = causal_depthwise_conv(u, conv_buf, conv_w, conv_b)
    c = jax.nn.silu(layernorm(c, ln_g, ln_b))
    q = rmsnorm(q.reshape(b, t, SB_HEADS, SB_HEAD_DIM), q_g)
    k = rmsnorm(k.reshape(b, t, SB_HEADS, SB_HEAD_DIM), k_g)
    v = v.reshape(b, t, SB_HEADS, SB_HEAD_DIM)
    if k_past is None:
        o = stick_breaking_prompt(q, k, v, sb_bias)
    else:
        pos = k_past.shape[1] + jnp.arange(t, dtype=jnp.int32)
        k_all = jnp.concatenate([k_past.astype(k.dtype), k], axis=1)
        v_all = jnp.concatenate([v_past.astype(v.dtype), v], axis=1)
        o = stick_breaking_block(q, k_all, v_all, pos, sb_bias)
    mixed = jnp.concatenate([c, o.reshape(b, t, SB_WIDTH)], axis=-1) @ w_out
    return mixed, k, v, new_buf

def rotary(x, pos):
    half = x.shape[-1] // 2
    inv_freq = ROPE_BASE ** (-jnp.linspace(0.0, 1.0, half, dtype=jnp.float32))
    ang = pos.astype(jnp.float32)[:, None] * inv_freq[None, :]
    cos = jnp.cos(ang)[None, :, None, :]
    sin = jnp.sin(ang)[None, :, None, :]
    xf = x.astype(jnp.float32)
    x1, x2 = xf[..., :half], xf[..., half:]
    return jnp.concatenate([x1 * cos - x2 * sin, x1 * sin + x2 * cos], axis=-1).astype(x.dtype)

def retention_chunk(state, qkv):
    q, k, v = qkv
    c = q.shape[1]
    log_g = jnp.log1p(-jnp.exp2(-5.0 - jnp.arange(RET_HEADS, dtype=jnp.float32)))
    idx = jnp.arange(c, dtype=jnp.float32)
    diff = idx[:, None] - idx[None, :]
    decay = jnp.where(diff >= 0, jnp.exp(log_g[:, None, None] * jnp.maximum(diff, 0.0)), 0.0)
    qf, kf, vf = q.astype(jnp.float32), k.astype(jnp.float32), v.astype(jnp.float32)
    scores = jnp.einsum('bnhd,bmhd->bhnm', qf, kf) * decay[None]
    inner = jnp.einsum('bhnm,bmhe->bnhe', scores, vf)
    q_decay = jnp.exp(log_g[None, :] * (idx[:, None] + 1.0))
    cross = jnp.einsum('bnhd,bhde->bnhe', qf, state) * q_decay[None, :, :, None]
    k_decay = jnp.exp(log_g[None, :] * (c - 1.0 - idx[:, None]))
    new_state = (jnp.exp(log_g * c)[None, :, None, None] * state
                 + jnp.einsum('bmhd,mh,bmhe->bhde', kf, k_decay, vf))
    return new_state, inner + cross

def retention_scan(q, k, v, state0):
    b, t = q.shape[:2]
    c = RET_CHUNK if t % RET_CHUNK == 0 else t
    n = t // c

    def chunks(x):
        return x.reshape(b, n, c, *x.shape[2:]).swapaxes(0, 1)

    state, o = lax.scan(retention_chunk, state0.astype(jnp.float32), (chunks(q), chunks(k), chunks(v)))
    return o.swapaxes(0, 1).reshape(b, t, RET_HEADS, RET_DV), state

def retention_mixer(h, w_in, gn_g, gn_b, w_out, pos, state0):
    b, t, _ = h.shape
    q, k, v, g = jnp.split(h @ w_in, [RET_QK, 2 * RET_QK, 2 * RET_QK + RET_V], axis=-1)
    q = rotary(q.reshape(b, t, RET_HEADS, RET_DK), pos)
    k = rotary(k.reshape(b, t, RET_HEADS, RET_DK), pos) * (RET_DK ** -0.5)
    v = v.reshape(b, t, RET_HEADS, RET_DV)
    o, state = retention_scan(q, k, v, state0)
    mu = jnp.mean(o, axis=-1, keepdims=True)
    var = jnp.mean(jnp.square(o - mu), axis=-1, keepdims=True)
    o = ((o - mu) * lax.rsqrt(var + EPS)).reshape(b, t, RET_V) * gn_g.astype(jnp.float32) + gn_b.astype(jnp.float32)
    y = (jax.nn.silu(g) * o.astype(h.dtype)) @ w_out
    return y, state

def setup_inputs(seed: int = 0) -> dict:
    key = jax.random.key(seed)
    ks = iter(jax.random.split(key, 40))

    def nrm(shape, scale):
        return jax.random.normal(next(ks), shape, jnp.float32) * scale

    def gain(shape):
        return 1.0 + nrm(shape, 0.02)

    n_pages = PAST_LEN // PAGE_SIZE
    n_used = DEC_BATCH * n_pages
    n_pool = n_used + max(1, n_used // 4)
    page_table = jax.random.permutation(next(ks), n_pool)[:n_used].reshape(DEC_BATCH, n_pages).astype(jnp.int32)
    return {
        'x_prompt': nrm((BATCH, SEQ, D_MODEL), 1.0),
        'x_sample': nrm((DEC_BATCH, DEC_SEQ, D_MODEL), 1.0),
        'cache_sb_k': nrm((N_EVEN, n_pool, PAGE_SIZE, SB_HEADS, SB_HEAD_DIM), 1.0),
        'cache_sb_v': nrm((N_EVEN, n_pool, PAGE_SIZE, SB_HEADS, SB_HEAD_DIM), 1.0),
        'cache_conv': nrm((N_EVEN, DEC_BATCH, CONV_W - 1, CONV_CH), 0.5),
        'state_ret': nrm((N_ODD, DEC_BATCH, RET_HEADS, RET_DK, RET_DV), 0.5),
        'page_table': page_table,
        'norm_mix_even': gain((N_EVEN, D_MODEL)),
        'w_in_even': nrm((N_EVEN, D_MODEL, EVEN_IN), D_MODEL ** -0.5),
        'conv_w': nrm((N_EVEN, CONV_W, CONV_CH), CONV_W ** -0.5),
        'conv_b': nrm((N_EVEN, CONV_CH), 0.02),
        'conv_ln_g': gain((N_EVEN, CONV_CH)),
        'conv_ln_b': nrm((N_EVEN, CONV_CH), 0.02),
        'sb_q_norm': gain((N_EVEN, SB_HEAD_DIM)),
        'sb_k_norm': gain((N_EVEN, SB_HEAD_DIM)),
        'sb_bias': SB_BIAS_INIT + nrm((N_EVEN, SB_HEADS), 0.5),
        'w_out_even': nrm((N_EVEN, EVEN_MIX, D_MODEL), EVEN_MIX ** -0.5),
        'norm_ffn_even': gain((N_EVEN, D_MODEL)),
        'ffn_w_gate': nrm((N_EVEN, D_MODEL, D_FF), D_MODEL ** -0.5),
        'ffn_w_up': nrm((N_EVEN, D_MODEL, D_FF), D_MODEL ** -0.5),
        'ffn_w_down': nrm((N_EVEN, D_FF, D_MODEL), D_FF ** -0.5),
        'norm_mix_odd': gain((N_ODD, D_MODEL)),
        'w_in_odd': nrm((N_ODD, D_MODEL, ODD_IN), D_MODEL ** -0.5),
        'ret_gn_g': gain((N_ODD, RET_V)),
        'ret_gn_b': nrm((N_ODD, RET_V), 0.02),
        'w_out_odd': nrm((N_ODD, RET_V, D_MODEL), RET_V ** -0.5),
        'norm_ffn_odd': gain((N_ODD, D_MODEL)),
        'router_w': nrm((N_ODD, D_MODEL, N_EXPERTS), D_MODEL ** -0.5),
        'moe_w_gate': nrm((N_ODD, N_EXPERTS, D_MODEL, D_FF_EXPERT), D_MODEL ** -0.5),
        'moe_w_up': nrm((N_ODD, N_EXPERTS, D_MODEL, D_FF_EXPERT), D_MODEL ** -0.5),
        'moe_w_down': nrm((N_ODD, N_EXPERTS, D_FF_EXPERT, D_MODEL), D_FF_EXPERT ** -0.5),
    }

def reference(x_prompt, x_sample, cache_sb_k, cache_sb_v, cache_conv, state_ret, page_table,
              norm_mix_even, w_in_even, conv_w, conv_b, conv_ln_g, conv_ln_b, sb_q_norm, sb_k_norm, sb_bias,
              w_out_even, norm_ffn_even, ffn_w_gate, ffn_w_up, ffn_w_down,
              norm_mix_odd, w_in_odd, ret_gn_g, ret_gn_b, w_out_odd,
              norm_ffn_odd, router_w, moe_w_gate, moe_w_up, moe_w_down):
    n_ctx = page_table.shape[1] * cache_sb_k.shape[2]
    pos_p = jnp.arange(x_prompt.shape[1], dtype=jnp.int32)
    pos_s = n_ctx + jnp.arange(x_sample.shape[1], dtype=jnp.int32)
    yp, ys = x_prompt, x_sample
    kp_l, vp_l, ks_l, vs_l, cp_l, cs_l, rp_l, rs_l = [], [], [], [], [], [], [], []
    for layer in range(DEPTH):
        li = layer // 2
        if layer % 2 == 0:
            even_w = (w_in_even[li], conv_w[li], conv_b[li], conv_ln_g[li], conv_ln_b[li],
                      sb_q_norm[li], sb_k_norm[li], sb_bias[li], w_out_even[li])
            buf0 = jnp.zeros((yp.shape[0], CONV_W - 1, CONV_CH), yp.dtype)
            k_past = cache_sb_k[li][page_table].reshape(ys.shape[0], n_ctx, SB_HEADS, SB_HEAD_DIM)
            v_past = cache_sb_v[li][page_table].reshape(ys.shape[0], n_ctx, SB_HEADS, SB_HEAD_DIM)
            mp, kp, vp, cp = conv_sb_mixer(rmsnorm(yp, norm_mix_even[li]), *even_w, buf0, None, None)
            ms, k_s, v_s, c_s = conv_sb_mixer(rmsnorm(ys, norm_mix_even[li]), *even_w, cache_conv[li], k_past, v_past)
            yp = yp + mp
            ys = ys + ms
            ffn_w = (ffn_w_gate[li], ffn_w_up[li], ffn_w_down[li])
            yp = yp + swiglu(rmsnorm(yp, norm_ffn_even[li]), *ffn_w)
            ys = ys + swiglu(rmsnorm(ys, norm_ffn_even[li]), *ffn_w)
            kp_l.append(kp)
            vp_l.append(vp)
            ks_l.append(k_s)
            vs_l.append(v_s)
            cp_l.append(cp)
            cs_l.append(c_s)
        else:
            ret_w = (w_in_odd[li], ret_gn_g[li], ret_gn_b[li], w_out_odd[li])
            s0 = jnp.zeros((yp.shape[0], RET_HEADS, RET_DK, RET_DV), jnp.float32)
            mp, sp = retention_mixer(rmsnorm(yp, norm_mix_odd[li]), *ret_w, pos_p, s0)
            ms, ss = retention_mixer(rmsnorm(ys, norm_mix_odd[li]), *ret_w, pos_s, state_ret[li])
            yp = yp + mp
            ys = ys + ms
            moe_w = (router_w[li], moe_w_gate[li], moe_w_up[li], moe_w_down[li])
            yp = yp + moe_swiglu(rmsnorm(yp, norm_ffn_odd[li]), *moe_w)
            ys = ys + moe_swiglu(rmsnorm(ys, norm_ffn_odd[li]), *moe_w)
            rp_l.append(sp)
            rs_l.append(ss)
    return (yp, ys, jnp.stack(kp_l), jnp.stack(vp_l), jnp.stack(ks_l), jnp.stack(vs_l),
            jnp.stack(cp_l), jnp.stack(cs_l), jnp.stack(rp_l), jnp.stack(rs_l))


_drawn_inputs = setup_inputs


def setup_inputs(seed=0):
    import zlib

    import numpy as np

    out = dict(_drawn_inputs(seed))
    spreads = {}
    factors = {'sb_q_norm': 8.0,
     'sb_k_norm': 2.85,
     'conv_ln_g': 2.695,
     'conv_ln_b': 3.538,
     'ret_gn_g': 13.096,
     'ret_gn_b': 12.087,
     'norm_ffn_odd': 4.117}
    for name, (base, spread) in spreads.items():
        noise = np.random.default_rng([zlib.crc32(name.encode()), seed]).standard_normal(out[name].shape)
        drawn = base * np.exp(spread * noise) if base else spread * noise
        out[name] = jnp.asarray(drawn.astype(out[name].dtype))
    for name, factor in factors.items():
        out[name] = (out[name] * factor).astype(out[name].dtype)
    return out
```

```python
from contextlib import ExitStack

import concourse.bass as bass
from concourse import mybir
import numpy as np

F32 = mybir.dt.float32
I32 = mybir.dt.int32
U32 = mybir.dt.uint32
ALU = mybir.AluOpType
ACT = mybir.ActivationFunctionType
AX = mybir.AxisListType

P = 128
D = 1024
DK = D // P
SEQ = 256
NS = 8
T = SEQ + NS
NT = 3
TOK = [P, P, NS]
CH = 512
CT = CH // P
W = 31
H = 8
HD = 64
SBW = H * HD
HP = SBW // P
PAST = 256
PAGES = PAST // P
FF = 2816
FT = FF // P
RV = 2048
EV = RV // H
E = 8
FE = 3584
EPS = 1e-6
ZW = 384
ZP = H * ZW
ZS = PAGES * NS * H
GAMMA = [1.0 - 2.0 ** (-5 - h) for h in range(H)]

RING = 7
CW = 2048
IC = CW // DK
MSTEPS = FE // IC
MCH = 3 * MSTEPS
MAXI = 12
assert MCH % RING == 0

CONST = {}
_at = 0
for _name, _n in [("ident", P), ("negtri", P), ("negones", P), ("below", P), ("ones", P), ("mean_d", P),
                  ("mean_ch", P), ("mean_hd", P), ("mean_ev", P), ("cos", 2 * T), ("sin", 2 * T),
                  ("slot", P), ("kdecay", 2 * H), ("iota8", E), ("lt8", E * E), ("item", MAXI * E),
                  ("expert", MAXI * E), ("eps", 1), ("rows", 1)]:
    CONST[_name] = (_at, _n)
    _at += _n
NCONST = _at
PARAM = {}
_at = 0
for _name, _n in [("g0", DK), ("g1", DK), ("g2", DK), ("g3", DK), ("conv_w", CT * W), ("conv_b", CT),
                  ("ln_g", CT), ("ln_b", CT), ("q_g", 1), ("k_g", 1), ("bias", H), ("gn_g", RV // P),
                  ("gn_b", RV // P), ("router", DK * E)]:
    PARAM[_name] = (_at, _n)
    _at += _n
NPARAM = _at

C_EVEN = 0
C_OUTE = C_EVEN + 10
C_FFN = C_OUTE + 4
C_DOWN = C_FFN + 2 * FF // IC
C_ODD = C_DOWN + 12
C_OUTO = C_ODD + 24
C_MOE = C_OUTO + 8


def build(nc, x_prompt, x_sample, cache_k, cache_v, cache_conv, state_ret, page_table, const, decay, param,
          w_in_even, w_out_even, w_gate, w_up, w_down, w_in_odd, w_out_odd, m_gate, m_up, m_down,
          y_prompt, y_sample, k_prompt, v_prompt, k_sample, v_sample, conv_prompt, conv_sample,
          ret_prompt, ret_sample):
    with ExitStack() as ctx:
        def sb(name, shape, dt=F32):
            return ctx.enter_context(nc.sbuf_tensor(name, shape, dt))

        def sem(name):
            return ctx.enter_context(nc.semaphore(name))

        ring = sb("ring", [P, RING, CW])
        XT = sb("XT", [P, DK, T])
        HT = sb("HT", [P, DK, T])
        SQ = sb("SQ", [P, DK, T])
        RS = sb("RS", [P, 2, T])
        C = sb("C", [P, NCONST])
        R = sb("R", [P, NPARAM])
        PG = sb("PG", [1, NS * PAGES], I32)
        arena = sb("arena", [P, 28700])
        PB = [ctx.enter_context(nc.psum_tensor(f"bank{i}", [P, 512], F32)) for i in range(8)]

        used = {}

        def region(stage, *shape, parts=P):
            n = int(np.prod(shape))
            at = used.get(stage, 0)
            used[stage] = at + n
            assert used[stage] <= 28700
            v = arena[0:parts, at:at + n]
            if len(shape) == 2:
                v = v.rearrange("p (a b) -> p a b", b=shape[1])
            if len(shape) == 3:
                v = v.rearrange("p (a b c) -> p a b c", b=shape[1], c=shape[2])
            return v

        def const_(name, parts=P):
            at, n = CONST[name]
            return C[0:parts, at:at + n]

        def param_(name):
            at, n = PARAM[name]
            return R[:, at:at + n]

        ident = const_("ident")
        eps = const_("eps")

        KV = region("even", NS * PAGES, SBW)
        Z = region("even", ZP + ZS)
        L = region("even", ZP + ZS)
        A = region("even", ZP + ZS)
        QR = region("even", 2 * HP, T)
        QN = region("even", 2 * HP, T)
        VT = region("even", NT, SBW)
        U = region("even", CT, W - 1 + SEQ)
        UF = region("even", CT, NS, W)
        CA = region("even", CT, T)
        KO = region("even", NT, SBW)
        XI = Z[:, 0:3072].rearrange("p (a b) -> p a b", b=D)
        CC = L[:, 0:1024].rearrange("p (a b) -> p a b", b=CH)
        SG = L[:, 1024:1024 + CT * T].rearrange("p (a b) -> p a b", b=T)
        SW = A[:, 0:CT * NS * W].rearrange("p (a b c) -> p a b c", b=NS, c=W)
        CD = L[:, 0:CT * T].rearrange("p (a b) -> p a b", b=T)
        CQ = L[:, CT * T:2 * CT * T].rearrange("p (a b) -> p a b", b=T)
        UO = KO[32:32 + W - 1, 2, :]
        US = KO[64:64 + NS, 2, :]
        QS = A[0:NS, 2080:2080 + SBW]
        KQ = A[:, 1056:1056 + 2 * SBW].rearrange("p (a b) -> p a b", b=SBW)
        MIX = HT
        HID = region("ffn", FT, T)
        GA = region("ffn", 2, T)
        QT = region("odd", H, T)
        KT = region("odd", H, T)
        VR = region("odd", NT, RV)
        O = region("odd", 2 * H, T)
        DT = region("odd", H, ZW)
        ST = region("odd", 2, NS * EV)
        R1 = region("odd", 2, T)
        R2 = region("odd", 2, T)
        SC = region("odd", 2, ZW)
        KD = region("odd", 2, 2 * P)
        KM = region("odd", 2, NS * P)
        RP = region("odd", 2, EV)
        KS = region("odd", D)
        OD = SQ[:, 0:4, :].rearrange("p (u a) t -> p u a t", u=2)
        OQ = SQ[:, 4:8, :].rearrange("p (u a) t -> p u a t", u=2)
        HX = region("moe", NT, D)
        XE = region("moe", DK, P)
        OH = region("moe", NT, P)
        OG = region("moe", NT, P)
        OT = region("moe", T)
        SI = region("moe", 2, IC)
        AC = region("moe", 2, IC)
        AT = region("moe", 2, 2 * P)
        YE = region("moe", D)
        LG = region("moe", NT, E)
        MX = region("moe", NT, 8)
        MIF = region("moe", NT, 8)
        GE = region("moe", NT, 8)
        SE = region("moe", NT, E)
        S1 = region("moe", NT, E)
        RK = region("moe", NT, E)
        TI = region("moe", 8, E)
        LT = region("moe", E, E)
        M1 = region("moe", MAXI, E)
        M2 = region("moe", MAXI, E)
        M3 = region("moe", MAXI, E)
        BA = region("moe", MAXI)
        M4 = region("moe", NT, MAXI * E)
        CR = region("moe", MAXI, NT)
        CG = region("moe", MAXI, NT)
        EI = region("moe", MAXI + 1)
        CU = region("moe", 2, NT)
        YO = region("moe", NT, D)
        MI = sb("MI", [P, NT, 8], U32)
        EII = sb("EII", [P, MAXI + 1], I32)

        s_x = sem("s_x"); s_const = sem("s_const"); s_cc = sem("s_cc"); s_pt = sem("s_pt"); s_decay = sem("s_decay")
        s_ring = [sem(f"s_ring{i}") for i in range(RING)]
        s_kpage = sem("s_kpage"); s_vpage = sem("s_vpage"); s_state = [sem("s_state0"), sem("s_state1")]
        s_turn = sem("s_turn"); s_xt = sem("s_xt"); s_sq = sem("s_sq"); s_ms = sem("s_ms"); s_rt = sem("s_rt")
        s_ht = sem("s_ht")
        s_zero = sem("s_zero"); s_cct = sem("s_cct"); s_win = sem("s_win")
        s_ag = sem("s_ag"); s_sig = sem("s_sig"); s_u = sem("s_u"); s_ut = sem("s_ut"); s_uo = sem("s_uo")
        s_conv = sem("s_conv"); s_cm = sem("s_cm"); s_cd = sem("s_cd"); s_cq = sem("s_cq"); s_cv = sem("s_cv")
        s_crt = sem("s_crt"); s_cn = sem("s_cn"); s_mixc = sem("s_mixc")
        s_qk = sem("s_qk"); s_qks = sem("s_qks"); s_vp = sem("s_vp"); s_vev = sem("s_vev"); s_qms = sem("s_qms")
        s_qrt = sem("s_qrt"); s_qn = sem("s_qn"); s_ktm = sem("s_ktm"); s_kto = sem("s_kto"); s_qs = sem("s_qs")
        s_qse = sem("s_qse"); s_z = sem("s_z"); s_zev = sem("s_zev"); s_qb = sem("s_qb"); s_kq = sem("s_kq")
        s_zs = sem("s_zs"); s_ln = sem("s_ln"); s_lk = sem("s_lk"); s_suf = sem("s_suf"); s_la = sem("s_la")
        s_exp = sem("s_exp"); s_a = sem("s_a"); s_av = sem("s_av"); s_ava = sem("s_ava"); s_avs = sem("s_avs")
        s_mixa = sem("s_mixa")
        s_down = sem("s_down")
        s_gu = sem("s_gu"); s_silu = sem("s_silu"); s_hid = sem("s_hid")
        s_rq = sem("s_rq"); s_rot = sem("s_rot"); s_rv = sem("s_rv"); s_rve = sem("s_rve"); s_ks = sem("s_ks")
        s_kse = sem("s_kse"); s_sc = sem("s_sc"); s_sce = sem("s_sce"); s_kt = sem("s_kt"); s_kde = sem("s_kde")
        s_o = sem("s_o"); s_oe = sem("s_oe"); s_rp = sem("s_rp"); s_rpe = sem("s_rpe"); s_rpo = [sem("s_rpo0"), sem("s_rpo1")]
        s_km = sem("s_km"); s_out = sem("s_out"); s_new = sem("s_new"); s_os = sem("s_os"); s_ose = sem("s_ose")
        s_sto = [sem("s_sto0"), sem("s_sto1")]
        s_om = sem("s_om"); s_od = sem("s_od"); s_oq = sem("s_oq"); s_ov = sem("s_ov"); s_ort = sem("s_ort")
        s_on = sem("s_on"); s_g = sem("s_g"); s_gs = sem("s_gs"); s_y = sem("s_y")
        s_lg = sem("s_lg"); s_ht2 = sem("s_ht2"); s_hx = sem("s_hx"); s_lgx = sem("s_lgx"); s_e2 = sem("s_e2")
        s_sel = sem("s_sel"); s_rk = sem("s_rk"); s_items = sem("s_items"); s_oh = sem("s_oh")
        s_ga = sem("s_ga"); s_xe = sem("s_xe"); s_oht = sem("s_oht"); s_ot = sem("s_ot"); s_mm = sem("s_mm")
        s_si = sem("s_si"); s_ac = sem("s_ac"); s_at = sem("s_at"); s_ate = sem("s_ate"); s_ye = sem("s_ye")
        s_yee = sem("s_yee"); s_sca = sem("s_sca"); s_add = sem("s_add"); s_yt = sem("s_yt"); s_yo = sem("s_yo")
        s_dn = sem("s_dn")
        s_ach = sem("s_ach"); s_dch = sem("s_dch")
        s_ydone = sem("s_ydone"); s_done = sem("s_done")
        ctx.enter_context(nc.allow_non_contiguous_dma(reason="small rows"))
        block = ctx.enter_context(nc.Block())

        def chunk(q):
            return ring[:, q % RING, :]

        def icols(w, c0):
            return w[:, c0:c0 + IC].rearrange("(k p) n -> p k n", p=P)

        def as_in(ap):
            return ap.rearrange("p (k n) -> p k n", n=IC)

        def down_parts(kt):
            return [(k, min(4, kt - k)) for k in range(0, kt, 4)]

        DOWN = [(C_OUTE, w_out_even, DK, 0), (C_DOWN, w_down, FT, 4), (C_OUTO, w_out_odd, RV // P, 16)]
        NDOWN = 24

        released = [(s_ag, 2), (s_ag, 4), (s_ag, 6), (s_ag, 8), (s_qk, 2), (s_qk, 4), (s_qk, 6), (s_qk, 8),
                    (s_vp, NT), (s_vp, 2 * NT)]
        released += [(s_down, 1 + n) for n in range(4)]
        released += [(s_gu, 2 * n + 2) for n in range(2 * FF // IC)]
        released += [(s_down, 5 + n) for n in range(12)]
        released += [(s_rq, 2 * n + 2) for n in range(8)]
        released += [(s_rv, NT * (n + 1)) for n in range(8)]
        released += [(s_g, 2 * n + 2) for n in range(8)]
        released += [(s_down, 17 + n) for n in range(8)]
        assert len(released) == C_MOE

        ORDER = []
        for f in range(MSTEPS):
            ORDER += [("gate", f), ("up", f)] + ([("down", f - 2)] if f >= 2 else [])
        ORDER += [("down", MSTEPS - 2), ("down", MSTEPS - 1)]
        PLACE = {key: c for c, key in enumerate(ORDER)}

        @block.sync
        def _(sp):
            def load(q, dst, src):
                if q >= RING:
                    s, v = released[q - RING]
                    sp.wait_ge(s, v)
                sp.dma_start(dst, src).then_inc(s_ring[q % RING], 16)

            def load_in(q, w, c0):
                load(q, as_in(chunk(q)), icols(w, c0))

            def load_down(d):
                q, w, kt, _ = DOWN[d]
                for half in range(2):
                    for k0, n in down_parts(kt):
                        load(q, chunk(q)[:, 0:n * 512].rearrange("p (k n) -> p k n", n=512),
                             w[0, k0 * P:(k0 + n) * P, half * 512:half * 512 + 512]
                             .rearrange("(k p) n -> p k n", p=P))
                        q += 1

            sp.dma_start(XI[:, 0:2, :], x_prompt.rearrange("o (a p) d -> p (o a) d", p=P)).then_inc(s_x, 16)
            sp.dma_start(XI[0:NS, 2, :], x_sample.rearrange("b o d -> (b o) d")).then_inc(s_x, 16)
            sp.dma_start(C[:], const).then_inc(s_const, 16)
            sp.dma_start(R[:], param).then_inc(s_const, 16)
            q = C_EVEN
            for c0 in (0, CH, IC, CH + IC, 2 * CH, 2 * CH + IC, 2 * CH + SBW, 2 * CH + SBW + IC,
                       2 * CH + 2 * SBW, 2 * CH + 2 * SBW + IC):
                load_in(q, w_in_even[0], c0)
                q += 1
            load_down(0)
            for f in range(FF // IC):
                load_in(C_FFN + 2 * f, w_gate[0], f * IC)
                load_in(C_FFN + 2 * f + 1, w_up[0], f * IC)
            load_down(1)
            for c in range(24):
                load_in(C_ODD + c, w_in_odd[0], c * IC)
            load_down(2)

            def load_expert(e, it):
                for c, (kind, f) in enumerate(ORDER):
                    if kind == "down":
                        src = m_down[0, bass.ds(e, 1), f * IC:(f + 1) * IC, :].rearrange("o (k p) n -> p (o k) n", p=P)
                    else:
                        w = m_gate if kind == "gate" else m_up
                        src = w[0, bass.ds(e, 1), :, f * IC:(f + 1) * IC].rearrange("o (k p) n -> p (o k) n", p=P)
                    if c >= RING:
                        old, g = ORDER[c - RING]
                        if old == "down":
                            sp.wait_ge(s_dn, it * MSTEPS + g + 1)
                        else:
                            sp.wait_ge(s_mm, it * MSTEPS + g + 1)
                    elif isinstance(it, int):
                        s, v = released[C_MOE + c - RING]
                        sp.wait_ge(s, v)
                    else:
                        old, g = ORDER[MCH + c - RING]
                        if old == "down":
                            sp.wait_ge(s_dn, (it - 1) * MSTEPS + g + 1)
                        else:
                            sp.wait_ge(s_mm, (it - 1) * MSTEPS + g + 1)
                    q = C_MOE + c
                    sp.dma_start(chunk(q).rearrange("p (k n) -> p k n", n=src.shape[2]), src)\
                        .then_inc(s_ring[q % RING], 16)

            load_expert(0, 0)
            sp.wait_ge(s_items, 1)
            n_items = sp.value_load(EII[0:1, MAXI:MAXI + 1], min_val=E, max_val=MAXI)
            with sp.Fori(1, n_items) as it:
                e = sp.value_load(EII[0:1, bass.ds(it, 1)], min_val=0, max_val=E - 1)
                load_expert(e, it)
            sp.wait_ge(s_yo, 2 * NT)
            sp.dma_start(y_prompt.rearrange("o (a p) d -> p (o a) d", p=P), YO[:, 0:2, :]).then_inc(s_ydone, 16)
            sp.dma_start(y_sample.rearrange("b o d -> (b o) d"), YO[0:NS, 2, :]).then_inc(s_ydone, 16)
            sp.wait_ge(s_ydone, 32)
            sp.wait_ge(s_done, 16 * 7)
            for i in range(2):
                sp.wait_ge(s_sto[i], 16 * H // 2)

        @block.gpsimd
        def _(pool):
            pool.dma_start(PG[:], page_table.rearrange("(o b) g -> o (b g)", o=1)).then_inc(s_pt, 16)
            for b in range(2):
                pool.dma_start(CC[0:120, b, :], cache_conv[0, 4 * b:4 * b + 4].rearrange("b w c -> (b w) c"))\
                    .then_inc(s_cc, 16)
            nc.gpsimd.memset(U[:, :, 0:W - 1], 0.0).then_inc(s_zero, 1)
            pool.dma_start(conv_sample[0, :, 0:W - 2, :], cache_conv[0, :, 1:W - 1, :]).then_inc(s_done, 16)
            pool.wait_ge(s_pt, 16)
            for i in range(NS * PAGES):
                page = pool.value_load(PG[0:1, i:i + 1], min_val=0, max_val=cache_k.shape[1] - 1)
                pool.dma_start(KV[:, i, :], cache_k[0, bass.ds(page, 1)].rearrange("o p h d -> p (o h d)"))\
                    .then_inc(s_kpage, 16)
            pool.wait_ge(s_uo, 1)
            pool.dma_start(conv_prompt[0, 0], UO[:]).then_inc(s_done, 16)
            pool.wait_ge(s_uo, 2)
            pool.dma_start(conv_sample[0, :, W - 2, :], US[:]).then_inc(s_done, 16)
            pool.wait_ge(s_vev, 2 * NT)
            pool.dma_start(v_prompt[0, 0].rearrange("(a p) h d -> p a (h d)", p=P), VT[:, 0:2, :])\
                .then_inc(s_done, 16)
            pool.dma_start(v_sample[0].rearrange("b o h d -> (b o) (h d)"), VT[0:NS, 2, :]).then_inc(s_done, 16)
            pool.wait_ge(s_kto, NT)
            pool.dma_start(k_prompt[0, 0].rearrange("(a p) h d -> p a (h d)", p=P), KO[:, 0:2, :])\
                .then_inc(s_done, 16)
            pool.dma_start(k_sample[0].rearrange("b o h d -> (b o) (h d)"), KO[0:NS, 2, :]).then_inc(s_done, 16)
            for i in range(NS * PAGES):
                page = pool.value_load(PG[0:1, i:i + 1], min_val=0, max_val=cache_v.shape[1] - 1)
                pool.wait_ge(s_kq, i // PAGES + 1)
                pool.dma_start(KV[:, i, :], cache_v[0, bass.ds(page, 1)].rearrange("o p h d -> p (o h d)"))\
                    .then_inc(s_vpage, 16)
            pool.wait_ge(s_done, 16 * 7)
            pool.wait_ge(s_hid, 1)
            pool.dma_start(DT[:], decay.rearrange("p (h n) -> p h n", n=ZW)).then_inc(s_decay, 16)

            def state_in(h):
                pool.dma_start(ST[:, h % 2, :].rearrange("p (b e) -> p b e", e=EV),
                               state_ret[0, :, h].rearrange("b d e -> d b e")).then_inc(s_state[h % 2], 16)

            for h in range(2):
                state_in(h)
            for h in range(H):
                pool.wait_ge(s_rpe, h + 1)
                pool.dma_start(ret_prompt[0, 0, h], RP[:, h % 2, :]).then_inc(s_rpo[h % 2], 16)
            for h in range(H):
                pool.wait_ge(s_new, 4 * (h + 1))
                pool.dma_start(ret_sample[0, :, h].rearrange("b d e -> d b e"),
                               ST[:, h % 2, :].rearrange("p (b e) -> p b e", e=EV)).then_inc(s_sto[h % 2], 16)
                if h + 2 < H:
                    pool.wait_ge(s_sto[h % 2], 16 * (h // 2 + 1))
                    pool.wait_ge(s_os, h + 1)
                    state_in(h + 2)
            for i in range(2):
                pool.wait_ge(s_rpo[i], 16 * H // 2)

        @block.tensor
        def _(pe):
            mm = nc.tensor.matmul
            turn = nc.tensor.transpose

            def arrived(q):
                pe.wait_ge(s_ring[q % RING], 16 * (q // RING + 1))

            def sumsq(r):
                for k in range(DK):
                    if k % 2 == 0:
                        pe.wait_ge(s_sq, 4 * r + k // 2 + 1)
                    last = mm(PB[4][:, 0:T], const_("mean_d"), SQ[:, k, :], start=(k == 0), stop=(k == DK - 1))
                last.then_inc(s_ms, 1)

            def project(q, j, out, done, first=None):
                w = as_in(chunk(q))
                if j == 0:
                    arrived(q)
                for k in range(DK):
                    if first is not None:
                        pe.wait_ge(s_ht, DK * first + k + 1)
                    last = mm(out, w[:, k, j * P:(j + 1) * P], HT[:, k, :], start=(k == 0), stop=(k == DK - 1))
                last.then_inc(done, 1)

            def project_tokens(q, t, out, done):
                w = as_in(chunk(q))
                if t == 0:
                    arrived(q)
                for k in range(DK):
                    last = mm(out, HT[:, k, t * P:t * P + TOK[t]], w[:, k, :], start=(k == 0), stop=(k == DK - 1))
                last.then_inc(done, 1)

            def down(d, src, ready):
                q, _, kt, _ = DOWN[d]
                for half in range(2):
                    for k0, n in down_parts(kt):
                        arrived(q)
                        w = chunk(q)[:, 0:n * 512].rearrange("p (k n) -> p k n", n=512)
                        for kk in range(n):
                            k = k0 + kk
                            if half == 0:
                                ready(k)
                            for j in range(4):
                                last = mm(PB[4 * (1 - half) + j][:, 0:T], w[:, kk, j * P:(j + 1) * P], src[:, k, :],
                                          start=(k == 0), stop=(k == kt - 1))
                        last.then_inc(s_down, 1)
                        q += 1

            pe.wait_ge(s_x, 32)
            pe.wait_ge(s_const, 32)
            for k in range(DK):
                if k >= 4:
                    pe.wait_ge(s_xt, k - 3)
                for t in range(NT):
                    last = turn(PB[k % 4][:, t * P:t * P + TOK[t]],
                                XI[0:TOK[t], t, k * P:(k + 1) * P], ident[0:TOK[t], 0:TOK[t]])
                last.then_inc(s_turn, 1)
            pe.wait_ge(s_cc, 32)
            for c in range(CT):
                for b in range(2):
                    last = turn(PB[4 + c][:, b * 120:b * 120 + 120], CC[0:120, b, c * P:(c + 1) * P],
                                ident[0:120, 0:120])
                last.then_inc(s_cct, 1)
            pe.wait_ge(s_win, 1)
            sumsq(0)

            for c in range(2):
                if c == 1:
                    pe.wait_ge(s_win, CT)
                for g in range(2):
                    for j in range(2):
                        project(C_EVEN + 2 * c + g, j, PB[4 * c + 2 * g + j][:, 0:T], s_ag,
                                first=0 if c == g == j == 0 else None)
            for n in range(2 * HP):
                pe.wait_ge(s_u, 2 * (n // 4) + n % 2 + 1)
                project(C_EVEN + 4 + n // 2, n % 2, PB[n][:, 0:T], s_qk)
            for c in range(2):
                for t in range(NT):
                    m = NT * c + t
                    pe.wait_ge(s_qks, m + 1)
                    project_tokens(C_EVEN + 8 + c, t, PB[m][0:TOK[t], 0:IC], s_vp)
            for n in range(2 * HP):
                pe.wait_ge(s_qks, 8 if n < 2 else n + 1)
                if n >= 2:
                    pe.wait_ge(s_qrt, n - 1)
                mm(PB[6 + n % 2][:, 0:T], const_("mean_hd"), SQ[:, n, :], start=True, stop=True).then_inc(s_qms, 1)
            pe.wait_ge(s_vev, 2 * NT)
            for c in range(CT):
                last = turn(PB[4][0:W - 1, c * P:(c + 1) * P], U[:, c, SEQ:SEQ + W - 1], ident)
            last.then_inc(s_ut, 1)
            for c in range(CT):
                last = turn(PB[5][0:NS, c * P:(c + 1) * P], UF[:, c, :, W - 1], ident)
            last.then_inc(s_ut, 1)
            pe.wait_ge(s_qn, HP)
            for j in range(HP):
                last = turn(PB[3][0:NS, j * P:(j + 1) * P], QN[:, j, SEQ:T], ident)
            last.then_inc(s_qs, 1)
            pe.wait_ge(s_qn, 2 * HP)
            for t in range(NT):
                for j in range(HP):
                    last = turn(PB[t][0:TOK[t], j * P:(j + 1) * P], QN[:, HP + j, t * P:t * P + TOK[t]], ident)
                last.then_inc(s_ktm, 1)
            for h in range(H):
                if h < NT:
                    pe.wait_ge(s_kto, h + 1)
                elif h == NT:
                    pe.wait_ge(s_qse, 1)
                else:
                    pe.wait_ge(s_zev, h - 3)
                o = HD * (h % 2)
                q, k = QN[o:o + HD, h // 2, :], QN[o:o + HD, HP + h // 2, :]
                mm(PB[h % 4][:, 0:SEQ], k[:, 0:P], q[:, 0:SEQ], start=True, stop=True)
                mm(PB[h % 4][:, SEQ:ZW], k[:, P:SEQ], q[:, P:SEQ], start=True, stop=True).then_inc(s_z, 1)
            pe.wait_ge(s_uo, 2)
            pe.wait_ge(s_qrt, 2 * HP)
            pe.wait_ge(s_qse, 1)
            for b in range(NS):
                if b >= 4:
                    pe.wait_ge(s_kq, b - 3)
                mm(PB[4 + b % 4][:, 0:SBW], C[0:NS, b:b + 1].to_broadcast([NS, P]), QS[:], start=True, stop=True)\
                    .then_inc(s_qb, 1)
            for h in range(H + 1):
                if h < 4:
                    pe.wait_ge(s_zev, 4 + h + 1)
                else:
                    pe.wait_ge(s_la, h - 3)
                if h % 4 == 0:
                    pe.wait_ge(s_lk, min(h // 4 + 1, 2))
                if h < H:
                    lk = Z[:, h * ZW:(h + 1) * ZW]
                    mm(PB[h % 4][:, 0:ZW], const_("negtri"), lk, start=True, stop=False)
                    mm(PB[h % 4][:, P:SEQ], const_("negones"), lk[:, SEQ:ZW], start=False, stop=True)\
                        .then_inc(s_suf, 1)
                else:
                    lk = Z[:, ZP:ZP + ZS]
                    mm(PB[h % 4][:, 0:ZS], const_("negtri"), lk, start=True, stop=False)
                    mm(PB[h % 4][:, 0:ZS // 2], const_("negones"), lk[:, ZS // 2:ZS], start=False, stop=True)\
                        .then_inc(s_suf, 1)
            pe.wait_ge(s_la, H + 1)
            pe.wait_ge(s_conv, CT)
            for c in range(CT):
                last = mm(PB[1][:, 0:T], const_("mean_ch"), CA[:, c, :], start=(c == 0), stop=(c == CT - 1))
            last.then_inc(s_cm, 1)
            pe.wait_ge(s_cq, 1)
            for c in range(CT):
                last = mm(PB[2][:, 0:T], const_("mean_ch"), CQ[:, c, :], start=(c == 0), stop=(c == CT - 1))
            last.then_inc(s_cv, 1)
            pe.wait_ge(s_kq, NS)
            for h in range(H):
                if h % 4 == 0:
                    pe.wait_ge(s_a, h // 4 + 1)
                o = HD * (h % 2)
                out = PB[4 + h // 2][o:o + HD, :]
                a = A[:, h * ZW:(h + 1) * ZW]
                mm(out[:, 0:SEQ], VT[:, 0, h * HD:(h + 1) * HD], a[:, 0:SEQ], start=True, stop=False)
                mm(out[:, P:SEQ], VT[:, 1, h * HD:(h + 1) * HD], a[:, SEQ:ZW], start=False, stop=True)\
                    .then_inc(s_av, 1)
            pe.wait_ge(s_vpage, 16 * NS * PAGES)
            for hp in range(HP):
                for b in range(NS):
                    for g in range(PAGES):
                        at = ZP + (g * NS + b) * H + 2 * hp
                        last = mm(PB[0][:, (hp * NS + b) * 2:(hp * NS + b) * 2 + 2],
                                  KV[:, b * PAGES + g, hp * P:(hp + 1) * P], A[:, at:at + 2],
                                  start=(g == 0), stop=(g == PAGES - 1))
            last.then_inc(s_avs, 1)
            pe.wait_ge(s_mixa, HP + 2)
            down(0, MIX, lambda k: pe.wait_ge(s_mixc, k + 1) if k < CT else None)

            sumsq(1)
            for c in range(FF // IC):
                if c >= 2:
                    pe.wait_ge(s_hid, 2 * (c - 1))
                for g in range(2):
                    for j in range(2):
                        project(C_FFN + 2 * c + g, j, PB[4 * (c % 2) + 2 * g + j][:, 0:T], s_gu,
                                first=1 if c == g == j == 0 else None)
            pe.wait_ge(s_hid, FT - 2)
            down(1, HID, lambda k: pe.wait_ge(s_hid, k + 1) if k >= FT - 2 else None)

            sumsq(2)
            for n in range(2 * H):
                if n >= 4:
                    pe.wait_ge(s_rot, n - 3)
                project(C_ODD + n // 2, n % 2, PB[n % 4][:, 0:T], s_rq, first=2 if n == 0 else None)
            for c in range(H):
                for t in range(NT):
                    m = NT * c + t
                    if m < 4:
                        pe.wait_ge(s_rot, 2 * H - 3 + m)
                    else:
                        pe.wait_ge(s_rve, m - 3)
                    project_tokens(C_ODD + 8 + c, t, PB[m % 4][0:TOK[t], 0:IC], s_rv)
            for h in range(H):
                last = turn(PB[4 + h // 4][0:NS, (h % 4) * P:(h % 4 + 1) * P], KT[:, h, SEQ:T], ident)
            last.then_inc(s_ks, 1)
            pe.wait_ge(s_kse, 2)
            pe.wait_ge(s_rve, NT * H)

            def scores(h):
                if h >= 2:
                    pe.wait_ge(s_sce, h - 1)
                    pe.wait_ge(s_kde, h - 1)
                    pe.wait_ge(s_rpe, h - 1)
                mm(PB[h % 2][:, 0:SEQ], KT[:, h, 0:P], QT[:, h, 0:SEQ], start=True, stop=True)
                mm(PB[h % 2][:, SEQ:ZW], KT[:, h, P:SEQ], QT[:, h, P:SEQ], start=True, stop=True).then_inc(s_sc, 1)
                for m in range(2):
                    last = turn(PB[2 + h % 2][:, m * P:(m + 1) * P], KT[:, h, m * P:(m + 1) * P], ident)
                last.then_inc(s_kt, 1)

            scores(0)
            for h in range(H):
                if h + 1 < H:
                    scores(h + 1)
                pe.wait_ge(s_sce, h + 1)
                if h >= 2:
                    pe.wait_ge(s_oe, 2 * (h - 1))
                for j in range(2):
                    out = PB[4 + 2 * (h % 2) + j]
                    v = VR[:, :, h * EV + j * P:h * EV + (j + 1) * P]
                    mm(out[:, 0:SEQ], v[:, 0, :], SC[:, h % 2, 0:SEQ], start=True, stop=False)
                    mm(out[:, P:SEQ], v[:, 1, :], SC[:, h % 2, SEQ:ZW], start=False, stop=True).then_inc(s_o, 1)
                pe.wait_ge(s_kde, h + 1)
                for m in range(2):
                    last = mm(PB[2 + h % 2][:, EV:2 * EV], KD[:, h % 2, m * P:(m + 1) * P],
                              VR[:, m, h * EV:(h + 1) * EV], start=(m == 0), stop=(m == 1))
                last.then_inc(s_rp, 1)
            pe.wait_ge(s_oe, 2 * H)
            pe.wait_ge(s_rpe, H)

            def outer(h):
                pe.wait_ge(s_km, h + 1)
                for g in range(4):
                    if h >= 1:
                        pe.wait_ge(s_new, 4 * (h - 1) + g + 1)
                    for i in range(2):
                        b = 2 * g + i
                        last = mm(PB[4 + g][:, i * EV:(i + 1) * EV], KM[0:NS, h % 2, b * P:(b + 1) * P],
                                  VR[0:NS, 2, h * EV:(h + 1) * EV], start=True, stop=True)
                    last.then_inc(s_out, 1)

            outer(0)
            for h in range(H):
                if h + 1 < H:
                    outer(h + 1)
                pe.wait_ge(s_new, 4 * (h + 1))
                if h >= 2:
                    pe.wait_ge(s_ose, h - 1)
                for j in range(2):
                    for b in range(NS):
                        last = mm(PB[h % 2][:, j * NS + b:j * NS + b + 1],
                                  ST[:, h % 2, b * EV + j * P:b * EV + (j + 1) * P],
                                  QT[:, h, SEQ + b:SEQ + b + 1], start=True, stop=True)
                last.then_inc(s_os, 1)

            def mean(h):
                pe.wait_ge(s_ose, H if h < 2 else h + 1)
                if h >= 2:
                    pe.wait_ge(s_od, h - 1)
                for j in range(2):
                    last = mm(PB[h % 2][:, 0:T], const_("mean_ev"), O[:, 2 * h + j, :], start=(j == 0), stop=(j == 1))
                last.then_inc(s_om, 1)

            mean(0)
            mean(1)
            for h in range(H):
                pe.wait_ge(s_oq, h + 1)
                if h >= 2:
                    pe.wait_ge(s_ort, h - 1)
                for j in range(2):
                    last = mm(PB[2 + h % 2][:, 0:T], const_("mean_ev"), OQ[:, h % 2, j, :],
                              start=(j == 0), stop=(j == 1))
                last.then_inc(s_ov, 1)
                if h + 2 < H:
                    mean(h + 2)
                for j in range(2):
                    n = 2 * h + j
                    if n < 4:
                        pe.wait_ge(s_new, 4 * H)
                    else:
                        pe.wait_ge(s_y, n - 3)
                    project(C_ODD + 16 + h, j, PB[4 + n % 4][:, 0:T], s_g)
            pe.wait_ge(s_y, 2 * H)
            down(2, O, lambda k: None)

            sumsq(3)
            pe.wait_ge(s_ht, 4 * DK)
            router = param_("router").rearrange("p (k e) -> p k e", e=E)
            for t in range(NT):
                for k in range(DK):
                    last = mm(PB[0][0:TOK[t], t * E:(t + 1) * E], HT[:, k, t * P:t * P + TOK[t]], router[:, k, :],
                              start=(k == 0), stop=(k == DK - 1))
            last.then_inc(s_lg, 1)
            for i in range(2 * NT):
                t, half = i // 2, i % 2
                if i >= 4:
                    pe.wait_ge(s_hx, i - 3)
                for k in range(4):
                    last = turn(PB[2 + i % 4][0:TOK[t], k * P:(k + 1) * P],
                                HT[:, 4 * half + k, t * P:t * P + TOK[t]], ident)
                last.then_inc(s_ht2, 1)
            pe.wait_ge(s_sel, 1)
            for t in range(NT):
                for u in range(t):
                    mm(PB[1][:, t * E:(t + 1) * E], const_("ones"), SE[:, u, :], start=(u == 0), stop=False)
                mm(PB[1][:, t * E:(t + 1) * E], const_("below"), SE[:, t, :], start=(t == 0), stop=True)
            for t in range(NT):
                last = mm(PB[1][:, NT * E:(NT + 1) * E], const_("ones"), SE[:, t, :], start=(t == 0), stop=(t == NT - 1))
            last.then_inc(s_rk, 1)
            pe.wait_ge(s_hx, 2 * NT)
            pe.wait_ge(s_items, 1)
            n_items = pe.value_load(EII[0:1, MAXI:MAXI + 1], min_val=E, max_val=MAXI)
            with pe.Fori(0, n_items) as it:
                pe.wait_ge(s_oh, it + 1)
                for k in range(DK):
                    for t in range(NT):
                        last = mm(PB[k // 4][:, (k % 4) * P:(k % 4 + 1) * P], HX[0:TOK[t], t, k * P:(k + 1) * P],
                                  OH[0:TOK[t], t, :], start=(t == 0), stop=(t == NT - 1))
                    if k % 4 == 3:
                        last.then_inc(s_ga, 1)
                for t in range(NT):
                    last = turn(PB[6][:, t * P:t * P + TOK[t]], OG[0:TOK[t], t, :], ident[0:TOK[t], 0:TOK[t]])
                last.then_inc(s_oht, 1)

                def hidden(f):
                    if f >= 2:
                        pe.wait_ge(s_ac, it * MSTEPS + f - 1)
                    for g, kind in enumerate(("gate", "up")):
                        c = PLACE[(kind, f)]
                        q = C_MOE + c
                        pe.wait_ge(s_ring[q % RING], it * (16 * MCH // RING) + 16 * (q // RING + 1))
                        w = as_in(chunk(q))
                        for k in range(DK):
                            if f == 0 and k % 4 == 0:
                                pe.wait_ge(s_xe, it * 2 + k // 4 + 1)
                            last = mm(PB[2 + f % 2][:, g * IC:(g + 1) * IC], XE[:, k, :], w[:, k, :],
                                      start=(k == 0), stop=(k == DK - 1))
                    last.then_inc(s_mm, 1)

                def turn_hidden(f):
                    pe.wait_ge(s_ac, it * MSTEPS + f + 1)
                    if f == 0:
                        pe.wait_ge(s_ot, it + 1)
                    if f >= 2:
                        pe.wait_ge(s_ate, it * MSTEPS + f - 1)
                    for j in range(2):
                        last = turn(PB[6 + f % 2][:, j * P:(j + 1) * P], AC[:, f % 2, j * P:(j + 1) * P], ident)
                    last.then_inc(s_at, 1)

                def project_down(f):
                    c = PLACE[("down", f)]
                    q = C_MOE + c
                    pe.wait_ge(s_ring[q % RING], it * (16 * MCH // RING) + 16 * (q // RING + 1))
                    pe.wait_ge(s_ate, it * MSTEPS + f + 1)
                    w = chunk(q).rearrange("p (k n) -> p k n", n=D)
                    for j in range(2):
                        for half in range(2):
                            last = mm(PB[4 + half][:, :], AT[:, f % 2, j * P:(j + 1) * P],
                                      w[:, j, half * 512:(half + 1) * 512],
                                      start=(f == 0 and j == 0), stop=(f == MSTEPS - 1 and j == 1))
                    last.then_inc(s_dn, 1)

                for f in range(MSTEPS):
                    hidden(f)
                    if f >= 1:
                        turn_hidden(f - 1)
                    if f >= 2:
                        project_down(f - 2)
                turn_hidden(MSTEPS - 1)
                project_down(MSTEPS - 2)
                project_down(MSTEPS - 1)
                for k in range(DK):
                    pe.wait_ge(s_yee, it * 2 + k // 4 + 1)
                    if k >= 2:
                        pe.wait_ge(s_add, it * DK + k - 1)
                    mm(PB[k % 2][:, 0:T], YE[:, k * P:(k + 1) * P], OT, start=True, stop=True).then_inc(s_sca, 1)
            pe.wait_ge(s_add, n_items * DK)
            for i in range(2 * NT):
                t, half = i // 2, i % 2
                for k in range(4):
                    last = turn(PB[i][0:TOK[t], k * P:(k + 1) * P], XT[:, 4 * half + k, t * P:t * P + TOK[t]], ident)
                last.then_inc(s_yt, 1)

        @block.scalar
        def _(act):
            func = nc.scalar.activation

            def norm_act(r):
                for i in range(4):
                    act.wait_ge(s_xt, DK * r + 2 * i + 2)
                    func(SQ[:, 2 * i:2 * i + 2, :], XT[:, 2 * i:2 * i + 2, :], ACT.Square).then_inc(s_sq, 1)
                act.wait_ge(s_ms, r + 1)
                func(RS[:, 0, :], PB[4][:, 0:T], ACT.Sqrt, bias=eps).then_inc(s_rt, 1)

            act.wait_ge(s_const, 32)
            for c in range(CT):
                act.wait_ge(s_cct, c + 1)
                func(UF[:, c, :, 0:W - 1], PB[4 + c][:, 0:NS * (W - 1)].rearrange("p (b w) -> p b w", w=W - 1),
                     ACT.Copy).then_inc(s_win, 1)
            norm_act(0)
            for c in range(CT):
                act.wait_ge(s_ag, 4 * (c // 2) + 2 + c % 2 + 1)
                func(SG[:, c, :], PB[4 * (c // 2) + 2 + c % 2][:, 0:T], ACT.Sigmoid).then_inc(s_sig, 1)
            for n in range(2 * HP):
                act.wait_ge(s_qk, n + 1)
                func(QR[:, n, :], PB[n][:, 0:T], ACT.Copy)
                func(SQ[:, n, :], PB[n][:, 0:T], ACT.Square).then_inc(s_qks, 1)
            for m in range(2 * NT):
                c, t = m // NT, m % NT
                act.wait_ge(s_vp, m + 1)
                func(VT[0:TOK[t], t, c * IC:(c + 1) * IC], PB[m][0:TOK[t], 0:IC], ACT.Copy).then_inc(s_vev, 1)
            for n in range(2 * HP):
                act.wait_ge(s_qms, n + 1)
                if n >= 2:
                    act.wait_ge(s_qn, n - 1)
                func(RS[:, n % 2, :], PB[6 + n % 2][:, 0:T], ACT.Sqrt, bias=eps).then_inc(s_qrt, 1)
            act.wait_ge(s_ut, 1)
            func(UO[:], PB[4][0:W - 1, :], ACT.Copy).then_inc(s_uo, 1)
            act.wait_ge(s_ut, 2)
            func(US[:], PB[5][0:NS, :], ACT.Copy).then_inc(s_uo, 1)
            act.wait_ge(s_qs, 1)
            func(QS[:], PB[3][0:NS, :], ACT.Copy).then_inc(s_qse, 1)
            for t in range(NT):
                act.wait_ge(s_ktm, t + 1)
                func(KO[0:TOK[t], t, :], PB[t][0:TOK[t], :], ACT.Copy).then_inc(s_kto, 1)
            bias = param_("bias")
            for h in range(H):
                act.wait_ge(s_z, h + 1)
                func(Z[:, h * ZW:(h + 1) * ZW], PB[h % 4][:, 0:ZW], ACT.Identity, bias=bias[:, h:h + 1],
                     scale=HD ** -0.5).then_inc(s_zev, 1)
            step = 0
            for g in range(2):
                part = slice(g * ZP // 2, ZP // 2 if g == 0 else ZP + ZS)
                act.wait_ge(s_zev, 4 * (g + 1))
                if g == 1:
                    act.wait_ge(s_zs, 1)
                for src, f, kw in ((Z, ACT.Abs, {}), (L, ACT.Exp, dict(scale=-1.0)), (L, ACT.Ln, dict(bias=1.0))):
                    if step % 3:
                        act.wait_ge(s_ach, step - step // 3)
                    func(L[:, part], src[:, part], f, **kw).then_inc(s_ln if f == ACT.Ln else s_ach, 1)
                    step += 1
            for g in range(2):
                part = slice(g * ZP // 2, ZP // 2 if g == 0 else ZP + ZS)
                act.wait_ge(s_la, 4 if g == 0 else H + 1)
                func(A[:, part], A[:, part], ACT.Exp).then_inc(s_exp, 1)
            act.wait_ge(s_cd, 1)
            func(CQ[:], CD[:], ACT.Square).then_inc(s_cq, 1)
            act.wait_ge(s_cv, 1)
            func(RS[:, 0, :], PB[2][:, 0:T], ACT.Sqrt, bias=eps).then_inc(s_crt, 1)
            ln_b = param_("ln_b")
            for c in range(CT):
                act.wait_ge(s_cn, c + 1)
                func(MIX[:, c, :], CD[:, c, :], ACT.Silu, bias=ln_b[:, c:c + 1]).then_inc(s_mixc, 1)

            norm_act(1)
            for i in range(FT):
                c, j = i // 2, i % 2
                act.wait_ge(s_gu, 4 * c + j + 1)
                if i >= 2:
                    act.wait_ge(s_hid, i - 1)
                func(GA[:, i % 2, :], PB[4 * (c % 2) + j][:, 0:T], ACT.Silu).then_inc(s_silu, 1)

            norm_act(2)
            act.wait_ge(s_done, 16 * 7)
            for m in range(NT * H):
                c, t = m // NT, m % NT
                act.wait_ge(s_rv, m + 1)
                func(VR[0:TOK[t], t, c * IC:(c + 1) * IC], PB[m % 4][0:TOK[t], 0:IC], ACT.Copy).then_inc(s_rve, 1)
            act.wait_ge(s_ks, 1)
            for i in range(2):
                func(KS[0:NS, i * 512:(i + 1) * 512], PB[4 + i][0:NS, :], ACT.Copy).then_inc(s_kse, 1)
            kdecay = const_("kdecay")
            for h in range(H):
                act.wait_ge(s_kt, h + 1)
                if h >= 2:
                    act.wait_ge(s_rp, h - 1)
                for m in range(2):
                    last = func(KD[:, h % 2, m * P:(m + 1) * P], PB[2 + h % 2][:, m * P:(m + 1) * P], ACT.Copy,
                                scale=kdecay[:, 2 * h + m:2 * h + m + 1])
                last.then_inc(s_kde, 1)
                for j in range(2):
                    act.wait_ge(s_o, 2 * h + j + 1)
                    func(O[:, 2 * h + j, 0:SEQ], PB[4 + 2 * (h % 2) + j][:, 0:SEQ], ACT.Copy).then_inc(s_oe, 1)
            for h in range(H):
                act.wait_ge(s_os, h + 1)
                func(O[:, 2 * h:2 * h + 2, SEQ:T], PB[h % 2][:, 0:2 * NS].rearrange("p (j b) -> p j b", b=NS),
                     ACT.Copy).then_inc(s_ose, 1)
            for h in range(H):
                act.wait_ge(s_od, h + 1)
                if h >= 2:
                    act.wait_ge(s_ov, h - 1)
                func(OQ[:, h % 2], OD[:, h % 2], ACT.Square).then_inc(s_oq, 1)
                act.wait_ge(s_ov, h + 1)
                if h >= 2:
                    act.wait_ge(s_on, 2 * (h - 1))
                func(RS[:, h % 2, :], PB[2 + h % 2][:, 0:T], ACT.Sqrt, bias=eps).then_inc(s_ort, 1)
                for j in range(2):
                    n = 2 * h + j
                    act.wait_ge(s_g, n + 1)
                    if n >= 2:
                        act.wait_ge(s_y, n - 1)
                    func(R2[:, n % 2, :], PB[4 + n % 4][:, 0:T], ACT.Silu).then_inc(s_gs, 1)

            norm_act(3)
            for i in range(2 * NT):
                t, half = i // 2, i % 2
                act.wait_ge(s_ht2, i + 1)
                func(HX[0:TOK[t], t, half * 512:(half + 1) * 512], PB[2 + i % 4][0:TOK[t], :], ACT.Copy)\
                    .then_inc(s_hx, 1)
            act.wait_ge(s_lgx, 1)
            func(GE[:, :, 0], MX[:, :, 2], ACT.Exp).then_inc(s_e2, 1)
            act.wait_ge(s_items, 1)
            n_items = act.value_load(EII[0:1, MAXI:MAXI + 1], min_val=E, max_val=MAXI)
            with act.Fori(0, n_items) as it:
                for i in range(2):
                    act.wait_ge(s_ga, it * 2 + i + 1)
                    func(XE[:, 4 * i:4 * i + 4, :], PB[i][:, :].rearrange("p (k n) -> p k n", n=P), ACT.Copy)\
                        .then_inc(s_xe, 1)
                for f in range(MSTEPS + 1):
                    if f < MSTEPS:
                        act.wait_ge(s_mm, it * MSTEPS + f + 1)
                        if f >= 2:
                            act.wait_ge(s_ac, it * MSTEPS + f - 1)
                        func(SI[:, f % 2, :], PB[2 + f % 2][:, 0:IC], ACT.Silu).then_inc(s_si, 1)
                    if f >= 1:
                        act.wait_ge(s_at, it * MSTEPS + f)
                        if f >= 3:
                            act.wait_ge(s_dn, it * MSTEPS + f - 2)
                        func(AT[:, (f - 1) % 2, :], PB[6 + (f - 1) % 2][:, 0:2 * P], ACT.Copy).then_inc(s_ate, 1)
                act.wait_ge(s_dn, (it + 1) * MSTEPS)
                for i in range(2):
                    func(YE[:, i * 512:(i + 1) * 512], PB[4 + i][:, :], ACT.Copy).then_inc(s_yee, 1)
            for i in range(2 * NT):
                t, half = i // 2, i % 2
                act.wait_ge(s_yt, i + 1)
                func(YO[0:TOK[t], t, half * 512:(half + 1) * 512], PB[i][0:TOK[t], :], ACT.Copy).then_inc(s_yo, 1)

        @block.vector
        def _(dve):
            V = nc.vector
            steps = [0]

            def link(ins):
                steps[0] += 1
                ins.then_inc(s_dch, 1)
                dve.wait_ge(s_dch, steps[0])

            def norm_dve(r, gain):
                dve.wait_ge(s_rt, r + 1)
                link(V.reciprocal(RS[:, 1, :], RS[:, 0, :]))
                g = param_(gain)
                for k in range(DK):
                    V.scalar_tensor_tensor(out=HT[:, k, :], in0=XT[:, k, :], scalar=g[:, k:k + 1], in1=RS[:, 1, :],
                                           op0=ALU.mult, op1=ALU.mult).then_inc(s_ht, 1)

            def add_down(d):
                _, _, kt, before = DOWN[d]
                n = len(down_parts(kt))
                for half in range(2):
                    dve.wait_ge(s_down, before + n * (half + 1))
                    for j in range(4):
                        x = XT[:, 4 * half + j, :]
                        V.tensor_tensor(x, x, PB[4 * (1 - half) + j][:, 0:T], ALU.add).then_inc(s_xt, 1)

            for k in range(DK):
                dve.wait_ge(s_turn, k + 1)
                V.tensor_copy(XT[:, k, :], PB[k % 4][:, 0:T]).then_inc(s_xt, 1)
            norm_dve(0, "g0")
            dve.wait_ge(s_win, CT)
            for c in range(CT):
                dve.wait_ge(s_sig, c + 1)
                bank = PB[4 * (c // 2) + c % 2]
                V.tensor_tensor(U[:, c, W - 1:W - 1 + SEQ], bank[:, 0:SEQ], SG[:, c, 0:SEQ], ALU.mult)
                V.tensor_tensor(UF[:, c, :, W - 1], bank[:, SEQ:T], SG[:, c, SEQ:T], ALU.mult).then_inc(s_u, 1)
            dve.wait_ge(s_u, CT)
            dve.wait_ge(s_zero, 1)
            cw = param_("conv_w").rearrange("p (c w) -> p c w", w=W)
            cb = param_("conv_b")
            taps = steps[0]
            for w in range(W):
                for c in range(CT):
                    u = U[:, c, w:w + SEQ]
                    if w == 0:
                        V.tensor_scalar(CA[:, c, 0:SEQ], u, cw[:, c, w:w + 1], cb[:, c:c + 1], ALU.mult, ALU.add)\
                            .then_inc(s_dch, 1)
                    else:
                        dve.wait_ge(s_dch, taps + CT * (w - 1) + c + 1)
                        V.scalar_tensor_tensor(out=CA[:, c, 0:SEQ], in0=u, scalar=cw[:, c, w:w + 1],
                                               in1=CA[:, c, 0:SEQ], op0=ALU.mult, op1=ALU.add).then_inc(s_dch, 1)
            for c in range(CT):
                V.tensor_tensor(SW[:, c], UF[:, c], cw[:, c:c + 1, :].to_broadcast([P, NS, W]), ALU.mult)\
                    .then_inc(s_dch, 1)
            steps[0] = taps + CT * (W + 1)
            dve.wait_ge(s_dch, steps[0])
            link(V.tensor_reduce(CA[:, :, SEQ:T], SW[:], AX.X, ALU.add))
            for c in range(CT):
                V.tensor_scalar(CA[:, c, SEQ:T], CA[:, c, SEQ:T], cb[:, c:c + 1], None, ALU.add).then_inc(s_conv, 1)
            for n in range(2 * HP):
                dve.wait_ge(s_qrt, n + 1)
                link(V.reciprocal(RS[:, n % 2, :], RS[:, n % 2, :]))
                V.scalar_tensor_tensor(out=QN[:, n, :], in0=QR[:, n, :], scalar=param_("q_g" if n < HP else "k_g"),
                                       in1=RS[:, n % 2, :], op0=ALU.mult, op1=ALU.mult).then_inc(s_qn, 1)
            zs = Z[:, ZP:ZP + ZS].rearrange("p (g b h) -> p g b h", b=NS, h=H)
            dve.wait_ge(s_kpage, 16 * NS * PAGES)
            for b in range(NS):
                dve.wait_ge(s_qb, b + 1)
                V.tensor_tensor(KQ[:], KV[:, b * PAGES:(b + 1) * PAGES, :],
                                PB[4 + b % 4][:, 0:SBW].rearrange("p (o n) -> p o n", o=1)
                                .to_broadcast([P, PAGES, SBW]), ALU.mult).then_inc(s_kq, 1)
                dve.wait_ge(s_kq, b + 1)
                link(V.tensor_reduce(zs[:, :, b, :], KQ[:].rearrange("p g (h d) -> p g h d", d=HD), AX.X, ALU.add))
            V.scalar_tensor_tensor(out=Z[:, ZP:ZP + ZS].rearrange("p (g h) -> p g h", h=H),
                                   in0=Z[:, ZP:ZP + ZS].rearrange("p (g h) -> p g h", h=H), scalar=HD ** -0.5,
                                   in1=param_("bias").rearrange("p (o h) -> p o h", o=1)
                                   .to_broadcast([P, PAGES * NS, H]), op0=ALU.mult, op1=ALU.add).then_inc(s_zs, 1)
            below = const_("below").rearrange("p (a b n) -> p a b n", a=1, b=1)

            def mask(buf, g, done):
                v = buf[:, g * ZP // 2:(g + 1) * ZP // 2].rearrange("p (h c n) -> p h c n", h=4, c=3)[:, :, 0:3:2, :]
                V.tensor_tensor(v, v, below.to_broadcast([P, 4, 2, P]), ALU.mult).then_inc(done, 1)

            for g in range(2):
                part = slice(g * ZP // 2, ZP // 2 if g == 0 else ZP + ZS)
                dve.wait_ge(s_ln, g + 1)
                link(V.scalar_tensor_tensor(out=A[:, part], in0=Z[:, part], scalar=0.0, in1=L[:, part],
                                            op0=ALU.min, op1=ALU.subtract))
                link(V.scalar_tensor_tensor(out=Z[:, part], in0=Z[:, part], scalar=0.0, in1=L[:, part],
                                            op0=ALU.max, op1=ALU.add))
                mask(Z, g, s_lk)
            for h in range(H + 1):
                dve.wait_ge(s_suf, h + 1)
                n = ZW if h < H else ZS
                a = A[:, h * ZW:h * ZW + n]
                V.tensor_tensor(a, a, PB[h % 4][:, 0:n], ALU.add).then_inc(s_la, 1)
            for g in range(2):
                dve.wait_ge(s_exp, g + 1)
                mask(A, g, s_a)
            dve.wait_ge(s_cm, 1)
            V.tensor_tensor(CD[:], CA[:], PB[1][:, 0:T].rearrange("p (o n) -> p o n", o=1).to_broadcast([P, CT, T]),
                            ALU.subtract).then_inc(s_cd, 1)
            dve.wait_ge(s_cd, 1)
            dve.wait_ge(s_crt, 1)
            link(V.reciprocal(RS[:, 0, :], RS[:, 0, :]))
            for c in range(CT):
                V.scalar_tensor_tensor(out=CD[:, c, :], in0=CD[:, c, :], scalar=param_("ln_g")[:, c:c + 1],
                                       in1=RS[:, 0, :], op0=ALU.mult, op1=ALU.mult).then_inc(s_cn, 1)
            for hp in range(HP):
                dve.wait_ge(s_av, 2 * hp + 2)
                V.tensor_copy(MIX[:, CT + hp, 0:SEQ], PB[4 + hp][:, 0:SEQ]).then_inc(s_mixa, 1)
            dve.wait_ge(s_avs, 1)
            avs = PB[0][:, 0:HP * NS * 2].rearrange("p (a b i) -> p a b i", b=NS, i=2)
            for i in range(2):
                V.tensor_copy(MIX[i * HD:(i + 1) * HD, CT:CT + HP, SEQ:T], avs[i * HD:(i + 1) * HD, :, :, i])\
                    .then_inc(s_mixa, 1)
            add_down(0)

            norm_dve(1, "g1")
            for i in range(FT):
                c, j = i // 2, i % 2
                dve.wait_ge(s_gu, 4 * c + 2 + j + 1)
                dve.wait_ge(s_silu, i + 1)
                V.tensor_tensor(HID[:, i, :], GA[:, i % 2, :], PB[4 * (c % 2) + 2 + j][:, 0:T], ALU.mult)\
                    .then_inc(s_hid, 1)
            add_down(1)

            norm_dve(2, "g2")
            dve.wait_ge(s_done, 16 * 7)
            cos, sin = (const_(x).rearrange("p (a n) -> p a n", a=2) for x in ("cos", "sin"))
            for n in range(2 * H):
                g, h = n // H, n % H
                dve.wait_ge(s_rq, n + 1)
                bank = PB[n % 4]
                if n >= 2:
                    dve.wait_ge(s_rot, n - 1)
                V.tensor_tensor(R1[:, n % 2, :], bank[:, 0:T], cos[:, g, :], ALU.mult)
                V.tensor_tensor(R2[0:HD, n % 2, :], bank[HD:P, 0:T], sin[HD:P, g, :], ALU.mult)
                link(V.tensor_tensor(R2[HD:P, n % 2, :], bank[0:HD, 0:T], sin[0:HD, g, :], ALU.mult))
                V.tensor_tensor((QT, KT)[g][:, h, :], R1[:, n % 2, :], R2[:, n % 2, :], ALU.add).then_inc(s_rot, 1)
            dve.wait_ge(s_decay, 16)
            for h in range(H):
                dve.wait_ge(s_sc, h + 1)
                if h >= 2:
                    dve.wait_ge(s_o, 2 * (h - 1))
                V.tensor_tensor(SC[:, h % 2, :], PB[h % 2][:, 0:ZW], DT[:, h, :], ALU.mult).then_inc(s_sce, 1)
                dve.wait_ge(s_rp, h + 1)
                if h >= 2:
                    dve.wait_ge(s_rpo[h % 2], 16 * (h // 2))
                V.tensor_copy(RP[:, h % 2, :], PB[2 + h % 2][:, EV:2 * EV]).then_inc(s_rpe, 1)

            def spread_k(h):
                if h >= 2:
                    dve.wait_ge(s_out, 4 * (h - 1))
                V.tensor_tensor(KM[0:NS, h % 2, :].rearrange("p (b n) -> p b n", n=P),
                                KS[0:NS, h * P:(h + 1) * P].rearrange("p (o n) -> p o n", o=1)
                                .to_broadcast([NS, NS, P]),
                                ident[0:NS, 0:NS].rearrange("p (b o) -> p b o", o=1).to_broadcast([NS, NS, P]),
                                ALU.mult).then_inc(s_km, 1)

            dve.wait_ge(s_kse, 2)
            spread_k(0)
            for h in range(H):
                if h + 1 < H:
                    spread_k(h + 1)
                dve.wait_ge(s_state[h % 2], 16 * (h // 2 + 1))
                for g in range(4):
                    dve.wait_ge(s_out, 4 * h + g + 1)
                    s = ST[:, h % 2, g * 512:(g + 1) * 512]
                    V.scalar_tensor_tensor(out=s, in0=s, scalar=GAMMA[h], in1=PB[4 + g][:, :], op0=ALU.mult,
                                           op1=ALU.add).then_inc(s_new, 1)
            for h in range(H):
                dve.wait_ge(s_om, h + 1)
                dve.wait_ge(s_ose, h + 1)
                if h >= 2:
                    dve.wait_ge(s_on, 2 * (h - 1))
                V.tensor_tensor(OD[:, h % 2], O[:, 2 * h:2 * h + 2, :],
                                PB[h % 2][:, 0:T].rearrange("p (o n) -> p o n", o=1).to_broadcast([P, 2, T]),
                                ALU.subtract).then_inc(s_od, 1)
                dve.wait_ge(s_od, h + 1)
                dve.wait_ge(s_ort, h + 1)
                link(V.reciprocal(RS[:, h % 2, :], RS[:, h % 2, :]))
                for j in range(2):
                    n = 2 * h + j
                    V.scalar_tensor_tensor(out=O[:, n, :], in0=OD[:, h % 2, j, :],
                                           scalar=param_("gn_g")[:, n:n + 1], in1=RS[:, h % 2, :],
                                           op0=ALU.mult, op1=ALU.mult).then_inc(s_on, 1)
                for j in range(2):
                    n = 2 * h + j
                    dve.wait_ge(s_on, n + 1)
                    dve.wait_ge(s_gs, n + 1)
                    V.scalar_tensor_tensor(out=O[:, n, :], in0=O[:, n, :], scalar=param_("gn_b")[:, n:n + 1],
                                           in1=R2[:, n % 2, :], op0=ALU.add, op1=ALU.mult).then_inc(s_y, 1)
            add_down(2)

            norm_dve(3, "g3")
            dve.wait_ge(s_down, NDOWN)
            link(V.memset(LG[:], 0.0))
            dve.wait_ge(s_lg, 1)
            for t in range(NT):
                link(V.tensor_copy(LG[0:TOK[t], t, :], PB[0][0:TOK[t], t * E:(t + 1) * E]))
            for t in range(NT):
                link(V.max(MX[:, t, :], LG[:, t, :]))
                link(V.max_index(MI[:, t, :], MX[:, t, :], LG[:, t, :]))
            link(V.tensor_copy(MIF[:], MI[:]))
            V.tensor_tensor(MX[:, :, 2], MX[:, :, 1], MX[:, :, 0], ALU.subtract).then_inc(s_lgx, 1)
            dve.wait_ge(s_lgx, 1)
            io8 = const_("iota8").rearrange("p (o e) -> p o e", o=1).to_broadcast([P, NT, E])
            link(V.tensor_tensor(S1[:], io8, MIF[:, :, 0:1].to_broadcast([P, NT, E]), ALU.is_equal))
            link(V.tensor_tensor(SE[:], io8, MIF[:, :, 1:2].to_broadcast([P, NT, E]), ALU.is_equal))
            dve.wait_ge(s_e2, 1)
            link(V.tensor_scalar(GE[:, :, 1], GE[:, :, 0], 1.0, None, ALU.add))
            link(V.reciprocal(GE[:, :, 2], GE[:, :, 1]))
            link(V.tensor_tensor(GE[:, :, 3], GE[:, :, 2], GE[:, :, 0], ALU.mult))
            GT = M1[:, 0:NT, :]
            G2 = M2[:, 0:NT, :]
            link(V.tensor_tensor(GT, S1[:], GE[:, :, 2:3].to_broadcast([P, NT, E]), ALU.mult))
            link(V.tensor_tensor(G2, SE[:], GE[:, :, 3:4].to_broadcast([P, NT, E]), ALU.mult))
            link(V.tensor_tensor(RK[:], GT, G2, ALU.add))
            link(V.tensor_tensor(SE[:], SE[:], S1[:], ALU.add))
            link(V.tensor_tensor(SE[:, 2, :], SE[:, 2, :], C[:, CONST["rows"][0]:CONST["rows"][0] + 1]
                                 .to_broadcast([P, E]), ALU.mult))
            link(V.tensor_copy(LG[:], RK[:]))
            V.tensor_copy(S1[:], SE[:]).then_inc(s_sel, 1)
            dve.wait_ge(s_sel, 1)
            dve.wait_ge(s_rk, 1)
            rank = PB[1][:, 0:NT * E].rearrange("p (t e) -> p t e", e=E)
            count = PB[1][:, NT * E:(NT + 1) * E]
            link(V.scalar_tensor_tensor(out=RK[:], in0=rank, scalar=1000.0, in1=SE[:], op0=ALU.add, op1=ALU.mult))
            link(V.tensor_scalar(RK[:], RK[:], -1000.0, None, ALU.add))
            link(V.tensor_scalar(TI[:, 0, :], count, 128.5, None, ALU.is_gt))
            link(V.tensor_scalar(TI[:, 1, :], count, 256.5, None, ALU.is_gt))
            link(V.scalar_tensor_tensor(out=TI[:, 2, :], in0=TI[:, 0, :], scalar=1.0, in1=TI[:, 1, :],
                                        op0=ALU.add, op1=ALU.add))
            link(V.tensor_tensor(LT[:], const_("lt8").rearrange("p (a b) -> p a b", b=E),
                                 TI[:, 2:3, :].to_broadcast([P, E, E]), ALU.mult))
            link(V.tensor_reduce(TI[:, 3, :], LT[:], AX.X, ALU.add))
            link(V.tensor_tensor(TI[:, 4, :], TI[:, 3, :], TI[:, 2, :], ALU.add))
            item = const_("item").rearrange("p (i e) -> p i e", e=E)
            link(V.tensor_tensor(M1[:], item, TI[:, 3:4, :].to_broadcast([P, MAXI, E]), ALU.is_ge))
            link(V.tensor_tensor(M2[:], item, TI[:, 4:5, :].to_broadcast([P, MAXI, E]), ALU.is_lt))
            link(V.tensor_tensor(M1[:], M1[:], M2[:], ALU.mult))
            link(V.tensor_tensor(M2[:], item, TI[:, 3:4, :].to_broadcast([P, MAXI, E]), ALU.subtract))
            link(V.tensor_tensor(M2[:], M2[:], M1[:], ALU.mult))
            link(V.tensor_reduce(BA, M2[:], AX.X, ALU.add))
            link(V.tensor_tensor(M3[:], const_("expert").rearrange("p (i e) -> p i e", e=E), M1[:], ALU.mult))
            link(V.tensor_reduce(EI[:, 0:MAXI], M3[:], AX.X, ALU.add))
            link(V.tensor_reduce(EI[:, MAXI:MAXI + 1], TI[:, 2, :], AX.X, ALU.add))
            for src, dst in ((RK, CR), (LG, CG)):
                for t in range(NT):
                    m = M4[:, t, :].rearrange("p (i e) -> p i e", e=E)
                    link(V.tensor_tensor(m, M1[:], src[:, t:t + 1, :].to_broadcast([P, MAXI, E]), ALU.mult))
                    link(V.tensor_reduce(dst[:, :, t], m, AX.X, ALU.add))
            for t in range(NT):
                link(V.scalar_tensor_tensor(out=CR[:, :, t], in0=BA, scalar=-128.0, in1=CR[:, :, t],
                                            op0=ALU.mult, op1=ALU.add))
            V.tensor_copy(EII[:], EI).then_inc(s_items, 1)
            dve.wait_ge(s_items, 1)
            n_items = dve.value_load(EII[0:1, MAXI:MAXI + 1], min_val=E, max_val=MAXI)
            slot = const_("slot")
            base = steps[0]
            with dve.Fori(0, n_items) as it:
                V.tensor_copy(CU[:, 0:1, :], CR[:, bass.ds(it, 1), :]).then_inc(s_dch, 1)
                V.tensor_copy(CU[:, 1:2, :], CG[:, bass.ds(it, 1), :]).then_inc(s_dch, 1)
                dve.wait_ge(s_dch, it * 2 + base + 2)
                for t in range(NT):
                    V.tensor_scalar(OH[:, t, :], slot, CU[:, 0, t:t + 1], None, ALU.is_equal)
                    last = V.tensor_scalar(OG[:, t, :], slot, CU[:, 0, t:t + 1], CU[:, 1, t:t + 1], ALU.is_equal,
                                           ALU.mult)
                last.then_inc(s_oh, 1)
                dve.wait_ge(s_oht, it + 1)
                V.tensor_copy(OT, PB[6][:, 0:T]).then_inc(s_ot, 1)
                for f in range(MSTEPS):
                    dve.wait_ge(s_si, it * MSTEPS + f + 1)
                    if f >= 2:
                        dve.wait_ge(s_at, it * MSTEPS + f - 1)
                    V.tensor_tensor(AC[:, f % 2, :], SI[:, f % 2, :], PB[2 + f % 2][:, IC:2 * IC], ALU.mult)\
                        .then_inc(s_ac, 1)
                for k in range(DK):
                    dve.wait_ge(s_sca, it * DK + k + 1)
                    V.tensor_tensor(XT[:, k, :], XT[:, k, :], PB[k % 2][:, 0:T], ALU.add).then_inc(s_add, 1)


def tables():
    C = np.zeros((P, NCONST), np.float32)
    p = np.arange(P)

    def put(name, a):
        at, n = CONST[name]
        C[:, at:at + n] = np.broadcast_to(np.asarray(a, np.float64), (P, n))

    put("ident", np.eye(P))
    put("negtri", -(p[:, None] > p[None, :]).astype(float))
    put("negones", -1.0)
    put("below", (p[:, None] < p[None, :]).astype(float))
    put("ones", 1.0)
    put("mean_d", 1.0 / D)
    put("mean_ch", 1.0 / CH)
    put("mean_hd", (p[:, None] // HD == p[None, :] // HD) / HD)
    put("mean_ev", 1.0 / EV)
    half = P // 2
    inv = np.float32(10000.0) ** (-np.linspace(0.0, 1.0, half, dtype=np.float32))
    pos = np.concatenate([np.arange(SEQ), np.full(NS, PAST)]).astype(np.float32)
    ang = (pos[None, :] * inv[:, None]).astype(np.float32)
    cos, sin = np.cos(ang), np.sin(ang)
    scale = np.float32(P) ** np.float32(-0.5)
    put("cos", np.concatenate([np.concatenate([cos, cos]), np.concatenate([cos, cos]) * scale], axis=1))
    put("sin", np.concatenate([np.concatenate([sin, -sin]), np.concatenate([sin, -sin]) * scale], axis=1))
    put("slot", p)
    gamma = np.array(GAMMA)
    put("kdecay", np.stack([gamma[h] ** (SEQ - 1 - (m * P + p)) for h in range(H) for m in range(2)], axis=1))
    e = np.arange(E)
    put("iota8", e)
    put("lt8", (e[None, :] < e[:, None]).astype(float).ravel())
    put("item", np.repeat(np.arange(MAXI), E))
    put("expert", np.tile(e, MAXI))
    put("eps", EPS)
    put("rows", (p < NS).astype(float)[:, None])
    key, query = np.meshgrid(np.arange(SEQ), np.arange(SEQ), indexing="ij")
    diff = query - key
    table = []
    for h in range(H):
        d = np.where(diff >= 0, gamma[h] ** np.maximum(diff, 0), 0.0)
        table += [d[0:P], d[P:SEQ, P:SEQ]]
    return C, np.concatenate(table, axis=1).astype(np.float32)


_OUTS = [(1, SEQ, D), (NS, 1, D), (1, 1, SEQ, H, HD), (1, 1, SEQ, H, HD), (1, NS, 1, H, HD), (1, NS, 1, H, HD),
         (1, 1, W - 1, CH), (1, NS, W - 1, CH), (1, 1, H, P, EV), (1, NS, H, P, EV)]
_INS = ["x_prompt", "x_sample", "cache_sb_k", "cache_sb_v", "cache_conv", "state_ret", "page_table"]
_WEIGHTS = ["w_in_even", "w_out_even", "ffn_w_gate", "ffn_w_up", "ffn_w_down", "w_in_odd", "w_out_odd",
            "moe_w_gate", "moe_w_up", "moe_w_down"]


def kernel(**inputs):
    import concourse.bacc as bacc
    from concourse.bass_utils import run_bass_kernel_spmd

    a = {k: np.asarray(v) for k, v in inputs.items()}
    const, decay = tables()

    def tiles(x):
        return x.reshape(-1, P).T

    param = np.concatenate([
        tiles(a["norm_mix_even"][0]), tiles(a["norm_ffn_even"][0]), tiles(a["norm_mix_odd"][0]),
        tiles(a["norm_ffn_odd"][0]), a["conv_w"][0].reshape(W, CT, P).transpose(2, 1, 0).reshape(P, CT * W),
        tiles(a["conv_b"][0]), tiles(a["conv_ln_g"][0]), tiles(a["conv_ln_b"][0]),
        np.tile(a["sb_q_norm"][0], 2)[:, None], np.tile(a["sb_k_norm"][0], 2)[:, None],
        np.broadcast_to(a["sb_bias"][0], (P, H)), tiles(a["ret_gn_g"][0]), tiles(a["ret_gn_b"][0]),
        a["router_w"][0].reshape(DK, P, E).transpose(1, 0, 2).reshape(P, DK * E)], axis=1)
    arrays = {n: a[n] for n in _INS}
    arrays.update(const=const, decay=decay, param=param)
    arrays.update({n: a[n] for n in _WEIGHTS})
    nc = bacc.Bacc("TRN2", target_bir_lowering=False, num_devices=1)
    feed, args = {}, []
    for name, x in arrays.items():
        x = np.ascontiguousarray(x)
        feed[f"in_{name}"] = x
        args.append(nc.dram_tensor(f"in_{name}", x.shape, mybir.dt.from_np(x.dtype), kind="ExternalInput").ap())
    names = ["y_prompt", "y_sample", "k_prompt", "v_prompt", "k_sample", "v_sample", "conv_prompt", "conv_sample",
             "ret_prompt", "ret_sample"]
    for name, shape in zip(names, _OUTS):
        args.append(nc.dram_tensor(f"out_{name}", shape, F32, kind="ExternalOutput").ap())
    build(nc, *args)
    r = run_bass_kernel_spmd(nc, [feed], core_ids=[0])
    return tuple(r.results[0][f"out_{name}"] for name in names)
```

```python
from contextlib import ExitStack

import concourse.bass as bass
from concourse import mybir
import numpy as np

F32 = mybir.dt.float32
F32R = mybir.dt.float32r
I32 = mybir.dt.int32
U32 = mybir.dt.uint32
ALU = mybir.AluOpType
ACT = mybir.ActivationFunctionType
AX = mybir.AxisListType

P = 128
D = 1024
DK = D // P
SEQ = 256
NS = 8
T = SEQ + NS
NT = 3
TOK = [P, P, NS]
CH = 512
CT = CH // P
W = 31
H = 8
HD = 64
SBW = H * HD
HP = SBW // P
PAST = 256
PAGES = PAST // P
FF = 2816
FT = FF // P
RV = 2048
EV = RV // H
E = 8
FE = 3584
EPS = 1e-6
ZW = 384
ZP = H * ZW
ZS = PAGES * NS * H
GAMMA = [1.0 - 2.0 ** (-5 - h) for h in range(H)]

RING = 3
MRING = 7
WRING = 3
CW = 2048
IC = CW // DK
MSTEPS = FE // IC
MCH = 3 * MSTEPS
ARENA = 22800
MAXI = 12
TI_N = MAXI + 1
assert MCH % MRING == 0 and MCH % WRING == 0

CONST = {}
_at = 0
for _name, _n in [("ident", P), ("negtri", P), ("negones", P), ("below", P), ("ones", P), ("mean_d", P),
                  ("mean_ch", P), ("mean_hd", P), ("mean_ev", P), ("cos", 2 * T), ("sin", 2 * T),
                  ("slot", P), ("kdecay", 2 * H), ("iota8", E), ("lt8", E * E), ("item", TI_N * E),
                  ("expert", TI_N * E), ("eps", 1), ("rows", 1)]:
    CONST[_name] = (_at, _n)
    _at += _n
NCONST = _at
PARAM = {}
_at = 0
for _name, _n in [("g0", DK), ("g1", DK), ("g2", DK), ("g3", DK), ("conv_w", CT * W), ("conv_b", CT),
                  ("ln_g", CT), ("ln_b", CT), ("q_g", 1), ("k_g", 1), ("bias", H), ("gn_g", RV // P),
                  ("gn_b", RV // P), ("router", DK * E)]:
    PARAM[_name] = (_at, _n)
    _at += _n
NPARAM = _at

C_EVEN = 0
C_OUTE = C_EVEN + 10
C_FFN = C_OUTE + 4
C_DOWN = C_FFN + 2 * FF // IC
C_ODD = C_DOWN + 12
C_OUTO = C_ODD + 24
C_MOE = C_OUTO + 8


def build(nc, x_prompt, x_sample, cache_k, cache_v, cache_conv, state_ret, page_table, const, decay, param,
          w_in_even, w_out_even, w_gate, w_up, w_down, w_in_odd, w_out_odd, m_gate, m_up, m_down,
          y_prompt, y_sample, k_prompt, v_prompt, k_sample, v_sample, conv_prompt, conv_sample,
          ret_prompt, ret_sample):
    with ExitStack() as ctx:
        def sb(name, shape, dt=F32):
            return ctx.enter_context(nc.sbuf_tensor(name, shape, dt))

        def sem(name):
            return ctx.enter_context(nc.semaphore(name))

        ring = sb("ring", [P, RING, CW])
        WH = sb("WH", [P, WRING, CW], F32R)
        WL = sb("WL", [P, WRING, CW], F32R)
        XT = sb("XT", [P, DK, T])
        HH = sb("HH", [P, DK, T], F32R)
        HL = sb("HL", [P, DK, T], F32R)
        SQ = sb("SQ", [P, DK, T])
        HT = SQ
        RS = sb("RS", [P, 2, T])
        C = sb("C", [P, NCONST])
        R = sb("R", [P, NPARAM])
        PG = sb("PG", [1, NS * PAGES], I32)
        EII = sb("EII", [P, TI_N + 1], I32)
        MI = sb("MI", [P, NT, 8], U32)
        arena_at = -(-nc.sbuf_base // 32) * 32
        sb("arena", [P, ARENA])
        PB = [ctx.enter_context(nc.psum_tensor(f"bank{i}", [P, 512], F32)) for i in range(8)]

        used = {}

        def region(stage, name, *shape, dt=F32, at=None):
            n = int(np.prod(shape))
            if at is None:
                at = used.get(stage, 0)
                used[stage] = at + -(-n // 8) * 8
            assert at + n <= ARENA, (stage, name, at + n)
            return nc.alloc_sbuf_tensor_at(f"{stage}_{name}", [P, *shape], dt, offset=arena_at + 4 * at)

        def full(ap):
            return ap.bitcast(F32)

        def const_(name, parts=P):
            at, n = CONST[name]
            return C[0:parts, at:at + n]

        def param_(name):
            at, n = PARAM[name]
            return R[:, at:at + n]

        ident = const_("ident")
        eps = const_("eps")

        KV = region("even", "KV", NS, SBW)
        Z = region("even", "Z", ZP + ZS)
        L = region("even", "L", ZP // 2 + ZS)
        A = region("even", "A", ZP + ZS)
        QR = region("even", "QR", 2 * HP, T)
        QN = region("even", "QN", 2 * HP, T)
        VT = region("even", "VT", NT, SBW)
        U = region("even", "U", CT, W - 1 + SEQ)
        UF = region("even", "UF", CT, NS, W)
        CA = region("even", "CA", CT, T)
        KO = region("even", "KO", NT, SBW)
        XI = Z[:, 0:3072].rearrange("p (a b) -> p a b", b=D)
        CC = L[:, 0:1024].rearrange("p (a b) -> p a b", b=CH)
        FVE = L[:, 0:HP * T].rearrange("p (a b) -> p a b", b=T)
        SG = Z[:, 0:CT * T].rearrange("p (a b) -> p a b", b=T)
        SW = A[:, 0:CT * NS * W].rearrange("p (a b c) -> p a b c", b=NS, c=W)
        CD = Z[:, 0:CT * T].rearrange("p (a b) -> p a b", b=T)
        CQ = Z[:, CT * T:2 * CT * T].rearrange("p (a b) -> p a b", b=T)
        UO = KO[32:32 + W - 1, 2, :]
        US = KO[64:64 + NS, 2, :]
        QS = A[0:NS, 2080:2080 + SBW]
        KQ = A[:, 1056:1056 + 2 * SBW].rearrange("p (a b) -> p a b", b=SBW)
        MIX = SQ
        HDH = region("ffn", "HDH", FT, T, dt=F32R)
        HDL = region("ffn", "HDL", FT, T, dt=F32R)
        HF = region("ffn", "HF", 2, T)
        GA = region("ffn", "GA", 2, T)
        QT = region("odd", "QT", H, T)
        KT = region("odd", "KT", H, T)
        VR = region("odd", "VR", NT, RV)
        O = region("odd", "O", 2 * H, T)
        DT = region("odd", "DT", H, 2 * P)
        ST0 = region("odd", "ST0", NS * EV)
        R1 = region("odd", "R1", 2, T)
        R2 = region("odd", "R2", 2, T)
        SC = region("odd", "SC", 2, ZW)
        KD = region("odd", "KD", 2, 2 * P)
        RP = region("odd", "RP", 2, EV)
        KM = region("odd", "KM", NS * P)
        ST = [ST0[:, :], DT[:, :, :].rearrange("p h n -> p (h n)")]
        KS = VR[32:32 + NS, 2, 0:D]
        FV = region("odd", "FV", 4, T, at=used["odd"] - NS * P - 2 * EV - 2 * 2 * P)
        YH = region("odd", "YH", 2 * H, T, dt=F32R, at=0)
        YL = region("odd", "YL", 2 * H, T, dt=F32R, at=2 * H * T)
        OD = SQ[:, 0:4, :].rearrange("p (u a) t -> p u a t", u=2)
        OQ = SQ[:, 4:8, :].rearrange("p (u a) t -> p u a t", u=2)
        HXH = region("moe", "HXH", NT, D, dt=F32R)
        HXL = region("moe", "HXL", NT, D, dt=F32R)
        XEH = region("moe", "XEH", DK, P, dt=F32R)
        XEL = region("moe", "XEL", DK, P, dt=F32R)
        OH = region("moe", "OH", NT, P, dt=F32R)
        OG = region("moe", "OG", NT, P)
        OT = region("moe", "OT", T)
        SI = region("moe", "SI", 2, IC)
        AC = region("moe", "AC", 2, IC)
        ATH = region("moe", "ATH", 2, 2 * P, dt=F32R)
        ATL = region("moe", "ATL", 2, 2 * P, dt=F32R)
        YE = region("moe", "YE", D)
        LG = region("moe", "LG", NT, E)
        MX = region("moe", "MX", NT, 8)
        MIF = region("moe", "MIF", NT, 8)
        GE = region("moe", "GE", NT, 8)
        SE = region("moe", "SE", NT, E)
        S1 = region("moe", "S1", NT, E)
        RK = region("moe", "RK", NT, E)
        TI = region("moe", "TI", 8, E)
        LT = region("moe", "LT", E, E)
        M1 = region("moe", "M1", TI_N, E)
        M2 = region("moe", "M2", TI_N, E)
        M3 = region("moe", "M3", TI_N, E)
        BA = region("moe", "BA", TI_N)
        M4 = region("moe", "M4", NT, TI_N * E)
        CR = region("moe", "CR", TI_N, NT)
        CG = region("moe", "CG", TI_N, NT)
        CU = region("moe", "CU", 2, NT)
        EI = region("moe", "EI", TI_N + 1)
        YO = region("moe", "YO", NT, D, at=0)
        used["moe"] = max(used["moe"], 10368 + 2 * H * T)
        MORE = region("moe", "MORE", MRING - RING, CW)

        s_x = sem("s_x"); s_const = sem("s_const"); s_cc = sem("s_cc"); s_pt = sem("s_pt"); s_decay = sem("s_decay")
        s_ring = [sem(f"s_ring{i}") for i in range(MRING)]
        s_hi = sem("s_hi"); s_lo = sem("s_lo")
        s_kv = [sem(f"s_kv{i}") for i in range(4)]; s_state = [sem("s_state0"), sem("s_state1")]
        s_turn = sem("s_turn"); s_xt = sem("s_xt"); s_sq = sem("s_sq"); s_ms = sem("s_ms"); s_rt = sem("s_rt")
        s_ht = sem("s_ht"); s_hh = sem("s_hh"); s_hl = sem("s_hl")
        s_zero = sem("s_zero"); s_cct = sem("s_cct"); s_win = sem("s_win")
        s_ag = sem("s_ag"); s_sig = sem("s_sig"); s_u = sem("s_u"); s_ut = sem("s_ut"); s_uo = sem("s_uo")
        s_conv = sem("s_conv"); s_cm = sem("s_cm"); s_cd = sem("s_cd"); s_cq = sem("s_cq"); s_cv = sem("s_cv")
        s_crt = sem("s_crt"); s_cn = sem("s_cn"); s_mixc = sem("s_mixc")
        s_qk = sem("s_qk"); s_qks = sem("s_qks"); s_vp = sem("s_vp"); s_vfe = sem("s_vfe"); s_vt = sem("s_vt"); s_vev = sem("s_vev"); s_qms = sem("s_qms")
        s_qrt = sem("s_qrt"); s_qn = sem("s_qn"); s_ktm = sem("s_ktm"); s_kto = sem("s_kto"); s_qs = sem("s_qs")
        s_qse = sem("s_qse"); s_z = sem("s_z"); s_zev = sem("s_zev"); s_qb = sem("s_qb"); s_kq = sem("s_kq")
        s_zs = sem("s_zs"); s_ln = sem("s_ln"); s_lk = sem("s_lk"); s_suf = sem("s_suf"); s_la = sem("s_la")
        s_exp = sem("s_exp"); s_a = sem("s_a"); s_av = sem("s_av"); s_ava = sem("s_ava"); s_avs = sem("s_avs")
        s_mixa = sem("s_mixa"); s_mh = sem("s_mh"); s_ml = sem("s_ml")
        s_down = sem("s_down")
        s_gu = sem("s_gu"); s_silu = sem("s_silu"); s_hid = sem("s_hid"); s_hdh = sem("s_hdh"); s_hdl = sem("s_hdl")
        s_rq = sem("s_rq"); s_rot = sem("s_rot"); s_rv = sem("s_rv"); s_rvf = sem("s_rvf"); s_rvt = sem("s_rvt"); s_rve = sem("s_rve"); s_ks = sem("s_ks")
        s_kse = sem("s_kse"); s_sc = sem("s_sc"); s_sce = sem("s_sce"); s_kt = sem("s_kt"); s_kde = sem("s_kde")
        s_o = sem("s_o"); s_oe = sem("s_oe"); s_rp = sem("s_rp"); s_rpe = sem("s_rpe"); s_rpo = [sem("s_rpo0"), sem("s_rpo1")]
        s_km = sem("s_km"); s_out = sem("s_out"); s_new = sem("s_new"); s_os = sem("s_os"); s_ose = sem("s_ose")
        s_sto = [sem("s_sto0"), sem("s_sto1")]
        s_om = sem("s_om"); s_od = sem("s_od"); s_oq = sem("s_oq"); s_ov = sem("s_ov"); s_ort = sem("s_ort")
        s_on = sem("s_on"); s_g = sem("s_g"); s_gs = sem("s_gs"); s_y = sem("s_y"); s_yh = sem("s_yh"); s_yl = sem("s_yl")
        s_lg = sem("s_lg"); s_ht2 = sem("s_ht2"); s_hx = sem("s_hx"); s_hxl = sem("s_hxl"); s_lgx = sem("s_lgx"); s_e2 = sem("s_e2")
        s_sel = sem("s_sel"); s_rk = sem("s_rk"); s_items = sem("s_items"); s_oh = sem("s_oh")
        s_ga = sem("s_ga"); s_xe = sem("s_xe"); s_oht = sem("s_oht"); s_ot = sem("s_ot"); s_mm = sem("s_mm")
        s_si = sem("s_si"); s_ac = sem("s_ac"); s_at = sem("s_at"); s_ate = sem("s_ate"); s_atl = sem("s_atl"); s_ye = sem("s_ye")
        s_yee = sem("s_yee"); s_sca = sem("s_sca"); s_add = sem("s_add"); s_yt = sem("s_yt"); s_yo = sem("s_yo")
        s_dn = sem("s_dn")
        s_ach = sem("s_ach"); s_dch = sem("s_dch")
        s_ydone = sem("s_ydone"); s_done = sem("s_done")
        ctx.enter_context(nc.allow_non_contiguous_dma(reason="small rows"))
        block = ctx.enter_context(nc.Block())

        def slot_of(q):
            return q % RING if q < C_MOE else (q - C_MOE + C_MOE % RING) % MRING

        def chunk(q):
            n = slot_of(q)
            return ring[:, n, :] if n < RING else MORE[:, n - RING, :]

        def uses_before(q):
            dense = len([i for i in range(min(q + 1, C_MOE)) if i % RING == slot_of(q)])
            return dense + len([i for i in range(C_MOE, q + 1) if slot_of(i) == slot_of(q)])

        def icols(w, c0):
            return w[:, c0:c0 + IC].rearrange("(k p) n -> p k n", p=P)

        def as_in(ap):
            return ap.rearrange("p (k n) -> p k n", n=IC)

        def down_parts(kt):
            return [(k, min(4, kt - k)) for k in range(0, kt, 4)]

        DOWN = [(C_OUTE, w_out_even, DK, 0), (C_DOWN, w_down, FT, 4), (C_OUTO, w_out_odd, RV // P, 16)]
        NDOWN = 24

        released = [(s_ag, 2), (s_ag, 4), (s_ag, 6), (s_ag, 8), (s_qk, 2), (s_qk, 4), (s_qk, 6), (s_qk, 8),
                    (s_vp, 2), (s_vp, 4)]
        released += [(s_down, 1 + n) for n in range(4)]
        released += [(s_gu, 2 * n + 2) for n in range(2 * FF // IC)]
        released += [(s_down, 5 + n) for n in range(12)]
        released += [(s_rq, 2 * n + 2) for n in range(8)]
        released += [(s_rv, 2 * (n + 1)) for n in range(8)]
        released += [(s_g, 2 * n + 2) for n in range(8)]
        released += [(s_down, 17 + n) for n in range(8)]
        assert len(released) == C_MOE

        def size(q):
            return 2 * 512 if q in (C_DOWN + 5, C_DOWN + 11) else CW

        ORDER = []
        for f in range(MSTEPS):
            ORDER += [("gate", f), ("up", f)] + ([("down", f - 2)] if f >= 2 else [])
        ORDER += [("down", MSTEPS - 2), ("down", MSTEPS - 1)]
        PLACE = {key: c for c, key in enumerate(ORDER)}

        def through(c):
            kind, f = ORDER[c]
            return {"gate": (s_mm, 2 * f + 1, 2 * MSTEPS), "up": (s_mm, 2 * f + 2, 2 * MSTEPS),
                    "down": (s_dn, f + 1, MSTEPS)}[kind]

        @block.sync
        def _(sp):
            def load(q, dst, src):
                if q >= RING:
                    sp.wait_ge(s_lo, q - RING + 1)
                sp.dma_start(dst, src).then_inc(s_ring[q % RING], 16)

            def load_in(q, w, c0):
                load(q, as_in(chunk(q)), icols(w, c0))

            def load_down(d):
                q, w, kt, _ = DOWN[d]
                for half in range(2):
                    for k0, n in down_parts(kt):
                        load(q, chunk(q)[:, 0:n * 512].rearrange("p (k n) -> p k n", n=512),
                             w[0, k0 * P:(k0 + n) * P, half * 512:half * 512 + 512]
                             .rearrange("(k p) n -> p k n", p=P))
                        q += 1

            sp.dma_start(XI[:, 0:2, :], x_prompt.rearrange("o (a p) d -> p (o a) d", p=P)).then_inc(s_x, 16)
            sp.dma_start(XI[0:NS, 2, :], x_sample.rearrange("b o d -> (b o) d")).then_inc(s_x, 16)
            sp.dma_start(C[:], const).then_inc(s_const, 16)
            sp.dma_start(R[:], param).then_inc(s_const, 16)
            q = C_EVEN
            for c0 in (0, CH, IC, CH + IC, 2 * CH, 2 * CH + IC, 2 * CH + SBW, 2 * CH + SBW + IC,
                       2 * CH + 2 * SBW, 2 * CH + 2 * SBW + IC):
                load_in(q, w_in_even[0], c0)
                q += 1
            load_down(0)
            for f in range(FF // IC):
                load_in(C_FFN + 2 * f, w_gate[0], f * IC)
                load_in(C_FFN + 2 * f + 1, w_up[0], f * IC)
            load_down(1)
            for c in range(24):
                load_in(C_ODD + c, w_in_odd[0], c * IC)
            load_down(2)

            def load_expert(e, it):
                for c, (kind, f) in enumerate(ORDER):
                    if kind == "down":
                        src = m_down[0, bass.ds(e, 1), f * IC:(f + 1) * IC, :].rearrange("o (k p) n -> p (o k) n", p=P)
                    else:
                        w = m_gate if kind == "gate" else m_up
                        src = w[0, bass.ds(e, 1), :, f * IC:(f + 1) * IC].rearrange("o (k p) n -> p (o k) n", p=P)
                    q = C_MOE + c
                    if isinstance(it, int) and c < MRING:
                        n = slot_of(q)
                        if n < RING:
                            sp.wait_ge(s_lo, C_MOE - RING + (n - C_MOE) % RING + 1)
                        elif n == RING:
                            sp.wait_ge(s_yl, 2 * H)
                            for i in range(2):
                                sp.wait_ge(s_sto[i], 16 * H // 2)
                                sp.wait_ge(s_rpo[i], 16 * H // 2)
                    else:
                        sp.wait_ge(s_lo, it * MCH + (q - MRING + 1))
                    sp.dma_start(chunk(q).rearrange("p (k n) -> p k n", n=src.shape[2]), src)\
                        .then_inc(s_ring[slot_of(q)], 16)

            load_expert(0, 0)
            sp.wait_ge(s_items, 1)
            n_items = sp.value_load(EII[0:1, TI_N:TI_N + 1], min_val=E, max_val=MAXI)
            with sp.Fori(1, n_items) as it:
                e = sp.value_load(EII[0:1, bass.ds(it, 1)], min_val=0, max_val=E - 1)
                load_expert(e, it)
            sp.wait_ge(s_yo, 2 * NT)
            sp.dma_start(y_prompt.rearrange("o (a p) d -> p (o a) d", p=P), YO[:, 0:2, :]).then_inc(s_ydone, 16)
            sp.dma_start(y_sample.rearrange("b o d -> (b o) d"), YO[0:NS, 2, :]).then_inc(s_ydone, 16)
            sp.wait_ge(s_ydone, 32)
            sp.wait_ge(s_done, 16 * 7)
            for i in range(2):
                sp.wait_ge(s_sto[i], 16 * H // 2)

        @block.gpsimd
        def _(pool):
            pool.dma_start(PG[:], page_table.rearrange("(o b) g -> o (b g)", o=1)).then_inc(s_pt, 16)
            for b in range(2):
                pool.dma_start(CC[0:120, b, :], cache_conv[0, 4 * b:4 * b + 4].rearrange("b w c -> (b w) c"))\
                    .then_inc(s_cc, 16)
            nc.gpsimd.memset(U[:, :, 0:W - 1], 0.0).then_inc(s_zero, 1)
            pool.dma_start(conv_sample[0, :, 0:W - 2, :], cache_conv[0, :, 1:W - 1, :]).then_inc(s_done, 16)
            pool.wait_ge(s_pt, 16)


            def pages(b, cache):
                for g in range(PAGES):
                    i = b * PAGES + g
                    page = pool.value_load(PG[0:1, i:i + 1], min_val=0, max_val=cache.shape[1] - 1)
                    pool.dma_start(KV[:, i % NS, :], cache[0, bass.ds(page, 1)].rearrange("o p h d -> p (o h d)"))\
                        .then_inc(s_kv[b % 4], 16)

            for b in range(NS):
                if b >= 4:
                    pool.wait_ge(s_kq, b - 3)
                pages(b, cache_k)
            pool.wait_ge(s_uo, 1)
            pool.dma_start(conv_prompt[0, 0], UO[:]).then_inc(s_done, 16)
            pool.wait_ge(s_uo, 2)
            pool.dma_start(conv_sample[0, :, W - 2, :], US[:]).then_inc(s_done, 16)
            pool.wait_ge(s_vev, NT)
            pool.dma_start(v_prompt[0, 0].rearrange("(a p) h d -> p a (h d)", p=P), VT[:, 0:2, :])\
                .then_inc(s_done, 16)
            pool.dma_start(v_sample[0].rearrange("b o h d -> (b o) (h d)"), VT[0:NS, 2, :]).then_inc(s_done, 16)
            pool.wait_ge(s_kto, NT)
            pool.dma_start(k_prompt[0, 0].rearrange("(a p) h d -> p a (h d)", p=P), KO[:, 0:2, :])\
                .then_inc(s_done, 16)
            pool.dma_start(k_sample[0].rearrange("b o h d -> (b o) (h d)"), KO[0:NS, 2, :]).then_inc(s_done, 16)
            for b in range(NS):
                if b < 4:
                    pool.wait_ge(s_kq, b + 5)
                else:
                    pool.wait_ge(s_avs, b - 3)
                pages(b, cache_v)
            pool.wait_ge(s_done, 16 * 7)
            pool.wait_ge(s_hid, 1)
            pool.dma_start(DT[:], decay.rearrange("p (h n) -> p h n", n=2 * P)).then_inc(s_decay, 16)

            def state_in(h):
                pool.dma_start(ST[h % 2].rearrange("p (b e) -> p b e", e=EV),
                               state_ret[0, :, h].rearrange("b d e -> d b e")).then_inc(s_state[h % 2], 16)

            state_in(0)
            for h in range(H):
                pool.wait_ge(s_rpe, h + 1)
                pool.dma_start(ret_prompt[0, 0, h], RP[:, h % 2, :]).then_inc(s_rpo[h % 2], 16)
            pool.wait_ge(s_sce, H)
            state_in(1)
            for h in range(H):
                pool.wait_ge(s_new, 4 * (h + 1))
                pool.dma_start(ret_sample[0, :, h].rearrange("b d e -> d b e"),
                               ST[h % 2].rearrange("p (b e) -> p b e", e=EV)).then_inc(s_sto[h % 2], 16)
                if h + 2 < H:
                    pool.wait_ge(s_sto[h % 2], 16 * (h // 2 + 1))
                    pool.wait_ge(s_os, h + 1)
                    state_in(h + 2)
            for i in range(2):
                pool.wait_ge(s_rpo[i], 16 * H // 2)

        @block.tensor
        def _(pe):
            mm = nc.tensor.matmul
            turn = nc.tensor.transpose

            def arrived(q):
                pe.wait_ge(s_lo, q + 1)

            def mm3(out, lh, ll, rh, rl, start, stop):
                mm(out, lh, rh, start=start, stop=False)
                mm(out, lh, rl, start=False, stop=False)
                return mm(out, ll, rh, start=False, stop=stop)

            def parts(q):
                return WH[:, q % WRING, :], WL[:, q % WRING, :]

            def sumsq(r):
                for k in range(DK):
                    if k % 2 == 0:
                        pe.wait_ge(s_sq, 4 * r + k // 2 + 1)
                    last = mm(PB[4][:, 0:T], const_("mean_d"), SQ[:, k, :], start=(k == 0), stop=(k == DK - 1))
                last.then_inc(s_ms, 1)

            def project(q, j, out, done, first=None):
                wh, wl = (as_in(x) for x in parts(q))
                if j == 0:
                    arrived(q)
                cols = slice(j * P, (j + 1) * P)
                for k in range(DK):
                    if first is not None:
                        pe.wait_ge(s_hl, DK * first + k + 1)
                    last = mm3(out, wh[:, k, cols], wl[:, k, cols], HH[:, k, :], HL[:, k, :], k == 0, k == DK - 1)
                last.then_inc(done, 1)

            def down(d, sh, sl, ready):
                q, _, kt, _ = DOWN[d]
                for half in range(2):
                    for k0, n in down_parts(kt):
                        arrived(q)
                        wh, wl = (x[:, 0:n * 512].rearrange("p (k n) -> p k n", n=512) for x in parts(q))
                        for kk in range(n):
                            k = k0 + kk
                            if half == 0:
                                ready(k)
                            for j in range(4):
                                cols = slice(j * P, (j + 1) * P)
                                last = mm3(PB[4 * (1 - half) + j][:, 0:T], wh[:, kk, cols], wl[:, kk, cols],
                                           sh[:, k, :], sl[:, k, :], k == 0, k == kt - 1)
                        last.then_inc(s_down, 1)
                        q += 1

            pe.wait_ge(s_x, 32)
            pe.wait_ge(s_const, 32)
            for k in range(DK):
                if k >= 4:
                    pe.wait_ge(s_xt, k - 3)
                for t in range(NT):
                    last = turn(PB[k % 4][:, t * P:t * P + TOK[t]],
                                XI[0:TOK[t], t, k * P:(k + 1) * P], ident[0:TOK[t], 0:TOK[t]])
                last.then_inc(s_turn, 1)
            pe.wait_ge(s_cc, 32)
            for c in range(CT):
                for b in range(2):
                    last = turn(PB[4 + c][:, b * 120:b * 120 + 120], CC[0:120, b, c * P:(c + 1) * P],
                                ident[0:120, 0:120])
                last.then_inc(s_cct, 1)
            pe.wait_ge(s_win, 1)
            sumsq(0)

            for c in range(2):
                if c == 1:
                    pe.wait_ge(s_win, CT)
                for g in range(2):
                    for j in range(2):
                        project(C_EVEN + 2 * c + g, j, PB[4 * c + 2 * g + j][:, 0:T], s_ag,
                                first=0 if c == g == j == 0 else None)
            for n in range(2 * HP):
                pe.wait_ge(s_u, 2 * (n // 4) + n % 2 + 1)
                project(C_EVEN + 4 + n // 2, n % 2, PB[n][:, 0:T], s_qk)
            for n in range(HP):
                pe.wait_ge(s_qks, n + 1)
                project(C_EVEN + 8 + n // 2, n % 2, PB[n][:, 0:T], s_vp)
            pe.wait_ge(s_vfe, HP)
            for t in range(NT):
                for j in range(HP):
                    last = turn(PB[t][0:TOK[t], j * P:(j + 1) * P], FVE[:, j, t * P:t * P + TOK[t]], ident)
                last.then_inc(s_vt, 1)
            pe.wait_ge(s_qks, 2 * HP)
            for c in range(CT):
                last = turn(PB[4][0:W - 1, c * P:(c + 1) * P], U[:, c, SEQ:SEQ + W - 1], ident)
            last.then_inc(s_ut, 1)
            for c in range(CT):
                last = turn(PB[5][0:NS, c * P:(c + 1) * P], UF[:, c, :, W - 1], ident)
            last.then_inc(s_ut, 1)
            for n in range(2 * HP):
                pe.wait_ge(s_qks, 8 if n < 2 else n + 1)
                if n >= 2:
                    pe.wait_ge(s_qrt, n - 1)
                mm(PB[6 + n % 2][:, 0:T], const_("mean_hd"), SQ[:, n, :], start=True, stop=True).then_inc(s_qms, 1)
            pe.wait_ge(s_qn, HP)
            for j in range(HP):
                last = turn(PB[3][0:NS, j * P:(j + 1) * P], QN[:, j, SEQ:T], ident)
            last.then_inc(s_qs, 1)
            pe.wait_ge(s_qn, 2 * HP)
            for t in range(NT):
                pe.wait_ge(s_vev, t + 1)
                for j in range(HP):
                    last = turn(PB[t][0:TOK[t], j * P:(j + 1) * P], QN[:, HP + j, t * P:t * P + TOK[t]], ident)
                last.then_inc(s_ktm, 1)
            for h in range(H):
                if h < NT:
                    pe.wait_ge(s_kto, h + 1)
                elif h == NT:
                    pe.wait_ge(s_qse, 1)
                else:
                    pe.wait_ge(s_zev, h - 3)
                o = HD * (h % 2)
                q, k = QN[o:o + HD, h // 2, :], QN[o:o + HD, HP + h // 2, :]
                mm(PB[h % 4][:, 0:SEQ], k[:, 0:P], q[:, 0:SEQ], start=True, stop=True)
                mm(PB[h % 4][:, SEQ:ZW], k[:, P:SEQ], q[:, P:SEQ], start=True, stop=True).then_inc(s_z, 1)
            pe.wait_ge(s_uo, 2)
            pe.wait_ge(s_qrt, 2 * HP)
            pe.wait_ge(s_qse, 1)
            for b in range(NS):
                if b >= 4:
                    pe.wait_ge(s_kq, b - 3)
                mm(PB[4 + b % 4][:, 0:SBW], C[0:NS, b:b + 1].to_broadcast([NS, P]), QS[:], start=True, stop=True)\
                    .then_inc(s_qb, 1)
            for h in range(H + 1):
                if h < 4:
                    pe.wait_ge(s_zev, 4 + h + 1)
                else:
                    pe.wait_ge(s_la, h - 3)
                if h % 4 == 0:
                    pe.wait_ge(s_lk, min(h // 4 + 1, 2))
                if h < H:
                    lk = Z[:, h * ZW:(h + 1) * ZW]
                    mm(PB[h % 4][:, 0:ZW], const_("negtri"), lk, start=True, stop=False)
                    mm(PB[h % 4][:, P:SEQ], const_("negones"), lk[:, SEQ:ZW], start=False, stop=True)\
                        .then_inc(s_suf, 1)
                else:
                    lk = Z[:, ZP:ZP + ZS]
                    mm(PB[h % 4][:, 0:ZS], const_("negtri"), lk, start=True, stop=False)
                    mm(PB[h % 4][:, 0:ZS // 2], const_("negones"), lk[:, ZS // 2:ZS], start=False, stop=True)\
                        .then_inc(s_suf, 1)
            pe.wait_ge(s_la, H + 1)
            pe.wait_ge(s_conv, CT)
            for c in range(CT):
                last = mm(PB[1][:, 0:T], const_("mean_ch"), CA[:, c, :], start=(c == 0), stop=(c == CT - 1))
            last.then_inc(s_cm, 1)
            pe.wait_ge(s_cq, 1)
            for c in range(CT):
                last = mm(PB[2][:, 0:T], const_("mean_ch"), CQ[:, c, :], start=(c == 0), stop=(c == CT - 1))
            last.then_inc(s_cv, 1)
            pe.wait_ge(s_kq, NS)
            for h in range(H):
                if h % 4 == 0:
                    pe.wait_ge(s_a, h // 4 + 1)
                o = HD * (h % 2)
                out = PB[4 + h // 2][o:o + HD, :]
                a = A[:, h * ZW:(h + 1) * ZW]
                mm(out[:, 0:SEQ], VT[:, 0, h * HD:(h + 1) * HD], a[:, 0:SEQ], start=True, stop=False)
                mm(out[:, P:SEQ], VT[:, 1, h * HD:(h + 1) * HD], a[:, SEQ:ZW], start=False, stop=True)\
                    .then_inc(s_av, 1)
            for b in range(NS):
                pe.wait_ge(s_kv[b % 4], 32 * (3 + b // 4))
                for hp in range(HP):
                    for g in range(PAGES):
                        at = ZP + (g * NS + b) * H + 2 * hp
                        last = mm(PB[0][:, (hp * NS + b) * 2:(hp * NS + b) * 2 + 2],
                                  KV[:, (b * PAGES + g) % NS, hp * P:(hp + 1) * P], A[:, at:at + 2],
                                  start=(g == 0), stop=(g == PAGES - 1))
                last.then_inc(s_avs, 1)
            pe.wait_ge(s_mixa, HP + 2)
            down(0, HH, HL, lambda k: pe.wait_ge(s_ml, k + 1))

            sumsq(1)
            for c in range(FF // IC):
                if c >= 2:
                    pe.wait_ge(s_hid, 2 * (c - 1))
                for g in range(2):
                    for j in range(2):
                        project(C_FFN + 2 * c + g, j, PB[4 * (c % 2) + 2 * g + j][:, 0:T], s_gu,
                                first=1 if c == g == j == 0 else None)
            pe.wait_ge(s_hid, FT - 2)
            down(1, HDH, HDL, lambda k: pe.wait_ge(s_hdl, k + 1))

            sumsq(2)
            for n in range(2 * H):
                if n >= 4:
                    pe.wait_ge(s_rot, n - 3)
                project(C_ODD + n // 2, n % 2, PB[n % 4][:, 0:T], s_rq, first=2 if n == 0 else None)
            def turn_v(c):
                pe.wait_ge(s_rvf, 2 * c + 2)
                if c >= 2:
                    pe.wait_ge(s_rve, 2 * (c - 1))
                b = 4 + 2 * (c % 2)
                for t in range(NT):
                    for j in range(2):
                        out = PB[b + t // 2][0:TOK[t], (t % 2) * IC + j * P:(t % 2) * IC + (j + 1) * P]
                        last = turn(out, FV[:, 2 * (c % 2) + j, t * P:t * P + TOK[t]], ident)
                    if t >= 1:
                        last.then_inc(s_rvt, 1)

            for c in range(H):
                for j in range(2):
                    n = 2 * c + j
                    if n < 4:
                        pe.wait_ge(s_rot, 2 * H - 3 + n)
                    else:
                        pe.wait_ge(s_rvf, n - 3)
                    project(C_ODD + 8 + c, j, PB[n % 4][:, 0:T], s_rv)
                if c >= 1:
                    turn_v(c - 1)
            turn_v(H - 1)
            pe.wait_ge(s_rve, 2 * H)
            for h in range(H):
                last = turn(PB[4 + h // 4][0:NS, (h % 4) * P:(h % 4 + 1) * P], KT[:, h, SEQ:T], ident)
            last.then_inc(s_ks, 1)
            pe.wait_ge(s_kse, 2)

            def scores(h):
                if h >= 2:
                    pe.wait_ge(s_sce, h - 1)
                    pe.wait_ge(s_kde, h - 1)
                    pe.wait_ge(s_rpe, h - 1)
                mm(PB[h % 2][:, 0:SEQ], KT[:, h, 0:P], QT[:, h, 0:SEQ], start=True, stop=True)
                mm(PB[h % 2][:, SEQ:ZW], KT[:, h, P:SEQ], QT[:, h, P:SEQ], start=True, stop=True).then_inc(s_sc, 1)
                for m in range(2):
                    last = turn(PB[2 + h % 2][:, m * P:(m + 1) * P], KT[:, h, m * P:(m + 1) * P], ident)
                last.then_inc(s_kt, 1)

            scores(0)
            for h in range(H):
                if h + 1 < H:
                    scores(h + 1)
                pe.wait_ge(s_sce, h + 1)
                if h >= 2:
                    pe.wait_ge(s_oe, 2 * (h - 1))
                for j in range(2):
                    out = PB[4 + 2 * (h % 2) + j]
                    v = VR[:, :, h * EV + j * P:h * EV + (j + 1) * P]
                    mm(out[:, 0:SEQ], v[:, 0, :], SC[:, h % 2, 0:SEQ], start=True, stop=False)
                    mm(out[:, P:SEQ], v[:, 1, :], SC[:, h % 2, SEQ:ZW], start=False, stop=True).then_inc(s_o, 1)
                pe.wait_ge(s_kde, h + 1)
                for m in range(2):
                    last = mm(PB[2 + h % 2][:, EV:2 * EV], KD[:, h % 2, m * P:(m + 1) * P],
                              VR[:, m, h * EV:(h + 1) * EV], start=(m == 0), stop=(m == 1))
                last.then_inc(s_rp, 1)
            pe.wait_ge(s_oe, 2 * H)
            pe.wait_ge(s_rpe, H)

            def outer(h):
                pe.wait_ge(s_km, h + 1)
                for g in range(4):
                    if h >= 1:
                        pe.wait_ge(s_new, 4 * (h - 1) + g + 1)
                    for i in range(2):
                        b = 2 * g + i
                        last = mm(PB[4 + g][:, i * EV:(i + 1) * EV], KM[0:NS, b * P:(b + 1) * P],
                                  VR[0:NS, 2, h * EV:(h + 1) * EV], start=True, stop=True)
                    last.then_inc(s_out, 1)

            outer(0)
            for h in range(H):
                if h + 1 < H:
                    outer(h + 1)
                pe.wait_ge(s_new, 4 * (h + 1))
                if h >= 2:
                    pe.wait_ge(s_ose, h - 1)
                for j in range(2):
                    for b in range(NS):
                        last = mm(PB[h % 2][:, j * NS + b:j * NS + b + 1],
                                  ST[h % 2][:, b * EV + j * P:b * EV + (j + 1) * P],
                                  QT[:, h, SEQ + b:SEQ + b + 1], start=True, stop=True)
                last.then_inc(s_os, 1)

            def mean(h):
                pe.wait_ge(s_ose, H if h < 2 else h + 1)
                if h >= 2:
                    pe.wait_ge(s_od, h - 1)
                for j in range(2):
                    last = mm(PB[h % 2][:, 0:T], const_("mean_ev"), O[:, 2 * h + j, :], start=(j == 0), stop=(j == 1))
                last.then_inc(s_om, 1)

            mean(0)
            mean(1)
            for h in range(H):
                pe.wait_ge(s_oq, h + 1)
                if h >= 2:
                    pe.wait_ge(s_ort, h - 1)
                for j in range(2):
                    last = mm(PB[2 + h % 2][:, 0:T], const_("mean_ev"), OQ[:, h % 2, j, :],
                              start=(j == 0), stop=(j == 1))
                last.then_inc(s_ov, 1)
                if h + 2 < H:
                    mean(h + 2)
                for j in range(2):
                    n = 2 * h + j
                    if n < 4:
                        pe.wait_ge(s_new, 4 * H)
                    else:
                        pe.wait_ge(s_y, n - 3)
                    project(C_ODD + 16 + h, j, PB[4 + n % 4][:, 0:T], s_g)
            pe.wait_ge(s_y, 2 * H)
            down(2, YH, YL, lambda k: pe.wait_ge(s_yl, k + 1))

            sumsq(3)
            pe.wait_ge(s_ht, 4 * DK)
            router = param_("router").rearrange("p (k e) -> p k e", e=E)
            for t in range(NT):
                for k in range(DK):
                    last = mm(PB[0][0:TOK[t], t * E:(t + 1) * E], HT[:, k, t * P:t * P + TOK[t]], router[:, k, :],
                              start=(k == 0), stop=(k == DK - 1))
            last.then_inc(s_lg, 1)
            for i in range(2 * NT):
                t, half = i // 2, i % 2
                if i >= 4:
                    pe.wait_ge(s_hxl, i - 3)
                for k in range(4):
                    last = turn(PB[2 + i % 4][0:TOK[t], k * P:(k + 1) * P],
                                HT[:, 4 * half + k, t * P:t * P + TOK[t]], ident)
                last.then_inc(s_ht2, 1)
            pe.wait_ge(s_sel, 1)
            for t in range(NT):
                for u in range(t):
                    mm(PB[1][:, t * E:(t + 1) * E], const_("ones"), SE[:, u, :], start=(u == 0), stop=False)
                mm(PB[1][:, t * E:(t + 1) * E], const_("below"), SE[:, t, :], start=(t == 0), stop=True)
            for t in range(NT):
                last = mm(PB[1][:, NT * E:(NT + 1) * E], const_("ones"), SE[:, t, :], start=(t == 0), stop=(t == NT - 1))
            last.then_inc(s_rk, 1)
            pe.wait_ge(s_hxl, 2 * NT)
            pe.wait_ge(s_items, 1)
            n_items = pe.value_load(EII[0:1, TI_N:TI_N + 1], min_val=E, max_val=MAXI)

            def gather(it, part):
                if part == 0:
                    pe.wait_ge(s_oh, it + 1)
                for half in range(2):
                    for k in range(4):
                        at = (4 * half + k) * P
                        for t in range(NT):
                            last = mm(PB[2 * part + half][:, k * P:(k + 1) * P],
                                      (HXH, HXL)[part][0:TOK[t], t, at:at + P],
                                      OH[0:TOK[t], t, :], start=(t == 0), stop=(t == NT - 1))
                    last.then_inc(s_ga, 1)

            def scatter(it):
                pe.wait_ge(s_yee, it * 2 + 2)
                pe.wait_ge(s_ot, it + 1)
                pe.wait_ge(s_xe, it * 4 + 2)
                for k in range(DK):
                    if k >= 2:
                        pe.wait_ge(s_add, it * DK + k - 1)
                    mm(PB[k % 2][:, 0:T], YE[:, k * P:(k + 1) * P], OT[:, :], start=True, stop=True)\
                        .then_inc(s_sca, 1)

            gather(0, 0)
            gather(0, 1)
            with pe.Fori(0, n_items) as it:
                def hidden(f):
                    if f >= 2:
                        pe.wait_ge(s_ac, it * MSTEPS + f - 1)
                    for g, kind in enumerate(("gate", "up")):
                        q = C_MOE + PLACE[(kind, f)]
                        pe.wait_ge(s_lo, it * MCH + (q + 1))
                        wh, wl = (as_in(x) for x in parts(q))
                        for k in range(DK):
                            if f == 0 and g == 0 and k == 0:
                                pe.wait_ge(s_xe, it * 4 + 4)
                            last = mm3(PB[2 + f % 2][:, g * IC:(g + 1) * IC], XEH[:, k, :], XEL[:, k, :],
                                       wh[:, k, :], wl[:, k, :], k == 0, k == DK - 1)
                        last.then_inc(s_mm, 1)

                def turn_hidden(f):
                    pe.wait_ge(s_ac, it * MSTEPS + f + 1)
                    if f == 0:
                        pe.wait_ge(s_ot, it + 2)
                    if f >= 2:
                        pe.wait_ge(s_atl, it * MSTEPS + f - 1)
                    for j in range(2):
                        last = turn(PB[6 + f % 2][:, j * P:(j + 1) * P], AC[:, f % 2, j * P:(j + 1) * P], ident)
                    last.then_inc(s_at, 1)

                def project_down(f):
                    q = C_MOE + PLACE[("down", f)]
                    pe.wait_ge(s_lo, it * MCH + (q + 1))
                    pe.wait_ge(s_atl, it * MSTEPS + f + 1)
                    wh, wl = (x.rearrange("p (k n) -> p k n", n=D) for x in parts(q))
                    for j in range(2):
                        rows = slice(j * P, (j + 1) * P)
                        for half in range(2):
                            cols = slice(half * 512, (half + 1) * 512)
                            last = mm3(PB[4 + half][:, :], ATH[:, f % 2, rows], ATL[:, f % 2, rows],
                                       wh[:, j, cols], wl[:, j, cols], f == 0 and j == 0,
                                       f == MSTEPS - 1 and j == 1)
                    last.then_inc(s_dn, 1)

                for f in range(MSTEPS):
                    hidden(f)
                    if f == 0:
                        scatter(it)
                        for t in range(NT):
                            last = turn(PB[6][:, t * P:t * P + TOK[t]], OG[0:TOK[t], t, :], ident[0:TOK[t], 0:TOK[t]])
                        last.then_inc(s_oht, 1)
                    if f >= 1:
                        turn_hidden(f - 1)
                    if f >= 2:
                        project_down(f - 2)
                pe.wait_ge(s_add, it * DK + DK)
                gather(it + 1, 0)
                turn_hidden(MSTEPS - 1)
                gather(it + 1, 1)
                project_down(MSTEPS - 2)
                project_down(MSTEPS - 1)
            scatter(n_items)
            pe.wait_ge(s_add, n_items * DK + DK)
            for i in range(2 * NT):
                t, half = i // 2, i % 2
                for k in range(4):
                    last = turn(PB[i][0:TOK[t], k * P:(k + 1) * P], XT[:, 4 * half + k, t * P:t * P + TOK[t]], ident)
                last.then_inc(s_yt, 1)

        @block.scalar
        def _(act):
            func = nc.scalar.activation
            high = [0]

            def prepare(q):
                q = min(q, C_MOE - 1)
                for n in range(high[0], q + 1):
                    act.wait_ge(s_ring[slot_of(n)], 16 * uses_before(n))
                    if n >= WRING:
                        act.wait_ge(*released[n - WRING])
                    func(WH[:, n % WRING, 0:size(n)], chunk(n)[:, 0:size(n)], ACT.Copy).then_inc(s_hi, 1)
                high[0] = max(high[0], q + 1)

            def norm_act(r, q):
                for i in range(4):
                    act.wait_ge(s_xt, DK * r + 2 * i + 2)
                    if r and i == 0:
                        act.wait_ge(s_down, DOWN[r - 1][3] + 1)
                    func(SQ[:, 2 * i:2 * i + 2, :], XT[:, 2 * i:2 * i + 2, :], ACT.Square).then_inc(s_sq, 1)
                prepare(q)
                act.wait_ge(s_ms, r + 1)
                func(RS[:, 0, :], PB[4][:, 0:T], ACT.Sqrt, bias=eps).then_inc(s_rt, 1)
                if r < 3:
                    for k in range(DK):
                        act.wait_ge(s_ht, DK * r + k + 1)
                        func(HH[:, k, :], HT[:, k, :], ACT.Copy).then_inc(s_hh, 1)

            def down_act(d):
                q, _, kt, _ = DOWN[d]
                prepare(q + 2 * len(down_parts(kt)) + 1)

            act.wait_ge(s_const, 32)
            for c in range(CT):
                act.wait_ge(s_cct, c + 1)
                func(UF[:, c, :, 0:W - 1], PB[4 + c][:, 0:NS * (W - 1)].rearrange("p (b w) -> p b w", w=W - 1),
                     ACT.Copy).then_inc(s_win, 1)
            norm_act(0, 0)
            prepare(C_EVEN + 3)
            for c in range(CT):
                act.wait_ge(s_ag, 4 * (c // 2) + 2 + c % 2 + 1)
                func(SG[:, c, :], PB[4 * (c // 2) + 2 + c % 2][:, 0:T], ACT.Sigmoid).then_inc(s_sig, 1)
                if c == 1:
                    prepare(C_EVEN + 5)
            prepare(C_EVEN + 6)
            for n in range(2 * HP):
                act.wait_ge(s_qk, n + 1)
                func(QR[:, n, :], PB[n][:, 0:T], ACT.Copy)
                func(SQ[:, n, :], PB[n][:, 0:T], ACT.Square).then_inc(s_qks, 1)
                if n % 2:
                    prepare(C_EVEN + 7 + n // 2)
            for n in range(HP):
                act.wait_ge(s_vp, n + 1)
                func(FVE[:, n, :], PB[n][:, 0:T], ACT.Copy).then_inc(s_vfe, 1)
                if n % 2:
                    prepare(C_EVEN + 11 + n // 2)
            for t in range(NT):
                act.wait_ge(s_vt, t + 1)
                func(VT[0:TOK[t], t, :], PB[t][0:TOK[t], :], ACT.Copy).then_inc(s_vev, 1)
            act.wait_ge(s_ut, 1)
            func(UO[:], PB[4][0:W - 1, :], ACT.Copy).then_inc(s_uo, 1)
            act.wait_ge(s_ut, 2)
            func(US[:], PB[5][0:NS, :], ACT.Copy).then_inc(s_uo, 1)
            for n in range(2 * HP):
                act.wait_ge(s_qms, n + 1)
                if n >= 2:
                    act.wait_ge(s_qn, n - 1)
                func(RS[:, n % 2, :], PB[6 + n % 2][:, 0:T], ACT.Sqrt, bias=eps).then_inc(s_qrt, 1)
            act.wait_ge(s_qs, 1)
            func(QS[:], PB[3][0:NS, :], ACT.Copy).then_inc(s_qse, 1)
            for t in range(NT):
                act.wait_ge(s_ktm, t + 1)
                func(KO[0:TOK[t], t, :], PB[t][0:TOK[t], :], ACT.Copy).then_inc(s_kto, 1)
            bias = param_("bias")
            for h in range(H):
                act.wait_ge(s_z, h + 1)
                func(Z[:, h * ZW:(h + 1) * ZW], PB[h % 4][:, 0:ZW], ACT.Identity, bias=bias[:, h:h + 1],
                     scale=HD ** -0.5).then_inc(s_zev, 1)
            step = 0
            for g in range(2):
                part = slice(g * ZP // 2, ZP // 2 if g == 0 else ZP + ZS)
                act.wait_ge(s_zev, 4 * (g + 1))
                if g == 1:
                    act.wait_ge(s_zs, 1)
                for src, f, kw in ((Z, ACT.Abs, {}), (L, ACT.Exp, dict(scale=-1.0)), (L, ACT.Ln, dict(bias=1.0))):
                    if step % 3:
                        act.wait_ge(s_ach, step - step // 3)
                    n = part.stop - part.start
                    if step == 3:
                        act.wait_ge(s_lk, 1)
                    func(L[:, 0:n], src[:, part] if src is Z else L[:, 0:n], f, **kw).then_inc(s_ln if f == ACT.Ln else s_ach, 1)
                    step += 1
            for g in range(2):
                part = slice(g * ZP // 2, ZP // 2 if g == 0 else ZP + ZS)
                act.wait_ge(s_la, 4 if g == 0 else H + 1)
                func(A[:, part], A[:, part], ACT.Exp).then_inc(s_exp, 1)
            act.wait_ge(s_cd, 1)
            func(CQ[:], CD[:], ACT.Square).then_inc(s_cq, 1)
            act.wait_ge(s_cv, 1)
            func(RS[:, 0, :], PB[2][:, 0:T], ACT.Sqrt, bias=eps).then_inc(s_crt, 1)
            ln_b = param_("ln_b")
            for c in range(CT):
                act.wait_ge(s_cn, c + 1)
                func(MIX[:, c, :], CD[:, c, :], ACT.Silu, bias=ln_b[:, c:c + 1]).then_inc(s_mixc, 1)
            act.wait_ge(s_mixc, CT)
            for k in range(DK):
                if k == CT:
                    act.wait_ge(s_mixa, HP + 2)
                func(HH[:, k, :], MIX[:, k, :], ACT.Copy).then_inc(s_mh, 1)
            down_act(0)

            norm_act(1, C_FFN + 2)
            for c in range(FF // IC):
                for j in range(2):
                    i = 2 * c + j
                    act.wait_ge(s_gu, 4 * c + j + 1)
                    if i >= 2:
                        act.wait_ge(s_hid, i - 1)
                    func(GA[:, j, :], PB[4 * (c % 2) + j][:, 0:T], ACT.Silu).then_inc(s_silu, 1)
                prepare(C_FFN + 2 * c + 3)
                for j in range(2):
                    act.wait_ge(s_hid, 2 * c + j + 1)
                    func(HDH[:, 2 * c + j, :], HF[:, j, :], ACT.Copy).then_inc(s_hdh, 1)
                prepare(C_FFN + 2 * c + 4)
            down_act(1)

            norm_act(2, C_ODD + 2)
            for c in range(H):
                prepare(C_ODD + c + 3)
            act.wait_ge(s_done, 16 * 7)

            def copy_v(c):
                b = 4 + 2 * (c % 2)
                act.wait_ge(s_rvt, 2 * c + 1)
                func(VR[:, 0:2, c * IC:(c + 1) * IC], PB[b][:, :].rearrange("p (t n) -> p t n", n=IC), ACT.Copy)\
                    .then_inc(s_rve, 1)
                act.wait_ge(s_rvt, 2 * c + 2)
                func(VR[0:NS, 2, c * IC:(c + 1) * IC], PB[b + 1][0:NS, 0:IC], ACT.Copy).then_inc(s_rve, 1)

            for c in range(H):
                for j in range(2):
                    n = 2 * c + j
                    act.wait_ge(s_rv, n + 1)
                    func(FV[:, n % 4, :], PB[n % 4][:, 0:T], ACT.Copy).then_inc(s_rvf, 1)
                if c >= 1:
                    copy_v(c - 1)
                prepare(C_ODD + 8 + c + 3)
            copy_v(H - 1)
            act.wait_ge(s_ks, 1)
            for i in range(2):
                func(KS[:, i * 512:(i + 1) * 512], PB[4 + i][0:NS, :], ACT.Copy).then_inc(s_kse, 1)
            kdecay = const_("kdecay")
            for h in range(H):
                act.wait_ge(s_kt, h + 1)
                if h >= 2:
                    act.wait_ge(s_rp, h - 1)
                for m in range(2):
                    last = func(KD[:, h % 2, m * P:(m + 1) * P], PB[2 + h % 2][:, m * P:(m + 1) * P], ACT.Copy,
                                scale=kdecay[:, 2 * h + m:2 * h + m + 1])
                last.then_inc(s_kde, 1)
                for j in range(2):
                    act.wait_ge(s_o, 2 * h + j + 1)
                    func(O[:, 2 * h + j, 0:SEQ], PB[4 + 2 * (h % 2) + j][:, 0:SEQ], ACT.Copy).then_inc(s_oe, 1)
            for h in range(H):
                act.wait_ge(s_os, h + 1)
                func(O[:, 2 * h:2 * h + 2, SEQ:T], PB[h % 2][:, 0:2 * NS].rearrange("p (j b) -> p j b", b=NS),
                     ACT.Copy).then_inc(s_ose, 1)

            def squares(h):
                act.wait_ge(s_od, h + 1)
                if h >= 2:
                    act.wait_ge(s_ov, h - 1)
                func(OQ[:, h % 2], OD[:, h % 2], ACT.Square).then_inc(s_oq, 1)

            squares(0)
            for h in range(H):
                act.wait_ge(s_ov, h + 1)
                if h >= 2:
                    act.wait_ge(s_on, 2 * (h - 1))
                func(RS[:, h % 2, :], PB[2 + h % 2][:, 0:T], ACT.Sqrt, bias=eps).then_inc(s_ort, 1)
                if h + 1 < H:
                    squares(h + 1)
                for j in range(2):
                    n = 2 * h + j
                    act.wait_ge(s_g, n + 1)
                    if n >= 2:
                        act.wait_ge(s_y, n - 1)
                    func(R2[:, n % 2, :], PB[4 + n % 4][:, 0:T], ACT.Silu).then_inc(s_gs, 1)
                prepare(C_ODD + 16 + h + 3)
                for j in range(2):
                    n = 2 * h + j
                    act.wait_ge(s_y, n + 1)
                    func(YH[:, n, :], O[:, n, :], ACT.Copy).then_inc(s_yh, 1)
            down_act(2)

            def high_moe(it, c):
                q = C_MOE + c
                n = slot_of(q)
                act.wait_ge(s_ring[n], it * (16 * MCH // MRING) + 16 * uses_before(q))
                if c >= WRING:
                    signal, count, per_item = through(c - WRING)
                    act.wait_ge(signal, it * per_item + count)
                elif isinstance(it, int):
                    act.wait_ge(*released[q - WRING])
                else:
                    signal, count, per_item = through(MCH + c - WRING)
                    act.wait_ge(signal, it * per_item + (count - per_item))
                func(WH[:, q % WRING, :], chunk(q), ACT.Copy).then_inc(s_hi, 1)

            norm_act(3, C_MOE - 1)
            for i in range(2 * NT):
                t, half = i // 2, i % 2
                act.wait_ge(s_ht2, i + 1)
                func(HXH[0:TOK[t], t, half * 512:(half + 1) * 512], PB[2 + i % 4][0:TOK[t], :], ACT.Copy)\
                    .then_inc(s_hx, 1)
            act.wait_ge(s_lgx, 1)
            func(GE[:, :, 0], MX[:, :, 2], ACT.Exp).then_inc(s_e2, 1)
            act.wait_ge(s_items, 1)
            n_items = act.value_load(EII[0:1, TI_N:TI_N + 1], min_val=E, max_val=MAXI)
            for c in range(WRING):
                high_moe(0, c)

            def copy_gathered(it, part):
                for i in range(2):
                    act.wait_ge(s_ga, it * 4 + 2 * part + i + 1)
                    func((XEH, XEL)[part][:, 4 * i:4 * i + 4, :],
                         PB[2 * part + i][:, :].rearrange("p (k n) -> p k n", n=P), ACT.Copy).then_inc(s_xe, 1)

            copy_gathered(0, 0)
            copy_gathered(0, 1)
            with act.Fori(0, n_items) as it:
                def turned(f):
                    act.wait_ge(s_at, it * MSTEPS + f + 1)
                    if f >= 2:
                        act.wait_ge(s_dn, it * MSTEPS + f - 1)
                    func(ATH[:, f % 2, :], PB[6 + f % 2][:, 0:2 * P], ACT.Copy).then_inc(s_ate, 1)

                done = WRING
                for f in range(MSTEPS):
                    for kind in ("gate", "up"):
                        n = min(PLACE[(kind, f)] + WRING, MCH - 1)
                        for c in range(done, n + 1):
                            high_moe(it, c)
                        done = max(done, n + 1)
                    act.wait_ge(s_mm, it * (2 * MSTEPS) + 2 * f + 2)
                    if f >= 2:
                        act.wait_ge(s_ac, it * MSTEPS + f - 1)
                    func(SI[:, f % 2, :], PB[2 + f % 2][:, 0:IC], ACT.Silu).then_inc(s_si, 1)
                    if f >= 1:
                        turned(f - 1)
                    if f >= 2:
                        n = min(PLACE[("down", f - 2)] + WRING, MCH - 1)
                        for c in range(done, n + 1):
                            high_moe(it, c)
                        done = max(done, n + 1)
                assert done == MCH
                copy_gathered(it + 1, 0)
                turned(MSTEPS - 1)
                copy_gathered(it + 1, 1)
                with act.If(it < n_items - 1):
                    for c in range(WRING):
                        high_moe(it + 1, c)
                act.wait_ge(s_dn, (it + 1) * MSTEPS)
                act.wait_ge(s_sca, it * DK + DK)
                for i in range(2):
                    func(YE[:, i * 512:(i + 1) * 512], PB[4 + i][:, :], ACT.Copy).then_inc(s_yee, 1)
            for i in range(2 * NT):
                t, half = i // 2, i % 2
                act.wait_ge(s_yt, i + 1)
                func(YO[0:TOK[t], t, half * 512:(half + 1) * 512], PB[i][0:TOK[t], :], ACT.Copy).then_inc(s_yo, 1)

        @block.vector
        def _(dve):
            V = nc.vector
            steps = [0]

            def link(ins):
                steps[0] += 1
                ins.then_inc(s_dch, 1)
                dve.wait_ge(s_dch, steps[0])

            low = [0]

            def prepare(q):
                q = min(q, C_MOE - 1)
                for n in range(low[0], q + 1):
                    dve.wait_ge(s_hi, n + 1)
                    V.tensor_tensor(WL[:, n % WRING, 0:size(n)], chunk(n)[:, 0:size(n)],
                                    full(WH[:, n % WRING, 0:size(n)]), ALU.subtract).then_inc(s_lo, 1)
                low[0] = max(low[0], q + 1)

            def norm_dve(r, gain, q):
                prepare(q)
                dve.wait_ge(s_rt, r + 1)
                link(V.reciprocal(RS[:, 1, :], RS[:, 0, :]))
                g = param_(gain)
                for k in range(DK):
                    V.scalar_tensor_tensor(out=HT[:, k, :], in0=XT[:, k, :], scalar=g[:, k:k + 1], in1=RS[:, 1, :],
                                           op0=ALU.mult, op1=ALU.mult).then_inc(s_ht, 1)
                if r < 3:
                    for k in range(DK):
                        dve.wait_ge(s_hh, DK * r + k + 1)
                        V.tensor_tensor(HL[:, k, :], HT[:, k, :], full(HH[:, k, :]), ALU.subtract).then_inc(s_hl, 1)

            def add_down(d):
                q, _, kt, before = DOWN[d]
                n = len(down_parts(kt))
                for half in range(2):
                    prepare(q + n * (half + 1) + (1 if half else 2))
                    dve.wait_ge(s_down, before + n * (half + 1))
                    for j in range(4):
                        x = XT[:, 4 * half + j, :]
                        V.tensor_tensor(x, x, PB[4 * (1 - half) + j][:, 0:T], ALU.add).then_inc(s_xt, 1)

            for k in range(DK):
                dve.wait_ge(s_turn, k + 1)
                V.tensor_copy(XT[:, k, :], PB[k % 4][:, 0:T]).then_inc(s_xt, 1)
            norm_dve(0, "g0", 0)
            prepare(C_EVEN + 3)
            dve.wait_ge(s_win, CT)
            for c in range(CT):
                dve.wait_ge(s_sig, c + 1)
                bank = PB[4 * (c // 2) + c % 2]
                V.tensor_tensor(U[:, c, W - 1:W - 1 + SEQ], bank[:, 0:SEQ], SG[:, c, 0:SEQ], ALU.mult)
                V.tensor_tensor(UF[:, c, :, W - 1], bank[:, SEQ:T], SG[:, c, SEQ:T], ALU.mult).then_inc(s_u, 1)
                if c == 1:
                    prepare(C_EVEN + 5)
            prepare(C_EVEN + 6)
            dve.wait_ge(s_u, CT)
            dve.wait_ge(s_zero, 1)
            cw = param_("conv_w").rearrange("p (c w) -> p c w", w=W)
            cb = param_("conv_b")
            taps = steps[0]
            for w in range(W):
                for c in range(CT):
                    u = U[:, c, w:w + SEQ]
                    if w == 0:
                        V.tensor_scalar(CA[:, c, 0:SEQ], u, cw[:, c, w:w + 1], cb[:, c:c + 1], ALU.mult, ALU.add)\
                            .then_inc(s_dch, 1)
                    else:
                        dve.wait_ge(s_dch, taps + CT * (w - 1) + c + 1)
                        V.scalar_tensor_tensor(out=CA[:, c, 0:SEQ], in0=u, scalar=cw[:, c, w:w + 1],
                                               in1=CA[:, c, 0:SEQ], op0=ALU.mult, op1=ALU.add).then_inc(s_dch, 1)
                if w % 3 == 2:
                    prepare(min(C_EVEN + 12, C_EVEN + 7 + w // 3))
            for c in range(CT):
                V.tensor_tensor(SW[:, c], UF[:, c], cw[:, c:c + 1, :].to_broadcast([P, NS, W]), ALU.mult)\
                    .then_inc(s_dch, 1)
            steps[0] = taps + CT * (W + 1)
            dve.wait_ge(s_dch, steps[0])
            link(V.tensor_reduce(CA[:, :, SEQ:T], SW[:], AX.X, ALU.add))
            for c in range(CT):
                V.tensor_scalar(CA[:, c, SEQ:T], CA[:, c, SEQ:T], cb[:, c:c + 1], None, ALU.add).then_inc(s_conv, 1)
            for n in range(2 * HP):
                dve.wait_ge(s_qrt, n + 1)
                link(V.reciprocal(RS[:, n % 2, :], RS[:, n % 2, :]))
                V.scalar_tensor_tensor(out=QN[:, n, :], in0=QR[:, n, :], scalar=param_("q_g" if n < HP else "k_g"),
                                       in1=RS[:, n % 2, :], op0=ALU.mult, op1=ALU.mult).then_inc(s_qn, 1)
            zs = Z[:, ZP:ZP + ZS].rearrange("p (g b h) -> p g b h", b=NS, h=H)
            for b in range(NS):
                dve.wait_ge(s_kv[b % 4], 32 * (1 + b // 4))
                dve.wait_ge(s_qb, b + 1)
                slot = b * PAGES % NS
                V.tensor_tensor(KQ[:], KV[:, slot:slot + PAGES, :],
                                PB[4 + b % 4][:, 0:SBW].rearrange("p (o n) -> p o n", o=1)
                                .to_broadcast([P, PAGES, SBW]), ALU.mult).then_inc(s_kq, 1)
                dve.wait_ge(s_kq, b + 1)
                link(V.tensor_reduce(zs[:, :, b, :], KQ[:].rearrange("p g (h d) -> p g h d", d=HD), AX.X, ALU.add))
            V.scalar_tensor_tensor(out=Z[:, ZP:ZP + ZS].rearrange("p (g h) -> p g h", h=H),
                                   in0=Z[:, ZP:ZP + ZS].rearrange("p (g h) -> p g h", h=H), scalar=HD ** -0.5,
                                   in1=param_("bias").rearrange("p (o h) -> p o h", o=1)
                                   .to_broadcast([P, PAGES * NS, H]), op0=ALU.mult, op1=ALU.add).then_inc(s_zs, 1)
            below = const_("below").rearrange("p (a b n) -> p a b n", a=1, b=1)

            def mask(buf, g, done):
                v = buf[:, g * ZP // 2:(g + 1) * ZP // 2].rearrange("p (h c n) -> p h c n", h=4, c=3)[:, :, 0:3:2, :]
                V.tensor_tensor(v, v, below.to_broadcast([P, 4, 2, P]), ALU.mult).then_inc(done, 1)

            for g in range(2):
                part = slice(g * ZP // 2, ZP // 2 if g == 0 else ZP + ZS)
                dve.wait_ge(s_ln, g + 1)
                link(V.scalar_tensor_tensor(out=A[:, part], in0=Z[:, part], scalar=0.0, in1=L[:, 0:part.stop - part.start],
                                            op0=ALU.min, op1=ALU.subtract))
                link(V.scalar_tensor_tensor(out=Z[:, part], in0=Z[:, part], scalar=0.0, in1=L[:, 0:part.stop - part.start],
                                            op0=ALU.max, op1=ALU.add))
                mask(Z, g, s_lk)
            for h in range(H + 1):
                dve.wait_ge(s_suf, h + 1)
                n = ZW if h < H else ZS
                a = A[:, h * ZW:h * ZW + n]
                V.tensor_tensor(a, a, PB[h % 4][:, 0:n], ALU.add).then_inc(s_la, 1)
            for g in range(2):
                dve.wait_ge(s_exp, g + 1)
                mask(A, g, s_a)
            dve.wait_ge(s_cm, 1)
            V.tensor_tensor(CD[:], CA[:], PB[1][:, 0:T].rearrange("p (o n) -> p o n", o=1).to_broadcast([P, CT, T]),
                            ALU.subtract).then_inc(s_cd, 1)
            dve.wait_ge(s_cd, 1)
            dve.wait_ge(s_crt, 1)
            link(V.reciprocal(RS[:, 0, :], RS[:, 0, :]))
            for c in range(CT):
                V.scalar_tensor_tensor(out=CD[:, c, :], in0=CD[:, c, :], scalar=param_("ln_g")[:, c:c + 1],
                                       in1=RS[:, 0, :], op0=ALU.mult, op1=ALU.mult).then_inc(s_cn, 1)
            for hp in range(HP):
                dve.wait_ge(s_av, 2 * hp + 2)
                V.tensor_copy(MIX[:, CT + hp, 0:SEQ], PB[4 + hp][:, 0:SEQ]).then_inc(s_mixa, 1)
            dve.wait_ge(s_avs, NS)
            avs = PB[0][:, 0:HP * NS * 2].rearrange("p (a b i) -> p a b i", b=NS, i=2)
            for i in range(2):
                V.tensor_copy(MIX[i * HD:(i + 1) * HD, CT:CT + HP, SEQ:T], avs[i * HD:(i + 1) * HD, :, :, i])\
                    .then_inc(s_mixa, 1)
            dve.wait_ge(s_mixa, HP + 2)
            for k in range(DK):
                dve.wait_ge(s_mh, k + 1)
                V.tensor_tensor(HL[:, k, :], MIX[:, k, :], full(HH[:, k, :]), ALU.subtract).then_inc(s_ml, 1)
            add_down(0)

            norm_dve(1, "g1", C_FFN + 2)
            for c in range(FF // IC):
                prepare(C_FFN + 2 * c + 3)
                for j in range(2):
                    i = 2 * c + j
                    dve.wait_ge(s_gu, 4 * c + 2 + j + 1)
                    dve.wait_ge(s_silu, i + 1)
                    if c >= 1:
                        dve.wait_ge(s_hdl, i - 1)
                    V.tensor_tensor(HF[:, j, :], GA[:, j, :], PB[4 * (c % 2) + 2 + j][:, 0:T], ALU.mult)\
                        .then_inc(s_hid, 1)
                prepare(C_FFN + 2 * c + 4)
                for j in range(2):
                    i = 2 * c + j
                    dve.wait_ge(s_hdh, i + 1)
                    V.tensor_tensor(HDL[:, i, :], HF[:, j, :], full(HDH[:, i, :]), ALU.subtract).then_inc(s_hdl, 1)
            add_down(1)

            norm_dve(2, "g2", C_ODD + 2)
            dve.wait_ge(s_done, 16 * 7)
            cos, sin = (const_(x).rearrange("p (a n) -> p a n", a=2) for x in ("cos", "sin"))
            for n in range(2 * H):
                g, h = n // H, n % H
                dve.wait_ge(s_rq, n + 1)
                bank = PB[n % 4]
                if n >= 2:
                    dve.wait_ge(s_rot, n - 1)
                V.tensor_tensor(R1[:, n % 2, :], bank[:, 0:T], cos[:, g, :], ALU.mult)
                V.tensor_tensor(R2[0:HD, n % 2, :], bank[HD:P, 0:T], sin[HD:P, g, :], ALU.mult)
                link(V.tensor_tensor(R2[HD:P, n % 2, :], bank[0:HD, 0:T], sin[0:HD, g, :], ALU.mult))
                V.tensor_tensor((QT, KT)[g][:, h, :], R1[:, n % 2, :], R2[:, n % 2, :], ALU.add).then_inc(s_rot, 1)
                if n % 2:
                    prepare(C_ODD + 3 + n // 2)
            prepare(C_ODD + 8 + H + 2)
            dve.wait_ge(s_decay, 16)
            for h in range(H):
                dve.wait_ge(s_sc, h + 1)
                if h >= 2:
                    dve.wait_ge(s_o, 2 * (h - 1))
                V.tensor_tensor(SC[:, h % 2, 0:SEQ], PB[h % 2][:, 0:SEQ], DT[:, h, :], ALU.mult)
                V.tensor_tensor(SC[:, h % 2, SEQ:ZW], PB[h % 2][:, SEQ:ZW], DT[:, h, 0:P], ALU.mult)\
                    .then_inc(s_sce, 1)
                dve.wait_ge(s_rp, h + 1)
                if h >= 2:
                    dve.wait_ge(s_rpo[h % 2], 16 * (h // 2))
                V.tensor_copy(RP[:, h % 2, :], PB[2 + h % 2][:, EV:2 * EV]).then_inc(s_rpe, 1)

            def spread_k(h):
                if h >= 1:
                    dve.wait_ge(s_out, 4 * h)
                V.tensor_tensor(KM[0:NS, :].rearrange("p (b n) -> p b n", n=P),
                                KS[:, h * P:(h + 1) * P].rearrange("p (o n) -> p o n", o=1)
                                .to_broadcast([NS, NS, P]),
                                C[32:32 + NS, 32:32 + NS].rearrange("p (b o) -> p b o", o=1).to_broadcast([NS, NS, P]),
                                ALU.mult).then_inc(s_km, 1)

            dve.wait_ge(s_kse, 2)
            spread_k(0)
            for h in range(H):
                dve.wait_ge(s_state[h % 2], 16 * (h // 2 + 1))
                for g in range(4):
                    dve.wait_ge(s_out, 4 * h + g + 1)
                    s = ST[h % 2][:, g * 512:(g + 1) * 512]
                    V.scalar_tensor_tensor(out=s, in0=s, scalar=GAMMA[h], in1=PB[4 + g][:, :], op0=ALU.mult,
                                           op1=ALU.add).then_inc(s_new, 1)
                if h + 1 < H:
                    spread_k(h + 1)

            def centre(h):
                dve.wait_ge(s_om, h + 1)
                dve.wait_ge(s_ose, h + 1)
                if h >= 2:
                    dve.wait_ge(s_on, 2 * (h - 1))
                V.tensor_tensor(OD[:, h % 2], O[:, 2 * h:2 * h + 2, :],
                                PB[h % 2][:, 0:T].rearrange("p (o n) -> p o n", o=1).to_broadcast([P, 2, T]),
                                ALU.subtract).then_inc(s_od, 1)

            centre(0)
            for h in range(H):
                dve.wait_ge(s_od, h + 1)
                dve.wait_ge(s_ort, h + 1)
                link(V.reciprocal(RS[:, h % 2, :], RS[:, h % 2, :]))
                for j in range(2):
                    n = 2 * h + j
                    V.scalar_tensor_tensor(out=O[:, n, :], in0=OD[:, h % 2, j, :],
                                           scalar=param_("gn_g")[:, n:n + 1], in1=RS[:, h % 2, :],
                                           op0=ALU.mult, op1=ALU.mult).then_inc(s_on, 1)
                if h + 1 < H:
                    centre(h + 1)
                for j in range(2):
                    n = 2 * h + j
                    dve.wait_ge(s_on, n + 1)
                    dve.wait_ge(s_gs, n + 1)
                    V.scalar_tensor_tensor(out=O[:, n, :], in0=O[:, n, :], scalar=param_("gn_b")[:, n:n + 1],
                                           in1=R2[:, n % 2, :], op0=ALU.add, op1=ALU.mult).then_inc(s_y, 1)
                prepare(C_ODD + 16 + h + 3)
                for j in range(2):
                    n = 2 * h + j
                    dve.wait_ge(s_yh, n + 1)
                    V.tensor_tensor(YL[:, n, :], O[:, n, :], full(YH[:, n, :]), ALU.subtract).then_inc(s_yl, 1)
            add_down(2)

            norm_dve(3, "g3", C_MOE - 1)
            for i in range(2 * NT):
                t, half = i // 2, i % 2
                cols = slice(half * 512, (half + 1) * 512)
                dve.wait_ge(s_hx, i + 1)
                V.tensor_tensor(HXL[0:TOK[t], t, cols], PB[2 + i % 4][0:TOK[t], :], full(HXH[0:TOK[t], t, cols]),
                                ALU.subtract).then_inc(s_hxl, 1)
            dve.wait_ge(s_down, NDOWN)
            link(V.memset(LG[:], 0.0))
            dve.wait_ge(s_lg, 1)
            for t in range(NT):
                link(V.tensor_copy(LG[0:TOK[t], t, :], PB[0][0:TOK[t], t * E:(t + 1) * E]))
            for t in range(NT):
                link(V.max(MX[:, t, :], LG[:, t, :]))
                link(V.max_index(MI[:, t, :], MX[:, t, :], LG[:, t, :]))
            link(V.tensor_copy(MIF[:], MI[:]))
            V.tensor_tensor(MX[:, :, 2], MX[:, :, 1], MX[:, :, 0], ALU.subtract).then_inc(s_lgx, 1)
            dve.wait_ge(s_lgx, 1)
            io8 = const_("iota8").rearrange("p (o e) -> p o e", o=1).to_broadcast([P, NT, E])
            link(V.tensor_tensor(S1[:], io8, MIF[:, :, 0:1].to_broadcast([P, NT, E]), ALU.is_equal))
            link(V.tensor_tensor(SE[:], io8, MIF[:, :, 1:2].to_broadcast([P, NT, E]), ALU.is_equal))
            dve.wait_ge(s_e2, 1)
            link(V.tensor_scalar(GE[:, :, 1], GE[:, :, 0], 1.0, None, ALU.add))
            link(V.reciprocal(GE[:, :, 2], GE[:, :, 1]))
            link(V.tensor_tensor(GE[:, :, 3], GE[:, :, 2], GE[:, :, 0], ALU.mult))
            GT = M1[:, 0:NT, :]
            G2 = M2[:, 0:NT, :]
            link(V.tensor_tensor(GT, S1[:], GE[:, :, 2:3].to_broadcast([P, NT, E]), ALU.mult))
            link(V.tensor_tensor(G2, SE[:], GE[:, :, 3:4].to_broadcast([P, NT, E]), ALU.mult))
            link(V.tensor_tensor(RK[:], GT, G2, ALU.add))
            link(V.tensor_tensor(SE[:], SE[:], S1[:], ALU.add))
            link(V.tensor_tensor(SE[:, 2, :], SE[:, 2, :], C[:, CONST["rows"][0]:CONST["rows"][0] + 1]
                                 .to_broadcast([P, E]), ALU.mult))
            link(V.tensor_copy(LG[:], RK[:]))
            V.tensor_copy(S1[:], SE[:]).then_inc(s_sel, 1)
            dve.wait_ge(s_sel, 1)
            dve.wait_ge(s_rk, 1)
            rank = PB[1][:, 0:NT * E].rearrange("p (t e) -> p t e", e=E)
            count = PB[1][:, NT * E:(NT + 1) * E]
            link(V.scalar_tensor_tensor(out=RK[:], in0=rank, scalar=1000.0, in1=SE[:], op0=ALU.add, op1=ALU.mult))
            link(V.tensor_scalar(RK[:], RK[:], -1000.0, None, ALU.add))
            link(V.tensor_scalar(TI[:, 0, :], count, 128.5, None, ALU.is_gt))
            link(V.tensor_scalar(TI[:, 1, :], count, 256.5, None, ALU.is_gt))
            link(V.scalar_tensor_tensor(out=TI[:, 2, :], in0=TI[:, 0, :], scalar=1.0, in1=TI[:, 1, :],
                                        op0=ALU.add, op1=ALU.add))
            link(V.tensor_tensor(LT[:], const_("lt8").rearrange("p (a b) -> p a b", b=E),
                                 TI[:, 2:3, :].to_broadcast([P, E, E]), ALU.mult))
            link(V.tensor_reduce(TI[:, 3, :], LT[:], AX.X, ALU.add))
            link(V.tensor_tensor(TI[:, 4, :], TI[:, 3, :], TI[:, 2, :], ALU.add))
            item = const_("item").rearrange("p (i e) -> p i e", e=E)
            link(V.tensor_tensor(M1[:], item, TI[:, 3:4, :].to_broadcast([P, TI_N, E]), ALU.is_ge))
            link(V.tensor_tensor(M2[:], item, TI[:, 4:5, :].to_broadcast([P, TI_N, E]), ALU.is_lt))
            link(V.tensor_tensor(M1[:], M1[:], M2[:], ALU.mult))
            link(V.tensor_tensor(M2[:], item, TI[:, 3:4, :].to_broadcast([P, TI_N, E]), ALU.subtract))
            link(V.tensor_tensor(M2[:], M2[:], M1[:], ALU.mult))
            link(V.tensor_reduce(BA[:, :], M2[:], AX.X, ALU.add))
            link(V.tensor_tensor(M3[:], const_("expert").rearrange("p (i e) -> p i e", e=E), M1[:], ALU.mult))
            link(V.tensor_reduce(EI[:, 0:TI_N], M3[:], AX.X, ALU.add))
            link(V.tensor_reduce(EI[:, TI_N:TI_N + 1], TI[:, 2, :], AX.X, ALU.add))
            for src, dst in ((RK, CR), (LG, CG)):
                for t in range(NT):
                    m = M4[:, t, :].rearrange("p (i e) -> p i e", e=E)
                    link(V.tensor_tensor(m, M1[:], src[:, t:t + 1, :].to_broadcast([P, TI_N, E]), ALU.mult))
                    link(V.tensor_reduce(dst[:, :, t], m, AX.X, ALU.add))
            for t in range(NT):
                link(V.scalar_tensor_tensor(out=CR[:, :, t], in0=BA[:, :], scalar=-128.0, in1=CR[:, :, t],
                                            op0=ALU.mult, op1=ALU.add))
            V.tensor_copy(EII[:], EI[:, :]).then_inc(s_items, 1)
            dve.wait_ge(s_items, 1)
            n_items = dve.value_load(EII[0:1, TI_N:TI_N + 1], min_val=E, max_val=MAXI)
            slot = const_("slot")

            def low_moe(it, c):
                q = C_MOE + c
                dve.wait_ge(s_hi, it * MCH + (q + 1))
                V.tensor_tensor(WL[:, q % WRING, :], chunk(q), full(WH[:, q % WRING, :]), ALU.subtract)\
                    .then_inc(s_lo, 1)

            for c in range(WRING):
                low_moe(0, c)
            base = steps[0]
            V.memset(YE[:, 0:512], 0.0).then_inc(s_yee, 1)
            V.memset(YE[:, 512:D], 0.0).then_inc(s_yee, 1)
            V.memset(OT[:, :], 0.0).then_inc(s_ot, 1)

            def one_hot(it):
                if not isinstance(it, int):
                    dve.wait_ge(s_oh, it)
                V.tensor_copy(CU[:, 0:1, :], CR[:, bass.ds(it, 1), :]).then_inc(s_dch, 1)
                V.tensor_copy(CU[:, 1:2, :], CG[:, bass.ds(it, 1), :]).then_inc(s_dch, 1)
                dve.wait_ge(s_dch, it * 2 + (base + 2))
                for t in range(NT):
                    V.tensor_scalar(OH[:, t, :], slot, CU[:, 0, t:t + 1], None, ALU.is_equal)
                    last = V.tensor_scalar(OG[:, t, :], slot, CU[:, 0, t:t + 1], CU[:, 1, t:t + 1], ALU.is_equal,
                                           ALU.mult)
                last.then_inc(s_oh, 1)

            one_hot(0)
            with dve.Fori(0, n_items) as it:
                def turned(f):
                    dve.wait_ge(s_ate, it * MSTEPS + f + 1)
                    V.tensor_tensor(ATL[:, f % 2, :], PB[6 + f % 2][:, 0:2 * P], full(ATH[:, f % 2, :]),
                                    ALU.subtract).then_inc(s_atl, 1)

                done = WRING
                for f in range(MSTEPS):
                    for kind in ("gate", "up"):
                        n = min(PLACE[(kind, f)] + WRING, MCH - 1)
                        for c in range(done, n + 1):
                            low_moe(it, c)
                        done = max(done, n + 1)
                    dve.wait_ge(s_si, it * MSTEPS + f + 1)
                    if f >= 2:
                        dve.wait_ge(s_at, it * MSTEPS + f - 1)
                    V.tensor_tensor(AC[:, f % 2, :], SI[:, f % 2, :], PB[2 + f % 2][:, IC:2 * IC], ALU.mult)\
                        .then_inc(s_ac, 1)
                    if f == 0:
                        for k in range(DK):
                            dve.wait_ge(s_sca, it * DK + k + 1)
                            V.tensor_tensor(XT[:, k, :], XT[:, k, :], PB[k % 2][:, 0:T], ALU.add).then_inc(s_add, 1)
                        dve.wait_ge(s_oht, it + 1)
                        V.tensor_copy(OT[:, :], PB[6][:, 0:T]).then_inc(s_ot, 1)
                    if f == 6:
                        one_hot(it + 1)
                    if f >= 1:
                        turned(f - 1)
                    if f >= 2:
                        n = min(PLACE[("down", f - 2)] + WRING, MCH - 1)
                        for c in range(done, n + 1):
                            low_moe(it, c)
                        done = max(done, n + 1)
                turned(MSTEPS - 1)
                with dve.If(it < n_items - 1):
                    for c in range(WRING):
                        low_moe(it + 1, c)
            for k in range(DK):
                dve.wait_ge(s_sca, n_items * DK + k + 1)
                V.tensor_tensor(XT[:, k, :], XT[:, k, :], PB[k % 2][:, 0:T], ALU.add).then_inc(s_add, 1)


def tables():
    C = np.zeros((P, NCONST), np.float32)
    p = np.arange(P)

    def put(name, a):
        at, n = CONST[name]
        C[:, at:at + n] = np.broadcast_to(np.asarray(a, np.float64), (P, n))

    put("ident", np.eye(P))
    put("negtri", -(p[:, None] > p[None, :]).astype(float))
    put("negones", -1.0)
    put("below", (p[:, None] < p[None, :]).astype(float))
    put("ones", 1.0)
    put("mean_d", 1.0 / D)
    put("mean_ch", 1.0 / CH)
    put("mean_hd", (p[:, None] // HD == p[None, :] // HD) / HD)
    put("mean_ev", 1.0 / EV)
    half = P // 2
    inv = np.float32(10000.0) ** (-np.linspace(0.0, 1.0, half, dtype=np.float32))
    pos = np.concatenate([np.arange(SEQ), np.full(NS, PAST)]).astype(np.float32)
    ang = (pos[None, :] * inv[:, None]).astype(np.float32)
    cos, sin = np.cos(ang), np.sin(ang)
    scale = np.float32(P) ** np.float32(-0.5)
    put("cos", np.concatenate([np.concatenate([cos, cos]), np.concatenate([cos, cos]) * scale], axis=1))
    put("sin", np.concatenate([np.concatenate([sin, -sin]), np.concatenate([sin, -sin]) * scale], axis=1))
    put("slot", p)
    gamma = np.array(GAMMA)
    put("kdecay", np.stack([gamma[h] ** (SEQ - 1 - (m * P + p)) for h in range(H) for m in range(2)], axis=1))
    e = np.arange(E)
    put("iota8", e)
    put("lt8", (e[None, :] < e[:, None]).astype(float).ravel())
    put("item", np.repeat(np.arange(TI_N), E))
    put("expert", np.tile(e, TI_N))
    put("eps", EPS)
    put("rows", (p < NS).astype(float)[:, None])
    key, query = np.meshgrid(np.arange(SEQ), np.arange(SEQ), indexing="ij")
    diff = query - key
    table = []
    for h in range(H):
        d = np.where(diff >= 0, gamma[h] ** np.maximum(diff, 0), 0.0)
        table.append(d[0:P])
    return C, np.concatenate(table, axis=1).astype(np.float32)


_OUTS = [(1, SEQ, D), (NS, 1, D), (1, 1, SEQ, H, HD), (1, 1, SEQ, H, HD), (1, NS, 1, H, HD), (1, NS, 1, H, HD),
         (1, 1, W - 1, CH), (1, NS, W - 1, CH), (1, 1, H, P, EV), (1, NS, H, P, EV)]
_INS = ["x_prompt", "x_sample", "cache_sb_k", "cache_sb_v", "cache_conv", "state_ret", "page_table"]
_WEIGHTS = ["w_in_even", "w_out_even", "ffn_w_gate", "ffn_w_up", "ffn_w_down", "w_in_odd", "w_out_odd",
            "moe_w_gate", "moe_w_up", "moe_w_down"]


def kernel(**inputs):
    import concourse.bacc as bacc
    from concourse.bass_utils import run_bass_kernel_spmd

    a = {k: np.asarray(v) for k, v in inputs.items()}
    const, decay = tables()

    def tiles(x):
        return x.reshape(-1, P).T

    param = np.concatenate([
        tiles(a["norm_mix_even"][0]), tiles(a["norm_ffn_even"][0]), tiles(a["norm_mix_odd"][0]),
        tiles(a["norm_ffn_odd"][0]), a["conv_w"][0].reshape(W, CT, P).transpose(2, 1, 0).reshape(P, CT * W),
        tiles(a["conv_b"][0]), tiles(a["conv_ln_g"][0]), tiles(a["conv_ln_b"][0]),
        np.tile(a["sb_q_norm"][0], 2)[:, None], np.tile(a["sb_k_norm"][0], 2)[:, None],
        np.broadcast_to(a["sb_bias"][0], (P, H)), tiles(a["ret_gn_g"][0]), tiles(a["ret_gn_b"][0]),
        a["router_w"][0].reshape(DK, P, E).transpose(1, 0, 2).reshape(P, DK * E)], axis=1)
    arrays = {n: a[n] for n in _INS}
    arrays.update(const=const, decay=decay, param=param)
    arrays.update({n: a[n] for n in _WEIGHTS})
    nc = bacc.Bacc("TRN2", target_bir_lowering=False, num_devices=1)
    feed, args = {}, []
    for name, x in arrays.items():
        x = np.ascontiguousarray(x)
        feed[f"in_{name}"] = x
        args.append(nc.dram_tensor(f"in_{name}", x.shape, mybir.dt.from_np(x.dtype), kind="ExternalInput").ap())
    names = ["y_prompt", "y_sample", "k_prompt", "v_prompt", "k_sample", "v_sample", "conv_prompt", "conv_sample",
             "ret_prompt", "ret_sample"]
    for name, shape in zip(names, _OUTS):
        args.append(nc.dram_tensor(f"out_{name}", shape, F32, kind="ExternalOutput").ap())
    build(nc, *args)
    r = run_bass_kernel_spmd(nc, [feed], core_ids=[0])
    return tuple(r.results[0][f"out_{name}"] for name in names)
```

```python
from contextlib import ExitStack

import concourse.bass as bass
from concourse import mybir
import numpy as np

F32 = mybir.dt.float32
F32R = mybir.dt.float32r
I32 = mybir.dt.int32
U32 = mybir.dt.uint32
ALU = mybir.AluOpType
ACT = mybir.ActivationFunctionType
AX = mybir.AxisListType

P = 128
D = 1024
DK = D // P
SEQ = 256
NS = 8
T = SEQ + NS
NT = 3
TOK = [P, P, NS]
CH = 512
CT = CH // P
W = 31
H = 8
HD = 64
SBW = H * HD
HP = SBW // P
PAST = 256
PAGES = PAST // P
FF = 2816
FT = FF // P
RV = 2048
EV = RV // H
E = 8
FE = 3584
EPS = 1e-6
ZW = 384
ZP = H * ZW
ZS = PAGES * NS * H
GAMMA = [1.0 - 2.0 ** (-5 - h) for h in range(H)]

RING = 3
MRING = 7
WRING = 3
CW = 2048
IC = CW // DK
MSTEPS = FE // IC
MCH = 3 * MSTEPS
CG_N = 8
CGT = -(-W // CG_N)
ARENA = 22800
MAXI = 12
TI_N = MAXI + 1
assert MCH % MRING == 0 and MCH % WRING == 0

CONST = {}
_at = 0
for _name, _n in [("ident", P), ("negtri", P), ("negones", P), ("below", P), ("ones", P), ("mean_d", P),
                  ("mean_ch", P), ("mean_hd", P), ("mean_ev", P), ("cos", 2 * T), ("sin", 2 * T),
                  ("slot", P), ("kdecay", 2 * H), ("iota8", E), ("lt8", E * E), ("item", TI_N * E),
                  ("expert", TI_N * E), ("eps", 1), ("rows", 1), ("sample", NS)]:
    CONST[_name] = (_at, _n)
    _at += _n
NCONST = _at
PARAM = {}
_at = 0
for _name, _n in [("g0", DK), ("g1", DK), ("g2", DK), ("g3", DK), ("conv_w", CT * W), ("conv_b", CT),
                  ("ln_g", CT), ("ln_b", CT), ("q_g", 1), ("k_g", 1), ("bias", H), ("gn_g", RV // P),
                  ("gn_b", RV // P), ("router", DK * E)]:
    PARAM[_name] = (_at, _n)
    _at += _n
NPARAM = _at

C_EVEN = 0
C_OUTE = C_EVEN + 10
C_FFN = C_OUTE + 4
C_DOWN = C_FFN + 2 * FF // IC
C_ODD = C_DOWN + 12
C_OUTO = C_ODD + 24
C_MOE = C_OUTO + 8


def build(nc, x_prompt, x_sample, cache_k, cache_v, cache_conv, state_ret, page_table, const, decay, param,
          w_in_even, w_out_even, w_gate, w_up, w_down, w_in_odd, w_out_odd, m_gate, m_up, m_down,
          y_prompt, y_sample, k_prompt, v_prompt, k_sample, v_sample, conv_prompt, conv_sample,
          ret_prompt, ret_sample):
    with ExitStack() as ctx:
        def sb(name, shape, dt=F32):
            return ctx.enter_context(nc.sbuf_tensor(name, shape, dt))

        def sem(name):
            return ctx.enter_context(nc.semaphore(name))

        ring = sb("ring", [P, RING, CW])
        WH = sb("WH", [P, WRING, CW], F32R)
        WL = sb("WL", [P, WRING, CW], F32R)
        XT = sb("XT", [P, DK, T])
        HH = sb("HH", [P, DK, T], F32R)
        HL = sb("HL", [P, DK, T], F32R)
        SQ = sb("SQ", [P, DK, T])
        HT = SQ
        RS = sb("RS", [P, 2, T])
        C = sb("C", [P, NCONST])
        R = sb("R", [P, NPARAM])
        PG = sb("PG", [1, NS * PAGES], I32)
        EII = sb("EII", [P, TI_N + 1], I32)
        MI = sb("MI", [P, NT, 8], U32)
        arena_at = -(-nc.sbuf_base // 32) * 32
        sb("arena", [P, ARENA])
        PB = [ctx.enter_context(nc.psum_tensor(f"bank{i}", [P, 512], F32)) for i in range(8)]

        used = {}

        def region(stage, name, *shape, dt=F32, at=None):
            n = int(np.prod(shape))
            if at is None:
                at = used.get(stage, 0)
                used[stage] = at + -(-n // 8) * 8
            assert at + n <= ARENA, (stage, name, at + n)
            return nc.alloc_sbuf_tensor_at(f"{stage}_{name}", [P, *shape], dt, offset=arena_at + 4 * at)

        def full(ap):
            return ap.bitcast(F32)

        def const_(name, parts=P):
            at, n = CONST[name]
            return C[0:parts, at:at + n]

        def param_(name):
            at, n = PARAM[name]
            return R[:, at:at + n]

        ident = const_("ident")
        eps = const_("eps")

        KV = region("even", "KV", NS, SBW)
        Z = region("even", "Z", ZP + ZS)
        L = region("even", "L", ZP // 2 + ZS)
        A = region("even", "A", ZP + ZS)
        QR = region("even", "QR", 2 * HP, T)
        QN = region("even", "QN", 2 * HP, T)
        VT = region("even", "VT", NT, SBW)
        U = region("even", "U", CT, W - 1 + SEQ)
        UF = region("even", "UF", CT, NS, W)
        CA = region("even", "CA", CT, T)
        KO = region("even", "KO", NT, SBW)
        XI = Z[:, 0:3072].rearrange("p (a b) -> p a b", b=D)
        CC = L[:, 0:1024].rearrange("p (a b) -> p a b", b=CH)
        FVE = L[:, 0:HP * T].rearrange("p (a b) -> p a b", b=T)
        SG = Z[:, 0:CT * T].rearrange("p (a b) -> p a b", b=T)
        SW = A[:, 0:CT * NS * W].rearrange("p (a b c) -> p a b c", b=NS, c=W)
        CD = QR[:, 0:CT, :]
        CQ = QR[:, CT:2 * CT, :]
        UO = KO[32:32 + W - 1, 2, :]
        US = KO[64:64 + NS, 2, :]
        QS = A[0:NS, 2080:2080 + SBW]
        KQ = A[:, 1056:1056 + 2 * SBW].rearrange("p (a b) -> p a b", b=SBW)
        MIX = SQ
        DG = [x[:, at + i * CG_N * P:at + (i + 1) * CG_N * P].rearrange("p (w n) -> p w n", n=P)
              for x, at in ((A, 1056), (QR[:, :, :].rearrange("p n t -> p (n t)"), 0)) for i in range(2)]
        flat = "p a b -> p (a b)"
        LATE = [x[:, :, :].rearrange(flat)[:, i * SBW:(i + 1) * SBW]
                for x, n in ((QN, 4), (U, 2), (CA, 2)) for i in range(n)]
        HDH = region("ffn", "HDH", FT, T, dt=F32R)
        HDL = region("ffn", "HDL", FT, T, dt=F32R)
        HF = region("ffn", "HF", 2, T)
        GA = region("ffn", "GA", 2, T)
        QT = region("odd", "QT", H, T)
        KT = region("odd", "KT", H, T)
        VR = region("odd", "VR", 2, RV)
        KS = region("odd", "KS", D, dt=F32R)
        V3 = region("odd", "V3", 2, EV, dt=F32R)
        OS = region("odd", "OS", H, 2 * NS)
        O = region("odd", "O", 2 * H, T)
        DT = region("odd", "DT", H, 2 * P)
        ST0 = region("odd", "ST0", NS * EV)
        odd_o = used["odd"] - H * 2 * P - NS * EV
        R1 = region("odd", "R1", 2, T)
        R2 = region("odd", "R2", 2, T)
        odd_sc = used["odd"]
        SC = region("odd", "SC", 2, ZW)
        KD = region("odd", "KD", 2, 2 * P)
        RP = region("odd", "RP", 2, EV)
        KM = region("odd", "KM", NS * P, dt=F32R)
        OF = O[:, :, :].rearrange("p n t -> p (n t)")
        SB = NS * EV
        ST = [ST0[:, :], DT[:, :, :].rearrange("p h n -> p (h n)"), OF[:, 0:SB], OF[:, SB:2 * SB]]
        FV = region("odd", "FV", 4, T, at=odd_sc)
        assert 4 * T <= 2 * ZW + 2 * 2 * P + 2 * EV
        YH = region("odd", "YH", 2 * H, T, dt=F32R, at=0)
        YL = region("odd", "YL", 2 * H, T, dt=F32R, at=2 * H * T)
        OD = SQ[:, 0:4, :].rearrange("p (u a) t -> p u a t", u=2)
        OQ = SQ[:, 4:8, :].rearrange("p (u a) t -> p u a t", u=2)
        HXH = region("moe", "HXH", NT, D, dt=F32R)
        HXL = region("moe", "HXL", NT, D, dt=F32R)
        XEH = region("moe", "XEH", DK, P, dt=F32R)
        XEL = region("moe", "XEL", DK, P, dt=F32R)
        OH = region("moe", "OH", NT, P, dt=F32R)
        OG = region("moe", "OG", NT, P)
        OT = region("moe", "OT", T)
        SI = region("moe", "SI", 2, IC)
        AC = region("moe", "AC", 2, IC)
        ATH = region("moe", "ATH", 2, 2 * P, dt=F32R)
        ATL = region("moe", "ATL", 2, 2 * P, dt=F32R)
        YE = region("moe", "YE", D)
        LG = region("moe", "LG", NT, E)
        MX = region("moe", "MX", NT, 8)
        MIF = region("moe", "MIF", NT, 8)
        GE = region("moe", "GE", NT, 8)
        SE = region("moe", "SE", NT, E)
        S1 = region("moe", "S1", NT, E)
        RK = region("moe", "RK", NT, E)
        TI = region("moe", "TI", 8, E)
        LT = region("moe", "LT", E, E)
        M1 = region("moe", "M1", TI_N, E)
        M2 = region("moe", "M2", TI_N, E)
        M3 = region("moe", "M3", TI_N, E)
        BA = region("moe", "BA", TI_N)
        M4 = region("moe", "M4", NT, TI_N * E)
        M5 = region("moe", "M5", NT, TI_N * E)
        LF = region("moe", "LF", T)
        CR = region("moe", "CR", TI_N, NT)
        CG = region("moe", "CG", TI_N, NT)
        CU = region("moe", "CU", 2, NT)
        EI = region("moe", "EI", TI_N + 1)
        YO = region("moe", "YO", NT, D, at=0)
        used["moe"] = max(used["moe"], odd_o)
        MORE = region("moe", "MORE", MRING - RING, CW)

        s_x = sem("s_x"); s_const = sem("s_const"); s_cc = sem("s_cc"); s_pt = sem("s_pt"); s_decay = sem("s_decay")
        s_ring = [sem(f"s_ring{i}") for i in range(MRING)]
        s_hi = sem("s_hi"); s_lo = sem("s_lo")
        s_kv = [sem(f"s_kv{i}") for i in range(4)]
        s_state = [sem(f"s_state{i}") for i in range(4)]
        s_turn = sem("s_turn"); s_xt = sem("s_xt"); s_sq = sem("s_sq"); s_ms = sem("s_ms"); s_rt = sem("s_rt")
        s_ht = sem("s_ht"); s_hh = sem("s_hh"); s_hl = sem("s_hl")
        s_zero = sem("s_zero"); s_cct = sem("s_cct"); s_win = sem("s_win")
        s_ag = sem("s_ag"); s_sig = sem("s_sig"); s_u = sem("s_u"); s_ut = sem("s_ut"); s_uo = sem("s_uo")
        s_dg = sem("s_dg"); s_cg = sem("s_cg"); s_conv = sem("s_conv"); s_cm = sem("s_cm"); s_cd = sem("s_cd"); s_cq = sem("s_cq"); s_cv = sem("s_cv")
        s_crt = sem("s_crt"); s_cn = sem("s_cn"); s_mixc = sem("s_mixc")
        s_qk = sem("s_qk"); s_qks = sem("s_qks"); s_vp = sem("s_vp"); s_vfe = sem("s_vfe"); s_vt = sem("s_vt"); s_vev = sem("s_vev"); s_qms = sem("s_qms")
        s_qrt = sem("s_qrt"); s_qn = sem("s_qn"); s_ktm = sem("s_ktm"); s_kto = sem("s_kto"); s_qs = sem("s_qs")
        s_qse = sem("s_qse"); s_z = sem("s_z"); s_zev = sem("s_zev"); s_qb = sem("s_qb"); s_kq = sem("s_kq")
        s_zs = sem("s_zs"); s_ln = sem("s_ln"); s_lk = sem("s_lk"); s_suf = sem("s_suf"); s_la = sem("s_la")
        s_exp = sem("s_exp"); s_a = sem("s_a"); s_av = sem("s_av"); s_ava = sem("s_ava"); s_avs = sem("s_avs")
        s_mixa = sem("s_mixa"); s_mh = sem("s_mh"); s_ml = sem("s_ml")
        s_down = sem("s_down")
        s_gu = sem("s_gu"); s_silu = sem("s_silu"); s_hid = sem("s_hid"); s_hdh = sem("s_hdh"); s_hdl = sem("s_hdl")
        s_rq = sem("s_rq"); s_rot = sem("s_rot"); s_rv = sem("s_rv"); s_rvf = sem("s_rvf"); s_rvt = sem("s_rvt"); s_rve = sem("s_rve"); s_ks = sem("s_ks")
        s_kse = sem("s_kse"); s_sc = sem("s_sc"); s_sce = sem("s_sce"); s_kt = sem("s_kt"); s_kde = sem("s_kde")
        s_o = sem("s_o"); s_oe = sem("s_oe"); s_rp = sem("s_rp"); s_rpe = sem("s_rpe"); s_rpo = [sem("s_rpo0"), sem("s_rpo1")]
        s_km = sem("s_km"); s_out = sem("s_out"); s_new = sem("s_new"); s_os = sem("s_os"); s_ose = sem("s_ose")
        s_ksl = sem("s_ksl"); s_v3l = sem("s_v3l"); s_osc = sem("s_osc")
        s_sto = [sem(f"s_sto{i}") for i in range(4)]
        s_om = sem("s_om"); s_od = sem("s_od"); s_oq = sem("s_oq"); s_ov = sem("s_ov"); s_ort = sem("s_ort")
        s_on = sem("s_on"); s_g = sem("s_g"); s_gs = sem("s_gs"); s_y = sem("s_y"); s_yh = sem("s_yh"); s_yl = sem("s_yl")
        s_lf = sem("s_lf"); s_lfe = sem("s_lfe"); s_lg = sem("s_lg"); s_ht2 = sem("s_ht2"); s_hx = sem("s_hx"); s_hxl = sem("s_hxl"); s_lgx = sem("s_lgx"); s_e2 = sem("s_e2")
        s_sel = sem("s_sel"); s_rk = sem("s_rk"); s_items = sem("s_items"); s_oh = sem("s_oh")
        s_ga = sem("s_ga"); s_xe = sem("s_xe"); s_oht = sem("s_oht"); s_ot = sem("s_ot"); s_mm = sem("s_mm")
        s_si = sem("s_si"); s_ac = sem("s_ac"); s_at = sem("s_at"); s_ate = sem("s_ate"); s_atl = sem("s_atl"); s_ye = sem("s_ye")
        s_yee = sem("s_yee"); s_sca = sem("s_sca"); s_add = sem("s_add"); s_yo = sem("s_yo")
        s_dn = sem("s_dn")
        s_ach = sem("s_ach"); s_dch = sem("s_dch")
        s_ydone = sem("s_ydone"); s_done = sem("s_done")
        ctx.enter_context(nc.allow_non_contiguous_dma(reason="small rows"))
        block = ctx.enter_context(nc.Block())

        def slot_of(q):
            return q % RING if q < C_MOE else (q - C_MOE + C_MOE % RING) % MRING

        def chunk(q):
            n = slot_of(q)
            return ring[:, n, :] if n < RING else MORE[:, n - RING, :]

        def uses_before(q):
            dense = len([i for i in range(min(q + 1, C_MOE)) if i % RING == slot_of(q)])
            return dense + len([i for i in range(C_MOE, q + 1) if slot_of(i) == slot_of(q)])

        def icols(w, c0):
            return w[:, c0:c0 + IC].rearrange("(k p) n -> p k n", p=P)

        def as_in(ap):
            return ap.rearrange("p (k n) -> p k n", n=IC)

        def down_parts(kt):
            return [(k, min(4, kt - k)) for k in range(0, kt, 4)]

        DOWN = [(C_OUTE, w_out_even, DK, 0), (C_DOWN, w_down, FT, 4), (C_OUTO, w_out_odd, RV // P, 16)]
        NDOWN = 24

        released = [(s_ag, 2), (s_ag, 4), (s_ag, 6), (s_ag, 8), (s_qk, 2), (s_qk, 4), (s_qk, 6), (s_qk, 8),
                    (s_vp, 2), (s_vp, 4)]
        released += [(s_down, 1 + n) for n in range(4)]
        released += [(s_gu, 2 * n + 2) for n in range(2 * FF // IC)]
        released += [(s_down, 5 + n) for n in range(12)]
        released += [(s_rq, 2 * n + 2) for n in range(8)]
        released += [(s_rv, 2 * (n + 1)) for n in range(8)]
        released += [(s_g, 2 * n + 2) for n in range(8)]
        released += [(s_down, 17 + n) for n in range(8)]
        assert len(released) == C_MOE

        def size(q):
            return 2 * 512 if q in (C_DOWN + 5, C_DOWN + 11) else CW

        ORDER = []
        for f in range(MSTEPS):
            ORDER += [("gate", f), ("up", f)] + ([("down", f - 2)] if f >= 2 else [])
        ORDER += [("down", MSTEPS - 2), ("down", MSTEPS - 1)]
        PLACE = {key: c for c, key in enumerate(ORDER)}

        def taps(g):
            w = g % CGT * CG_N
            return range(w, min(w + CG_N, W))

        def diag(g):
            return DG[(0 if g < 4 else 2) + g % 2]

        SCATTER = (0, 1, 4, 5)

        def through(c):
            kind, f = ORDER[c]
            return {"gate": (s_mm, 2 * f + 1, 2 * MSTEPS), "up": (s_mm, 2 * f + 2, 2 * MSTEPS),
                    "down": (s_dn, f + 1, MSTEPS)}[kind]

        @block.sync
        def _(sp):
            def load(q, dst, src):
                if q >= RING:
                    sp.wait_ge(s_lo, q - RING + 1)
                sp.dma_start(dst, src).then_inc(s_ring[q % RING], 16)

            def load_in(q, w, c0):
                load(q, as_in(chunk(q)), icols(w, c0))

            def load_down(d):
                q, w, kt, _ = DOWN[d]
                for half in range(2):
                    for k0, n in down_parts(kt):
                        load(q, chunk(q)[:, 0:n * 512].rearrange("p (k n) -> p k n", n=512),
                             w[0, k0 * P:(k0 + n) * P, half * 512:half * 512 + 512]
                             .rearrange("(k p) n -> p k n", p=P))
                        q += 1

            sp.dma_start(XI[:, 0:2, :], x_prompt.rearrange("o (a p) d -> p (o a) d", p=P)).then_inc(s_x, 16)
            sp.dma_start(XI[0:NS, 2, :], x_sample.rearrange("b o d -> (b o) d")).then_inc(s_x, 16)
            sp.dma_start(C[:], const).then_inc(s_const, 16)
            sp.dma_start(R[:], param).then_inc(s_const, 16)
            q = C_EVEN
            for c0 in (0, CH, IC, CH + IC, 2 * CH, 2 * CH + IC, 2 * CH + SBW, 2 * CH + SBW + IC,
                       2 * CH + 2 * SBW, 2 * CH + 2 * SBW + IC):
                load_in(q, w_in_even[0], c0)
                q += 1
            load_down(0)
            for f in range(FF // IC):
                load_in(C_FFN + 2 * f, w_gate[0], f * IC)
                load_in(C_FFN + 2 * f + 1, w_up[0], f * IC)
            load_down(1)
            for c in range(24):
                load_in(C_ODD + c, w_in_odd[0], c * IC)
            load_down(2)

            def load_expert(e, it):
                for c, (kind, f) in enumerate(ORDER):
                    if kind == "down":
                        src = m_down[0, bass.ds(e, 1), f * IC:(f + 1) * IC, :].rearrange("o (k p) n -> p (o k) n", p=P)
                    else:
                        w = m_gate if kind == "gate" else m_up
                        src = w[0, bass.ds(e, 1), :, f * IC:(f + 1) * IC].rearrange("o (k p) n -> p (o k) n", p=P)
                    q = C_MOE + c
                    if isinstance(it, int) and c < MRING:
                        n = slot_of(q)
                        if n < RING:
                            sp.wait_ge(s_lo, C_MOE - RING + (n - C_MOE) % RING + 1)
                        elif n == RING:
                            sp.wait_ge(s_yl, 2 * H)
                            for i in range(4):
                                sp.wait_ge(s_sto[i], 16 * H // 4)
                            for i in range(2):
                                sp.wait_ge(s_rpo[i], 16 * H // 2)
                    else:
                        sp.wait_ge(s_lo, it * MCH + (q - MRING + 1))
                    sp.dma_start(chunk(q).rearrange("p (k n) -> p k n", n=src.shape[2]), src)\
                        .then_inc(s_ring[slot_of(q)], 16)

            load_expert(0, 0)
            sp.wait_ge(s_items, 1)
            n_items = sp.value_load(EII[0:1, TI_N:TI_N + 1], min_val=E, max_val=MAXI)
            with sp.Fori(1, n_items) as it:
                e = sp.value_load(EII[0:1, bass.ds(it, 1)], min_val=0, max_val=E - 1)
                load_expert(e, it)
            for t in range(2):
                sp.wait_ge(s_yo, 2 * (t + 1))
                sp.dma_start(y_prompt[0, t * P:(t + 1) * P, :], YO[:, t, :]).then_inc(s_ydone, 16)
            sp.wait_ge(s_yo, 2 * NT)
            sp.dma_start(y_sample.rearrange("b o d -> (b o) d"), YO[0:NS, 2, :]).then_inc(s_ydone, 16)
            sp.wait_ge(s_ydone, 48)
            sp.wait_ge(s_done, 16 * 7)
            for i in range(4):
                sp.wait_ge(s_sto[i], 16 * H // 4)

        @block.gpsimd
        def _(pool):
            pool.dma_start(PG[:], page_table.rearrange("(o b) g -> o (b g)", o=1)).then_inc(s_pt, 16)
            for b in range(2):
                pool.dma_start(CC[0:120, b, :], cache_conv[0, 4 * b:4 * b + 4].rearrange("b w c -> (b w) c"))\
                    .then_inc(s_cc, 16)
            nc.gpsimd.memset(U[:, :, 0:W - 1], 0.0).then_inc(s_zero, 1)
            pool.dma_start(conv_sample[0, :, 0:W - 2, :], cache_conv[0, :, 1:W - 1, :]).then_inc(s_done, 16)
            pool.wait_ge(s_pt, 16)


            def pages(b, cache):
                for g in range(PAGES):
                    i = b * PAGES + g
                    late = cache is cache_v and b >= 4
                    page = pool.value_load(PG[0:1, i:i + 1], min_val=0, max_val=cache.shape[1] - 1)
                    pool.dma_start(LATE[i % NS] if late else KV[:, i % NS, :],
                                   cache[0, bass.ds(page, 1)].rearrange("o p h d -> p (o h d)"))\
                        .then_inc((s_state if late else s_kv)[b % 4], 16)

            cw = param_("conv_w")

            def spread_taps(g):
                if g >= 4:
                    pool.wait_ge(s_qn, 2 * HP)
                if g % 4 >= 2:
                    pool.wait_ge(s_cg, g - 1)
                n = len(taps(g))
                at = g // CGT * W + taps(g)[0]
                nc.gpsimd.tensor_tensor(diag(g)[:, 0:n, :],
                                        ident.rearrange("p (o n) -> p o n", o=1).to_broadcast([P, n, P]),
                                        cw[:, at:at + n].rearrange("p (w o) -> p w o", o=1).to_broadcast([P, n, P]),
                                        ALU.mult).then_inc(s_dg, 1)

            for b in range(4):
                pages(b, cache_k)
            pool.wait_ge(s_const, 32)
            for g in range(2 * CGT):
                spread_taps(g)
            for b in range(4, NS):
                pool.wait_ge(s_kq, b - 3)
                pages(b, cache_k)
            pool.wait_ge(s_uo, 1)
            pool.dma_start(conv_prompt[0, 0], UO[:]).then_inc(s_done, 16)
            pool.wait_ge(s_uo, 2)
            pool.dma_start(conv_sample[0, :, W - 2, :], US[:]).then_inc(s_done, 16)
            pool.wait_ge(s_vev, NT)
            pool.dma_start(v_prompt[0, 0].rearrange("(a p) h d -> p a (h d)", p=P), VT[:, 0:2, :])\
                .then_inc(s_done, 16)
            pool.dma_start(v_sample[0].rearrange("b o h d -> (b o) (h d)"), VT[0:NS, 2, :]).then_inc(s_done, 16)
            pool.wait_ge(s_kto, NT)
            pool.dma_start(k_prompt[0, 0].rearrange("(a p) h d -> p a (h d)", p=P), KO[:, 0:2, :])\
                .then_inc(s_done, 16)
            pool.dma_start(k_sample[0].rearrange("b o h d -> (b o) (h d)"), KO[0:NS, 2, :]).then_inc(s_done, 16)
            pool.wait_ge(s_z, H)
            pool.wait_ge(s_cg, 2 * CGT)
            pool.wait_ge(s_ut, 1)
            pool.wait_ge(s_qn, 2 * HP)
            for b in range(4, NS - 1):
                pages(b, cache_v)
            for b in range(4):
                pool.wait_ge(s_kq, b + 5)
                pages(b, cache_v)
            pool.wait_ge(s_cd, 1)
            pages(NS - 1, cache_v)
            def state_in(h):
                pool.dma_start(ST[h % 4].rearrange("p (b e) -> p b e", e=EV),
                               state_ret[0, :, h].rearrange("b d e -> d b e")).then_inc(s_state[h % 4], 16)

            pool.wait_ge(s_done, 16 * 7)
            pool.wait_ge(s_hid, 1)
            state_in(0)
            state_in(1)
            pool.wait_ge(s_down, 16)
            state_in(2)
            state_in(3)
            for h in range(H):
                if h == H - 1:
                    pool.wait_ge(s_sto[1], 16 * H // 4)
                    pool.wait_ge(s_os, H - 2)
                    pool.dma_start(DT[:], decay.rearrange("p (h n) -> p h n", n=2 * P)).then_inc(s_decay, 16)
                pool.wait_ge(s_new, 4 * (h + 1))
                pool.dma_start(ret_sample[0, :, h].rearrange("b d e -> d b e"),
                               ST[h % 4].rearrange("p (b e) -> p b e", e=EV)).then_inc(s_sto[h % 4], 16)
                if h + 4 < H:
                    pool.wait_ge(s_sto[h % 4], 16)
                    pool.wait_ge(s_os, h + 1)
                    state_in(h + 4)
            for h in range(H):
                pool.wait_ge(s_rpe, h + 1)
                pool.dma_start(ret_prompt[0, 0, h], RP[:, h % 2, :]).then_inc(s_rpo[h % 2], 16)
            for i in range(2):
                pool.wait_ge(s_rpo[i], 16 * H // 2)

        @block.tensor
        def _(pe):
            mm = nc.tensor.matmul
            turn = nc.tensor.transpose

            def arrived(q):
                pe.wait_ge(s_lo, q + 1)

            def mm3(out, lh, ll, rh, rl, start, stop):
                mm(out, lh, rh, start=start, stop=False)
                mm(out, lh, rl, start=False, stop=False)
                return mm(out, ll, rh, start=False, stop=stop)

            def parts(q):
                return WH[:, q % WRING, :], WL[:, q % WRING, :]

            def sumsq(r):
                for k in range(DK):
                    if k % 2 == 0:
                        pe.wait_ge(s_sq, 4 * r + k // 2 + 1)
                    last = mm(PB[4][:, 0:T], const_("mean_d"), SQ[:, k, :], start=(k == 0), stop=(k == DK - 1))
                last.then_inc(s_ms, 1)

            def project(q, j, out, done, first=None):
                wh, wl = (as_in(x) for x in parts(q))
                if j == 0:
                    arrived(q)
                cols = slice(j * P, (j + 1) * P)
                for k in range(DK):
                    if first is not None:
                        pe.wait_ge(s_hl, DK * first + k + 1)
                    last = mm3(out, wh[:, k, cols], wl[:, k, cols], HH[:, k, :], HL[:, k, :], k == 0, k == DK - 1)
                last.then_inc(done, 1)

            def project_first(q, outs, done, r):
                arrived(q)
                wh, wl = (as_in(x) for x in parts(q))
                for k in range(DK):
                    pe.wait_ge(s_hl, DK * r + k + 1)
                    for i, out in enumerate(outs):
                        cols = slice(i * P, (i + 1) * P)
                        last = mm3(out, wh[:, k, cols], wl[:, k, cols], HH[:, k, :], HL[:, k, :], k == 0, k == DK - 1)
                        if k == DK - 1:
                            last.then_inc(done, 1)

            def down(d, sh, sl, ready):
                q, _, kt, _ = DOWN[d]
                for half in range(2):
                    for k0, n in down_parts(kt):
                        arrived(q)
                        wh, wl = (x[:, 0:n * 512].rearrange("p (k n) -> p k n", n=512) for x in parts(q))
                        for kk in range(n):
                            k = k0 + kk
                            if half == 0:
                                ready(k)
                            for j in range(4):
                                cols = slice(j * P, (j + 1) * P)
                                last = mm3(PB[4 * (1 - half) + j][:, 0:T], wh[:, kk, cols], wl[:, kk, cols],
                                           sh[:, k, :], sl[:, k, :], k == 0, k == kt - 1)
                        last.then_inc(s_down, 1)
                        q += 1

            pe.wait_ge(s_x, 32)
            pe.wait_ge(s_const, 32)
            for k in range(DK):
                if k >= 4:
                    pe.wait_ge(s_xt, k - 3)
                for t in range(NT):
                    last = turn(PB[k % 4][:, t * P:t * P + TOK[t]],
                                XI[0:TOK[t], t, k * P:(k + 1) * P], ident[0:TOK[t], 0:TOK[t]])
                last.then_inc(s_turn, 1)
            pe.wait_ge(s_cc, 32)
            for c in range(CT):
                for b in range(2):
                    last = turn(PB[4 + c][:, b * 120:b * 120 + 120], CC[0:120, b, c * P:(c + 1) * P],
                                ident[0:120, 0:120])
                last.then_inc(s_cct, 1)
            pe.wait_ge(s_win, 1)
            sumsq(0)

            for c in range(2):
                if c == 1:
                    pe.wait_ge(s_win, CT)
                for g in range(2):
                    for j in range(2):
                        project(C_EVEN + 2 * c + g, j, PB[4 * c + 2 * g + j][:, 0:T], s_ag,
                                first=0 if c == g == j == 0 else None)
            for n in range(2 * HP):
                pe.wait_ge(s_u, 2 * (n // 4) + n % 2 + 1)
                project(C_EVEN + 4 + n // 2, n % 2, PB[n][:, 0:T], s_qk)
            for n in range(HP):
                pe.wait_ge(s_qks, n + 1)
                project(C_EVEN + 8 + n // 2, n % 2, PB[n][:, 0:T], s_vp)
            pe.wait_ge(s_vfe, HP)
            for t in range(NT):
                for j in range(HP):
                    last = turn(PB[t][0:TOK[t], j * P:(j + 1) * P], FVE[:, j, t * P:t * P + TOK[t]], ident)
                last.then_inc(s_vt, 1)
            pe.wait_ge(s_qks, 2 * HP)
            for c in range(CT):
                last = turn(PB[4][0:W - 1, c * P:(c + 1) * P], U[:, c, SEQ:SEQ + W - 1], ident)
            last.then_inc(s_ut, 1)
            for c in range(CT):
                last = turn(PB[5][0:NS, c * P:(c + 1) * P], UF[:, c, :, W - 1], ident)
            last.then_inc(s_ut, 1)

            def conv(g):
                if g == 0:
                    pe.wait_ge(s_zero, 1)
                    pe.wait_ge(s_u, CT)
                    pe.wait_ge(s_uo, 1)
                pe.wait_ge(s_dg, g + 1)
                c = g // CGT
                for i, w in enumerate(taps(g)):
                    last = mm(PB[4][:, c % 2 * SEQ:(c % 2 + 1) * SEQ], diag(g)[:, i, :], U[:, c, w:w + SEQ],
                              start=(w == 0), stop=(w == W - 1))
                last.then_inc(s_cg, 1)

            for n in range(2 * HP):
                pe.wait_ge(s_qks, 8 if n < 2 else n + 1)
                if n >= 2:
                    pe.wait_ge(s_qrt, n - 1)
                mm(PB[6 + n % 2][:, 0:T], const_("mean_hd"), SQ[:, n, :], start=True, stop=True).then_inc(s_qms, 1)
                if n % 2:
                    conv(n // 2)
            pe.wait_ge(s_qn, HP)
            for j in range(HP):
                last = turn(PB[3][0:NS, j * P:(j + 1) * P], QN[:, j, SEQ:T], ident)
            last.then_inc(s_qs, 1)
            pe.wait_ge(s_qn, 2 * HP)
            for t in range(NT):
                pe.wait_ge(s_vev, t + 1)
                for j in range(HP):
                    last = turn(PB[t][0:TOK[t], j * P:(j + 1) * P], QN[:, HP + j, t * P:t * P + TOK[t]], ident)
                last.then_inc(s_ktm, 1)
            def scores_even(h):
                if h < NT:
                    pe.wait_ge(s_kto, h + 1)
                elif h == NT:
                    pe.wait_ge(s_qse, 1)
                else:
                    pe.wait_ge(s_zev, h - 3)
                o = HD * (h % 2)
                q, k = QN[o:o + HD, h // 2, :], QN[o:o + HD, HP + h // 2, :]
                mm(PB[h % 4][:, 0:SEQ], k[:, 0:P], q[:, 0:SEQ], start=True, stop=True)
                mm(PB[h % 4][:, SEQ:ZW], k[:, P:SEQ], q[:, P:SEQ], start=True, stop=True).then_inc(s_z, 1)

            def spread_q(b):
                if b >= 3:
                    pe.wait_ge(s_kq, b - 2)
                mm(PB[5 + b % 3][:, 0:SBW], C[0:NS, b:b + 1].to_broadcast([NS, P]), QS[:], start=True, stop=True)\
                    .then_inc(s_qb, 1)

            pe.wait_ge(s_uo, 2)
            pe.wait_ge(s_qrt, 2 * HP)
            pe.wait_ge(s_qse, 1)
            for b in range(3):
                spread_q(b)
            for h in range(4):
                scores_even(h)
            conv(4)
            for h in range(4, H):
                scores_even(h)
            for b in range(3, NS):
                if b < 6:
                    conv(2 + b)
                spread_q(b)
            pe.wait_ge(s_conv, 2)
            for c in range(CT):
                last = mm(PB[4][:, 0:T], const_("mean_ch"), CA[:, c, :], start=(c == 0), stop=(c == CT - 1))
            last.then_inc(s_cm, 1)
            for h in range(H + 1):
                if h < 4:
                    pe.wait_ge(s_zev, 4 + h + 1)
                else:
                    pe.wait_ge(s_la, h - 3)
                if h % 4 == 0:
                    pe.wait_ge(s_lk, min(h // 4 + 1, 2))
                if h < H:
                    lk = Z[:, h * ZW:(h + 1) * ZW]
                    mm(PB[h % 4][:, 0:ZW], const_("negtri"), lk, start=True, stop=False)
                    mm(PB[h % 4][:, P:SEQ], const_("negones"), lk[:, SEQ:ZW], start=False, stop=True)\
                        .then_inc(s_suf, 1)
                else:
                    lk = Z[:, ZP:ZP + ZS]
                    mm(PB[h % 4][:, 0:ZS], const_("negtri"), lk, start=True, stop=False)
                    mm(PB[h % 4][:, 0:ZS // 2], const_("negones"), lk[:, ZS // 2:ZS], start=False, stop=True)\
                        .then_inc(s_suf, 1)
            pe.wait_ge(s_la, H - 1)
            pe.wait_ge(s_cq, 1)
            for c in range(CT):
                last = mm(PB[2][:, 0:T], const_("mean_ch"), CQ[:, c, :], start=(c == 0), stop=(c == CT - 1))
            last.then_inc(s_cv, 1)
            pe.wait_ge(s_kq, NS)
            for h in range(H):
                if h % 4 == 0:
                    pe.wait_ge(s_a, h // 4 + 1)
                o = HD * (h % 2)
                out = PB[4 + h // 2][o:o + HD, :]
                a = A[:, h * ZW:(h + 1) * ZW]
                mm(out[:, 0:SEQ], VT[:, 0, h * HD:(h + 1) * HD], a[:, 0:SEQ], start=True, stop=False)
                mm(out[:, P:SEQ], VT[:, 1, h * HD:(h + 1) * HD], a[:, SEQ:ZW], start=False, stop=True)\
                    .then_inc(s_av, 1)
            for b in range(NS):
                if b < 4:
                    pe.wait_ge(s_kv[b], 32 * 3)
                else:
                    pe.wait_ge(s_state[b - 4], 32)
                for hp in range(HP):
                    for g in range(PAGES):
                        at = ZP + (g * NS + b) * H + 2 * hp
                        last = mm(PB[0][:, (hp * NS + b) * 2:(hp * NS + b) * 2 + 2],
                                  (KV[:, b * PAGES + g, :] if b < 4 else LATE[(b - 4) * PAGES + g])
                                  [:, hp * P:(hp + 1) * P], A[:, at:at + 2],
                                  start=(g == 0), stop=(g == PAGES - 1))
                last.then_inc(s_avs, 1)
            pe.wait_ge(s_mixa, HP + 2)
            down(0, HH, HL, lambda k: pe.wait_ge(s_ml, k + 1))

            sumsq(1)
            project_first(C_FFN, (PB[0][:, 0:T], PB[1][:, 0:T]), s_gu, 1)
            for c in range(FF // IC):
                if c >= 2:
                    pe.wait_ge(s_hid, 2 * (c - 1))
                for g in range(1 if c == 0 else 0, 2):
                    for j in range(2):
                        project(C_FFN + 2 * c + g, j, PB[4 * (c % 2) + 2 * g + j][:, 0:T], s_gu)
            pe.wait_ge(s_hid, FT - 2)
            down(1, HDH, HDL, lambda k: pe.wait_ge(s_hdl, k + 1))

            sumsq(2)
            project_first(C_ODD, (PB[0][:, 0:T], PB[1][:, 0:T]), s_rq, 2)
            for n in range(2, 2 * H):
                if n >= 4:
                    pe.wait_ge(s_rot, n - 3)
                project(C_ODD + n // 2, n % 2, PB[n % 4][:, 0:T], s_rq)

            def turn_v(c):
                pe.wait_ge(s_rvf, 2 * c + 2)
                if c >= 1:
                    pe.wait_ge(s_rve, 2 * c)
                    pe.wait_ge(s_v3l, c)
                for t in range(NT):
                    for j in range(2):
                        out = PB[2 + t // 2][0:TOK[t], (t % 2) * IC + j * P:(t % 2) * IC + (j + 1) * P]
                        last = turn(out, FV[:, 2 * (c % 2) + j, t * P:t * P + TOK[t]], ident)
                    if t >= 1:
                        last.then_inc(s_rvt, 1)

            def outer(h, groups):
                pe.wait_ge(s_v3l, h + 1)
                pe.wait_ge(s_km, h + 1)
                for g in groups:
                    u = 4 * h + g
                    if u >= 3:
                        pe.wait_ge(s_new, u - 2)
                    for i in range(2):
                        b = 2 * g + i
                        last = mm(PB[4 + u % 3][:, i * EV:(i + 1) * EV], KM[0:96, b * P:(b + 1) * P],
                                  V3[0:96, h % 2, :], start=True, stop=True)
                    last.then_inc(s_out, 1)

            def sample_outputs(h):
                pe.wait_ge(s_new, 4 * (h + 1))
                if h >= 1:
                    pe.wait_ge(s_ose, h)
                for j in range(2):
                    for b in range(NS):
                        last = mm(PB[7][:, j * NS + b:j * NS + b + 1],
                                  ST[h % 4][:, b * EV + j * P:b * EV + (j + 1) * P],
                                  QT[:, h, SEQ + b:SEQ + b + 1], start=True, stop=True)
                last.then_inc(s_os, 1)

            for c in range(H + 3):
                if c < H:
                    for j in range(2):
                        n = 2 * c + j
                        if n < 2:
                            pe.wait_ge(s_rot, 2 * H - 3 + n)
                        else:
                            pe.wait_ge(s_rvf, n - 1)
                        project(C_ODD + 8 + c, j, PB[n % 2][:, 0:T], s_rv)
                if c == 0:
                    pe.wait_ge(s_rot, 2 * H)
                    for h in range(H):
                        last = turn(PB[4 + h // 4][0:NS, (h % 4) * P:(h % 4 + 1) * P], KT[:, h, SEQ:T], ident)
                    last.then_inc(s_ks, 1)
                if 1 <= c <= H:
                    turn_v(c - 1)
                if 2 <= c <= H + 1:
                    outer(c - 2, range(3))
                if c >= 3:
                    sample_outputs(c - 3)
                if 2 <= c <= H + 1:
                    outer(c - 2, (3,))
            pe.wait_ge(s_rve, 2 * H)
            pe.wait_ge(s_ose, H)

            def scores(h):
                if h >= 2:
                    pe.wait_ge(s_sce, h - 1)
                    pe.wait_ge(s_kde, h - 1)
                    pe.wait_ge(s_rpe, h - 1)
                mm(PB[h % 2][:, 0:SEQ], KT[:, h, 0:P], QT[:, h, 0:SEQ], start=True, stop=True)
                mm(PB[h % 2][:, SEQ:ZW], KT[:, h, P:SEQ], QT[:, h, P:SEQ], start=True, stop=True).then_inc(s_sc, 1)
                for m in range(2):
                    last = turn(PB[2 + h % 2][:, m * P:(m + 1) * P], KT[:, h, m * P:(m + 1) * P], ident)
                last.then_inc(s_kt, 1)

            scores(0)
            for h in range(H):
                if h + 1 < H:
                    scores(h + 1)
                pe.wait_ge(s_sce, h + 1)
                if h >= 2:
                    pe.wait_ge(s_oe, 2 * (h - 1))
                for j in range(2):
                    out = PB[4 + 2 * (h % 2) + j]
                    v = VR[:, :, h * EV + j * P:h * EV + (j + 1) * P]
                    mm(out[:, 0:SEQ], v[:, 0, :], SC[:, h % 2, 0:SEQ], start=True, stop=False)
                    mm(out[:, P:SEQ], v[:, 1, :], SC[:, h % 2, SEQ:ZW], start=False, stop=True).then_inc(s_o, 1)
                pe.wait_ge(s_kde, h + 1)
                for m in range(2):
                    last = mm(PB[2 + h % 2][:, EV:2 * EV], KD[:, h % 2, m * P:(m + 1) * P],
                              VR[:, m, h * EV:(h + 1) * EV], start=(m == 0), stop=(m == 1))
                last.then_inc(s_rp, 1)
            pe.wait_ge(s_oe, 2 * H)
            pe.wait_ge(s_rpe, H)

            def mean(h):
                if h == 0:
                    pe.wait_ge(s_osc, 1)
                if h >= 2:
                    pe.wait_ge(s_od, h - 1)
                for j in range(2):
                    last = mm(PB[h % 2][:, 0:T], const_("mean_ev"), O[:, 2 * h + j, :], start=(j == 0), stop=(j == 1))
                last.then_inc(s_om, 1)

            mean(0)
            mean(1)
            for h in range(H):
                pe.wait_ge(s_oq, h + 1)
                if h >= 2:
                    pe.wait_ge(s_ort, h - 1)
                for j in range(2):
                    last = mm(PB[2 + h % 2][:, 0:T], const_("mean_ev"), OQ[:, h % 2, j, :],
                              start=(j == 0), stop=(j == 1))
                last.then_inc(s_ov, 1)
                if h + 2 < H:
                    mean(h + 2)
                for j in range(2):
                    n = 2 * h + j
                    if n >= 4:
                        pe.wait_ge(s_y, n - 3)
                    project(C_ODD + 16 + h, j, PB[4 + n % 4][:, 0:T], s_g)
            pe.wait_ge(s_y, 2 * H)
            down(2, YH, YL, lambda k: pe.wait_ge(s_yl, k + 1))

            sumsq(3)
            router = param_("router").rearrange("p (k e) -> p k e", e=E)
            for k in range(DK):
                pe.wait_ge(s_ht, 3 * DK + k + 1)
                last = mm(PB[0][0:E, 0:T], router[:, k, :], HT[:, k, :], start=(k == 0), stop=(k == DK - 1))
            last.then_inc(s_lf, 1)

            def turn_x(i):
                t, half = i // 2, i % 2
                for k in range(4):
                    last = turn(PB[2 + i][0:TOK[t], k * P:(k + 1) * P],
                                HT[:, 4 * half + k, t * P:t * P + TOK[t]], ident)
                last.then_inc(s_ht2, 1)

            turn_x(0)
            pe.wait_ge(s_lfe, 1)
            for t in range(NT):
                last = turn(PB[1][0:TOK[t], P + t * E:P + (t + 1) * E], LF[0:E, t * P:t * P + TOK[t]],
                            ident[0:E, 0:E])
            last.then_inc(s_lg, 1)
            for i in range(1, 2 * NT):
                turn_x(i)
            pe.wait_ge(s_sel, 1)
            mm(PB[1][:, 0:NT * E], const_("below"), SE[:, :, :], start=True, stop=False)
            mm(PB[1][:, E:NT * E], const_("ones"), SE[:, 0:2, :], start=False, stop=False)
            mm(PB[1][:, 2 * E:NT * E], const_("ones"), SE[:, 0, :], start=False, stop=True)
            mm(PB[1][:, 32:32 + NT * E], const_("ones"), SE[:, :, :], start=True, stop=True).then_inc(s_rk, 1)
            pe.wait_ge(s_hx, 2 * NT)
            pe.wait_ge(s_items, 1)
            n_items = pe.value_load(EII[0:1, TI_N:TI_N + 1], min_val=E, max_val=MAXI)

            def gather(it, part):
                if part == 0:
                    pe.wait_ge(s_oh, it + 1)
                for half in range(2):
                    for k in range(4):
                        at = (4 * half + k) * P
                        for t in range(NT):
                            last = mm(PB[2 * part + half][:, k * P:(k + 1) * P],
                                      (HXH, HXL)[part][0:TOK[t], t, at:at + P],
                                      OH[0:TOK[t], t, :], start=(t == 0), stop=(t == NT - 1))
                    last.then_inc(s_ga, 1)

            def scatter(it, ks):
                pe.wait_ge(s_yee, it * 2 + 2)
                pe.wait_ge(s_ot, it + 1)
                pe.wait_ge(s_xe, it * 4 + 2)
                for k in ks:
                    if k >= 4:
                        pe.wait_ge(s_add, it * DK + k - 3)
                    mm(PB[SCATTER[k % 4]][:, 0:T], YE[:, k * P:(k + 1) * P], OT[:, :], start=True, stop=True)\
                        .then_inc(s_sca, 1)

            gather(0, 0)
            pe.wait_ge(s_hxl, 2 * NT)
            gather(0, 1)
            with pe.Fori(0, n_items) as it:
                def hidden(f):
                    if f >= 2:
                        pe.wait_ge(s_ac, it * MSTEPS + f - 1)
                    for g, kind in enumerate(("gate", "up")):
                        q = C_MOE + PLACE[(kind, f)]
                        pe.wait_ge(s_lo, it * MCH + (q + 1))
                        wh, wl = (as_in(x) for x in parts(q))
                        for k in range(DK):
                            if f == 0 and g == 0 and k == 0:
                                pe.wait_ge(s_xe, it * 4 + 4)
                            last = mm3(PB[2 + f % 2][:, g * IC:(g + 1) * IC], XEH[:, k, :], XEL[:, k, :],
                                       wh[:, k, :], wl[:, k, :], k == 0, k == DK - 1)
                        last.then_inc(s_mm, 1)

                def turn_hidden(f):
                    pe.wait_ge(s_ac, it * MSTEPS + f + 1)
                    if f == 1:
                        pe.wait_ge(s_ot, it + 2)
                    if f >= 2:
                        pe.wait_ge(s_atl, it * MSTEPS + f - 1)
                    for j in range(2):
                        last = turn(PB[6 + f % 2][:, j * P:(j + 1) * P], AC[:, f % 2, j * P:(j + 1) * P], ident)
                    last.then_inc(s_at, 1)

                def project_down(f):
                    q = C_MOE + PLACE[("down", f)]
                    pe.wait_ge(s_lo, it * MCH + (q + 1))
                    pe.wait_ge(s_atl, it * MSTEPS + f + 1)
                    if f == 0:
                        pe.wait_ge(s_add, it * DK + DK)
                    wh, wl = (x.rearrange("p (k n) -> p k n", n=D) for x in parts(q))
                    for j in range(2):
                        rows = slice(j * P, (j + 1) * P)
                        for half in range(2):
                            cols = slice(half * 512, (half + 1) * 512)
                            last = mm3(PB[4 + half][:, :], ATH[:, f % 2, rows], ATL[:, f % 2, rows],
                                       wh[:, j, cols], wl[:, j, cols], f == 0 and j == 0,
                                       f == MSTEPS - 1 and j == 1)
                    last.then_inc(s_dn, 1)

                for f in range(MSTEPS):
                    hidden(f)
                    if f <= 1:
                        scatter(it, range(4 * f, 4 * f + 4))
                    if f == 1:
                        for t in range(NT):
                            last = turn(PB[7][:, t * P:t * P + TOK[t]], OG[0:TOK[t], t, :], ident[0:TOK[t], 0:TOK[t]])
                        last.then_inc(s_oht, 1)
                    if f >= 1:
                        turn_hidden(f - 1)
                    if f >= 2:
                        project_down(f - 2)
                gather(it + 1, 0)
                turn_hidden(MSTEPS - 1)
                gather(it + 1, 1)
                project_down(MSTEPS - 2)
                project_down(MSTEPS - 1)
            scatter(n_items, range(DK))
            pe.wait_ge(s_add, n_items * DK + DK)
            for i in range(2 * NT):
                t, half = i // 2, i % 2
                for k in range(4):
                    last = turn(PB[i][0:TOK[t], k * P:(k + 1) * P], XT[:, 4 * half + k, t * P:t * P + TOK[t]], ident)
                last.then_inc(s_turn, 1)

        @block.scalar
        def _(act):
            func = nc.scalar.activation
            high = [0]

            def prepare(q):
                q = min(q, C_MOE - 1)
                for n in range(high[0], q + 1):
                    act.wait_ge(s_ring[slot_of(n)], 16 * uses_before(n))
                    if n >= WRING:
                        act.wait_ge(*released[n - WRING])
                    func(WH[:, n % WRING, 0:size(n)], chunk(n)[:, 0:size(n)], ACT.Copy).then_inc(s_hi, 1)
                high[0] = max(high[0], q + 1)

            def norm_act(r, q):
                for i in range(4):
                    act.wait_ge(s_xt, DK * r + 2 * i + 2)
                    if r and i == 0:
                        act.wait_ge(s_down, DOWN[r - 1][3] + 1)
                    func(SQ[:, 2 * i:2 * i + 2, :], XT[:, 2 * i:2 * i + 2, :], ACT.Square).then_inc(s_sq, 1)
                prepare(q)
                act.wait_ge(s_ms, r + 1)
                func(RS[:, 0, :], PB[4][:, 0:T], ACT.Sqrt, bias=eps).then_inc(s_rt, 1)
                if r < 3:
                    for k in range(DK):
                        act.wait_ge(s_ht, DK * r + k + 1)
                        func(HH[:, k, :], HT[:, k, :], ACT.Copy).then_inc(s_hh, 1)

            def down_act(d):
                q, _, kt, _ = DOWN[d]
                prepare(q + 2 * len(down_parts(kt)) + 1)

            act.wait_ge(s_const, 32)
            for c in range(CT):
                act.wait_ge(s_cct, c + 1)
                func(UF[:, c, :, 0:W - 1], PB[4 + c][:, 0:NS * (W - 1)].rearrange("p (b w) -> p b w", w=W - 1),
                     ACT.Copy).then_inc(s_win, 1)
            norm_act(0, 0)
            prepare(C_EVEN + 3)
            for c in range(CT):
                act.wait_ge(s_ag, 4 * (c // 2) + 2 + c % 2 + 1)
                func(SG[:, c, :], PB[4 * (c // 2) + 2 + c % 2][:, 0:T], ACT.Sigmoid).then_inc(s_sig, 1)
                if c == 1:
                    prepare(C_EVEN + 5)
            prepare(C_EVEN + 6)
            for n in range(2 * HP):
                act.wait_ge(s_qk, n + 1)
                func(QR[:, n, :], PB[n][:, 0:T], ACT.Copy)
                func(SQ[:, n, :], PB[n][:, 0:T], ACT.Square).then_inc(s_qks, 1)
                if n % 2:
                    prepare(C_EVEN + 7 + n // 2)
            for n in range(HP):
                act.wait_ge(s_vp, n + 1)
                func(FVE[:, n, :], PB[n][:, 0:T], ACT.Copy).then_inc(s_vfe, 1)
                if n % 2:
                    prepare(C_EVEN + 11 + n // 2)
            for t in range(NT):
                act.wait_ge(s_vt, t + 1)
                func(VT[0:TOK[t], t, :], PB[t][0:TOK[t], :], ACT.Copy).then_inc(s_vev, 1)
            act.wait_ge(s_ut, 1)
            func(UO[:], PB[4][0:W - 1, :], ACT.Copy).then_inc(s_uo, 1)
            act.wait_ge(s_ut, 2)
            func(US[:], PB[5][0:NS, :], ACT.Copy).then_inc(s_uo, 1)
            for n in range(2 * HP):
                act.wait_ge(s_qms, n + 1)
                if n >= 2:
                    act.wait_ge(s_qn, n - 1)
                func(RS[:, n % 2, :], PB[6 + n % 2][:, 0:T], ACT.Sqrt, bias=eps).then_inc(s_qrt, 1)
            act.wait_ge(s_qs, 1)
            func(QS[:], PB[3][0:NS, :], ACT.Copy).then_inc(s_qse, 1)
            for t in range(NT):
                act.wait_ge(s_ktm, t + 1)
                func(KO[0:TOK[t], t, :], PB[t][0:TOK[t], :], ACT.Copy).then_inc(s_kto, 1)
            bias = param_("bias")
            for h in range(H):
                act.wait_ge(s_z, h + 1)
                func(Z[:, h * ZW:(h + 1) * ZW], PB[h % 4][:, 0:ZW], ACT.Identity, bias=bias[:, h:h + 1],
                     scale=HD ** -0.5).then_inc(s_zev, 1)

            act.wait_ge(s_cg, 2 * CGT)
            for c in range(2):
                func(CA[:, c, 0:SEQ], PB[4][:, c * SEQ:(c + 1) * SEQ], ACT.Identity,
                     bias=param_("conv_b")[:, c:c + 1]).then_inc(s_conv, 1)
            step = 0
            for g in range(2):
                part = slice(g * ZP // 2, ZP // 2 if g == 0 else ZP + ZS)
                act.wait_ge(s_zev, 4 * (g + 1))
                if g == 1:
                    act.wait_ge(s_zs, 1)
                for src, f, kw in ((Z, ACT.Abs, {}), (L, ACT.Exp, dict(scale=-1.0)), (L, ACT.Ln, dict(bias=1.0))):
                    if step % 3:
                        act.wait_ge(s_ach, step - step // 3)
                    n = part.stop - part.start
                    if step == 3:
                        act.wait_ge(s_lk, 1)
                    func(L[:, 0:n], src[:, part] if src is Z else L[:, 0:n], f, **kw).then_inc(s_ln if f == ACT.Ln else s_ach, 1)
                    step += 1
            act.wait_ge(s_cd, 1)
            func(CQ, CD, ACT.Square).then_inc(s_cq, 1)
            for g in range(2):
                part = slice(g * ZP // 2, ZP // 2 if g == 0 else ZP + ZS)
                act.wait_ge(s_la, 4 if g == 0 else H + 1)
                func(A[:, part], A[:, part], ACT.Exp).then_inc(s_exp, 1)
            act.wait_ge(s_cv, 1)
            func(RS[:, 0, :], PB[2][:, 0:T], ACT.Sqrt, bias=eps).then_inc(s_crt, 1)
            ln_b = param_("ln_b")
            for c in range(CT):
                act.wait_ge(s_cn, c + 1)
                func(MIX[:, c, :], CD[:, c, :], ACT.Silu, bias=ln_b[:, c:c + 1]).then_inc(s_mixc, 1)
            act.wait_ge(s_mixc, CT)
            for k in range(DK):
                if k == CT:
                    act.wait_ge(s_mixa, HP + 2)
                func(HH[:, k, :], MIX[:, k, :], ACT.Copy).then_inc(s_mh, 1)
            down_act(0)

            norm_act(1, C_FFN + 2)
            for c in range(FF // IC):
                for j in range(2):
                    i = 2 * c + j
                    act.wait_ge(s_gu, 4 * c + j + 1)
                    if i >= 2:
                        act.wait_ge(s_hid, i - 1)
                    func(GA[:, j, :], PB[4 * (c % 2) + j][:, 0:T], ACT.Silu).then_inc(s_silu, 1)
                prepare(C_FFN + 2 * c + 3)
                for j in range(2):
                    act.wait_ge(s_hid, 2 * c + j + 1)
                    func(HDH[:, 2 * c + j, :], HF[:, j, :], ACT.Copy).then_inc(s_hdh, 1)
                prepare(C_FFN + 2 * c + 4)
            down_act(1)

            norm_act(2, C_ODD + 2)
            for c in range(H):
                prepare(C_ODD + c + 3)
            act.wait_ge(s_done, 16 * 7)


            def copy_v(c):
                act.wait_ge(s_rvt, 2 * c + 1)
                func(VR[:, :, c * IC:(c + 1) * IC], PB[2][:, :].rearrange("p (t n) -> p t n", n=IC), ACT.Copy)\
                    .then_inc(s_rve, 1)
                act.wait_ge(s_rvt, 2 * c + 2)
                if c >= 2:
                    act.wait_ge(s_out, 4 * (c - 1))
                func(V3[0:NS, c % 2, :], PB[3][0:NS, 0:IC], ACT.Copy)
                func(V3[64:64 + NS, c % 2, :], PB[3][0:NS, 0:IC], ACT.Copy).then_inc(s_rve, 1)

            for c in range(H + 3):
                if c < H:
                    for j in range(2):
                        n = 2 * c + j
                        act.wait_ge(s_rv, n + 1)
                        func(FV[:, n % 4, :], PB[n % 2][:, 0:T], ACT.Copy).then_inc(s_rvf, 1)
                if c == 0:
                    act.wait_ge(s_zero, 3)
                    act.wait_ge(s_ks, 1)
                    for i in range(2):
                        func(KS[0:NS, i * 512:(i + 1) * 512], PB[4 + i][0:NS, :], ACT.Copy)
                        func(KS[32:32 + NS, i * 512:(i + 1) * 512], PB[4 + i][0:NS, :], ACT.Copy).then_inc(s_kse, 1)
                if 1 <= c <= H:
                    copy_v(c - 1)
                if c < H:
                    prepare(C_ODD + 8 + c + 3)
                if c >= 3:
                    h = c - 3
                    act.wait_ge(s_os, h + 1)
                    func(OS[:, h, :], PB[7][:, 0:2 * NS], ACT.Copy).then_inc(s_ose, 1)
            for i in (2, 3):
                act.wait_ge(s_sto[i], 16 * H // 4)
            kdecay = const_("kdecay")
            for h in range(H):
                act.wait_ge(s_kt, h + 1)
                if h >= 2:
                    act.wait_ge(s_rp, h - 1)
                for m in range(2):
                    last = func(KD[:, h % 2, m * P:(m + 1) * P], PB[2 + h % 2][:, m * P:(m + 1) * P], ACT.Copy,
                                scale=kdecay[:, 2 * h + m:2 * h + m + 1])
                last.then_inc(s_kde, 1)
                for j in range(2):
                    act.wait_ge(s_o, 2 * h + j + 1)
                    func(O[:, 2 * h + j, 0:SEQ], PB[4 + 2 * (h % 2) + j][:, 0:SEQ], ACT.Copy).then_inc(s_oe, 1)
            def squares(h):
                act.wait_ge(s_od, h + 1)
                if h >= 2:
                    act.wait_ge(s_ov, h - 1)
                func(OQ[:, h % 2], OD[:, h % 2], ACT.Square).then_inc(s_oq, 1)

            squares(0)
            for h in range(H):
                act.wait_ge(s_ov, h + 1)
                if h >= 2:
                    act.wait_ge(s_on, 2 * (h - 1))
                func(RS[:, h % 2, :], PB[2 + h % 2][:, 0:T], ACT.Sqrt, bias=eps).then_inc(s_ort, 1)
                if h + 1 < H:
                    squares(h + 1)
                for j in range(2):
                    n = 2 * h + j
                    act.wait_ge(s_g, n + 1)
                    if n >= 2:
                        act.wait_ge(s_y, n - 1)
                    func(R2[:, n % 2, :], PB[4 + n % 4][:, 0:T], ACT.Silu).then_inc(s_gs, 1)
                prepare(C_ODD + 16 + h + 3)
                for j in range(2):
                    n = 2 * h + j
                    act.wait_ge(s_y, n + 1)
                    func(YH[:, n, :], O[:, n, :], ACT.Copy).then_inc(s_yh, 1)
            down_act(2)

            def high_moe(it, c):
                q = C_MOE + c
                n = slot_of(q)
                act.wait_ge(s_ring[n], it * (16 * MCH // MRING) + 16 * uses_before(q))
                if c >= WRING:
                    signal, count, per_item = through(c - WRING)
                    act.wait_ge(signal, it * per_item + count)
                elif isinstance(it, int):
                    act.wait_ge(*released[q - WRING])
                else:
                    signal, count, per_item = through(MCH + c - WRING)
                    act.wait_ge(signal, it * per_item + (count - per_item))
                func(WH[:, q % WRING, :], chunk(q), ACT.Copy).then_inc(s_hi, 1)

            norm_act(3, C_MOE - 1)
            for i in range(2 * NT):
                t, half = i // 2, i % 2
                act.wait_ge(s_ht2, i + 1)
                func(HXH[0:TOK[t], t, half * 512:(half + 1) * 512], PB[2 + i][0:TOK[t], :], ACT.Copy)\
                    .then_inc(s_hx, 1)
                if i == 1:
                    act.wait_ge(s_lgx, 1)
                    func(GE[:, :, 0], MX[:, :, 2], ACT.Exp).then_inc(s_e2, 1)
            for c in range(WRING):
                high_moe(0, c)
            act.wait_ge(s_items, 1)
            n_items = act.value_load(EII[0:1, TI_N:TI_N + 1], min_val=E, max_val=MAXI)

            def copy_gathered(it, part):
                for i in range(2):
                    act.wait_ge(s_ga, it * 4 + 2 * part + i + 1)
                    func((XEH, XEL)[part][:, 4 * i:4 * i + 4, :],
                         PB[2 * part + i][:, :].rearrange("p (k n) -> p k n", n=P), ACT.Copy).then_inc(s_xe, 1)

            copy_gathered(0, 0)
            copy_gathered(0, 1)
            with act.Fori(0, n_items) as it:
                def turned(f):
                    act.wait_ge(s_at, it * MSTEPS + f + 1)
                    if f >= 2:
                        act.wait_ge(s_dn, it * MSTEPS + f - 1)
                    func(ATH[:, f % 2, :], PB[6 + f % 2][:, 0:2 * P], ACT.Copy).then_inc(s_ate, 1)

                done = WRING
                for f in range(MSTEPS):
                    for kind in ("gate", "up"):
                        n = min(PLACE[(kind, f)] + WRING, MCH - 1)
                        for c in range(done, n + 1):
                            high_moe(it, c)
                        done = max(done, n + 1)
                    act.wait_ge(s_mm, it * (2 * MSTEPS) + 2 * f + 2)
                    if f >= 2:
                        act.wait_ge(s_ac, it * MSTEPS + f - 1)
                    func(SI[:, f % 2, :], PB[2 + f % 2][:, 0:IC], ACT.Silu).then_inc(s_si, 1)
                    if f >= 1:
                        turned(f - 1)
                    if f >= 2:
                        n = min(PLACE[("down", f - 2)] + WRING, MCH - 1)
                        for c in range(done, n + 1):
                            high_moe(it, c)
                        done = max(done, n + 1)
                assert done == MCH
                copy_gathered(it + 1, 0)
                turned(MSTEPS - 1)
                copy_gathered(it + 1, 1)
                with act.If(it < n_items - 1):
                    for c in range(WRING):
                        high_moe(it + 1, c)
                act.wait_ge(s_dn, (it + 1) * MSTEPS)
                act.wait_ge(s_sca, it * DK + DK)
                for i in range(2):
                    func(YE[:, i * 512:(i + 1) * 512], PB[4 + i][:, :], ACT.Copy).then_inc(s_yee, 1)
            for i in range(2 * NT):
                t, half = i // 2, i % 2
                act.wait_ge(s_turn, DK + i + 1)
                func(YO[0:TOK[t], t, half * 512:(half + 1) * 512], PB[i][0:TOK[t], :], ACT.Copy).then_inc(s_yo, 1)

        @block.vector
        def _(dve):
            V = nc.vector
            steps = [0]

            def link(ins):
                steps[0] += 1
                ins.then_inc(s_dch, 1)
                dve.wait_ge(s_dch, steps[0])

            low = [0]

            def prepare(q):
                q = min(q, C_MOE - 1)
                for n in range(low[0], q + 1):
                    dve.wait_ge(s_hi, n + 1)
                    V.tensor_tensor(WL[:, n % WRING, 0:size(n)], chunk(n)[:, 0:size(n)],
                                    full(WH[:, n % WRING, 0:size(n)]), ALU.subtract).then_inc(s_lo, 1)
                low[0] = max(low[0], q + 1)

            def norm_dve(r, gain, q):
                prepare(q)
                dve.wait_ge(s_rt, r + 1)
                link(V.reciprocal(RS[:, 1, :], RS[:, 0, :]))
                g = param_(gain)
                lag = 1 if r in (1, 2) else DK
                for k in range(DK + lag):
                    if k < DK:
                        V.scalar_tensor_tensor(out=HT[:, k, :], in0=XT[:, k, :], scalar=g[:, k:k + 1],
                                               in1=RS[:, 1, :], op0=ALU.mult, op1=ALU.mult).then_inc(s_ht, 1)
                    if r < 3 and k >= lag:
                        i = k - lag
                        dve.wait_ge(s_hh, DK * r + i + 1)
                        V.tensor_tensor(HL[:, i, :], HT[:, i, :], full(HH[:, i, :]), ALU.subtract).then_inc(s_hl, 1)

            def add_down(d):
                q, _, kt, before = DOWN[d]
                n = len(down_parts(kt))
                for half in range(2):
                    prepare(q + n * (half + 1) + (1 if half else 2))
                    dve.wait_ge(s_down, before + n * (half + 1))
                    for j in range(4):
                        x = XT[:, 4 * half + j, :]
                        V.tensor_tensor(x, x, PB[4 * (1 - half) + j][:, 0:T], ALU.add).then_inc(s_xt, 1)

            for k in range(DK):
                dve.wait_ge(s_turn, k + 1)
                V.tensor_copy(XT[:, k, :], PB[k % 4][:, 0:T]).then_inc(s_xt, 1)
            norm_dve(0, "g0", 0)
            prepare(C_EVEN + 3)
            dve.wait_ge(s_win, CT)
            for c in range(CT):
                dve.wait_ge(s_sig, c + 1)
                bank = PB[4 * (c // 2) + c % 2]
                V.tensor_tensor(U[:, c, W - 1:W - 1 + SEQ], bank[:, 0:SEQ], SG[:, c, 0:SEQ], ALU.mult)
                V.tensor_tensor(UF[:, c, :, W - 1], bank[:, SEQ:T], SG[:, c, SEQ:T], ALU.mult).then_inc(s_u, 1)
                if c == 1:
                    prepare(C_EVEN + 5)
            prepare(C_EVEN + 6)
            dve.wait_ge(s_u, CT)
            dve.wait_ge(s_zero, 1)
            cw = param_("conv_w").rearrange("p (c w) -> p c w", w=W)
            cb = param_("conv_b")
            before = steps[0]
            for w in range(W):
                for c in (2, 3):
                    u = U[:, c, w:w + SEQ]
                    if w == 0:
                        V.tensor_scalar(CA[:, c, 0:SEQ], u, cw[:, c, w:w + 1], cb[:, c:c + 1], ALU.mult, ALU.add)\
                            .then_inc(s_dch, 1)
                    else:
                        dve.wait_ge(s_dch, before + 2 * (w - 1) + c - 1)
                        V.scalar_tensor_tensor(out=CA[:, c, 0:SEQ], in0=u, scalar=cw[:, c, w:w + 1],
                                               in1=CA[:, c, 0:SEQ], op0=ALU.mult, op1=ALU.add).then_inc(s_dch, 1)
                if w % 5 == 4:
                    prepare(min(C_EVEN + 12, C_EVEN + 7 + w // 5))
            steps[0] = before + 2 * W
            for c in range(CT):
                last = V.tensor_tensor(SW[:, c], UF[:, c], cw[:, c:c + 1, :].to_broadcast([P, NS, W]), ALU.mult)
            link(last)
            link(V.tensor_reduce(CA[:, :, SEQ:T], SW[:], AX.X, ALU.add))
            for c in range(CT):
                last = V.tensor_scalar(CA[:, c, SEQ:T], CA[:, c, SEQ:T], cb[:, c:c + 1], None, ALU.add)
            link(last)
            for n in range(2 * HP):
                dve.wait_ge(s_qrt, n + 1)
                link(V.reciprocal(RS[:, n % 2, :], RS[:, n % 2, :]))
                V.scalar_tensor_tensor(out=QN[:, n, :], in0=QR[:, n, :], scalar=param_("q_g" if n < HP else "k_g"),
                                       in1=RS[:, n % 2, :], op0=ALU.mult, op1=ALU.mult).then_inc(s_qn, 1)
            zs = Z[:, ZP:ZP + ZS].rearrange("p (g b h) -> p g b h", b=NS, h=H)
            for b in range(NS):
                dve.wait_ge(s_kv[b % 4], 32 * (1 + b // 4))
                dve.wait_ge(s_qb, b + 1)
                slot = b * PAGES % NS
                V.tensor_tensor(KQ[:], KV[:, slot:slot + PAGES, :],
                                PB[5 + b % 3][:, 0:SBW].rearrange("p (o n) -> p o n", o=1)
                                .to_broadcast([P, PAGES, SBW]), ALU.mult).then_inc(s_kq, 1)
                dve.wait_ge(s_kq, b + 1)
                link(V.tensor_reduce(zs[:, :, b, :], KQ[:].rearrange("p g (h d) -> p g h d", d=HD), AX.X, ALU.add))
            V.scalar_tensor_tensor(out=Z[:, ZP:ZP + ZS].rearrange("p (g h) -> p g h", h=H),
                                   in0=Z[:, ZP:ZP + ZS].rearrange("p (g h) -> p g h", h=H), scalar=HD ** -0.5,
                                   in1=param_("bias").rearrange("p (o h) -> p o h", o=1)
                                   .to_broadcast([P, PAGES * NS, H]), op0=ALU.mult, op1=ALU.add).then_inc(s_zs, 1)
            below = const_("below").rearrange("p (a b n) -> p a b n", a=1, b=1)

            def mask(buf, g, done):
                v = buf[:, g * ZP // 2:(g + 1) * ZP // 2].rearrange("p (h c n) -> p h c n", h=4, c=3)[:, :, 0:3:2, :]
                V.tensor_tensor(v, v, below.to_broadcast([P, 4, 2, P]), ALU.mult).then_inc(done, 1)

            for g in range(2):
                part = slice(g * ZP // 2, ZP // 2 if g == 0 else ZP + ZS)
                dve.wait_ge(s_ln, g + 1)
                link(V.scalar_tensor_tensor(out=A[:, part], in0=Z[:, part], scalar=0.0, in1=L[:, 0:part.stop - part.start],
                                            op0=ALU.min, op1=ALU.subtract))
                link(V.scalar_tensor_tensor(out=Z[:, part], in0=Z[:, part], scalar=0.0, in1=L[:, 0:part.stop - part.start],
                                            op0=ALU.max, op1=ALU.add))
                mask(Z, g, s_lk)
                if g == 0:
                    dve.wait_ge(s_cm, 1)
                    V.tensor_tensor(CD, CA[:], PB[4][:, 0:T].rearrange("p (o n) -> p o n", o=1)
                                    .to_broadcast([P, CT, T]), ALU.subtract).then_inc(s_cd, 1)
            for h in range(H + 1):
                dve.wait_ge(s_suf, h + 1)
                n = ZW if h < H else ZS
                a = A[:, h * ZW:h * ZW + n]
                V.tensor_tensor(a, a, PB[h % 4][:, 0:n], ALU.add).then_inc(s_la, 1)
            for g in range(2):
                dve.wait_ge(s_exp, g + 1)
                mask(A, g, s_a)
            dve.wait_ge(s_cd, 1)
            dve.wait_ge(s_crt, 1)
            link(V.reciprocal(RS[:, 0, :], RS[:, 0, :]))
            for c in range(CT):
                V.scalar_tensor_tensor(out=CD[:, c, :], in0=CD[:, c, :], scalar=param_("ln_g")[:, c:c + 1],
                                       in1=RS[:, 0, :], op0=ALU.mult, op1=ALU.mult).then_inc(s_cn, 1)
            for hp in range(HP):
                dve.wait_ge(s_av, 2 * hp + 2)
                V.tensor_copy(MIX[:, CT + hp, 0:SEQ], PB[4 + hp][:, 0:SEQ]).then_inc(s_mixa, 1)
            dve.wait_ge(s_avs, NS)
            avs = PB[0][:, 0:HP * NS * 2].rearrange("p (a b i) -> p a b i", b=NS, i=2)
            for i in range(2):
                V.tensor_copy(MIX[i * HD:(i + 1) * HD, CT:CT + HP, SEQ:T], avs[i * HD:(i + 1) * HD, :, :, i])\
                    .then_inc(s_mixa, 1)
            dve.wait_ge(s_mixa, HP + 2)
            for k in range(DK):
                dve.wait_ge(s_mh, k + 1)
                V.tensor_tensor(HL[:, k, :], MIX[:, k, :], full(HH[:, k, :]), ALU.subtract).then_inc(s_ml, 1)
            add_down(0)

            norm_dve(1, "g1", C_FFN + 2)
            for c in range(FF // IC):
                prepare(C_FFN + 2 * c + 3)
                for j in range(2):
                    i = 2 * c + j
                    dve.wait_ge(s_gu, 4 * c + 2 + j + 1)
                    dve.wait_ge(s_silu, i + 1)
                    if c >= 1:
                        dve.wait_ge(s_hdl, i - 1)
                    V.tensor_tensor(HF[:, j, :], GA[:, j, :], PB[4 * (c % 2) + 2 + j][:, 0:T], ALU.mult)\
                        .then_inc(s_hid, 1)
                prepare(C_FFN + 2 * c + 4)
                for j in range(2):
                    i = 2 * c + j
                    dve.wait_ge(s_hdh, i + 1)
                    V.tensor_tensor(HDL[:, i, :], HF[:, j, :], full(HDH[:, i, :]), ALU.subtract).then_inc(s_hdl, 1)
            add_down(1)

            norm_dve(2, "g2", C_ODD + 2)
            dve.wait_ge(s_done, 16 * 7)
            V.memset(full(KS[0:96, :]), 0.0).then_inc(s_zero, 1)
            V.memset(full(V3[0:96, :, :]), 0.0).then_inc(s_zero, 1)
            cos, sin = (const_(x).rearrange("p (a n) -> p a n", a=2) for x in ("cos", "sin"))
            for n in range(2 * H):
                g, h = n // H, n % H
                dve.wait_ge(s_rq, n + 1)
                bank = PB[n % 4]
                if n >= 2:
                    dve.wait_ge(s_rot, n - 1)
                V.tensor_tensor(R1[:, n % 2, :], bank[:, 0:T], cos[:, g, :], ALU.mult)
                V.tensor_tensor(R2[0:HD, n % 2, :], bank[HD:P, 0:T], sin[HD:P, g, :], ALU.mult)
                link(V.tensor_tensor(R2[HD:P, n % 2, :], bank[0:HD, 0:T], sin[0:HD, g, :], ALU.mult))
                V.tensor_tensor((QT, KT)[g][:, h, :], R1[:, n % 2, :], R2[:, n % 2, :], ALU.add).then_inc(s_rot, 1)
                if n % 2:
                    prepare(C_ODD + 3 + n // 2)

            def spread_k(h):
                if h >= 1:
                    dve.wait_ge(s_out, 4 * h)
                V.tensor_tensor(KM[0:96, :].rearrange("p (b n) -> p b n", n=P),
                                full(KS[0:96, h * P:(h + 1) * P]).rearrange("p (o n) -> p o n", o=1)
                                .to_broadcast([96, NS, P]),
                                const_("sample", 96).rearrange("p (b o) -> p b o", o=1).to_broadcast([96, NS, P]),
                                ALU.mult).then_inc(s_km, 1)

            for c in range(H + 2):
                if c == 0:
                    for i in range(2):
                        dve.wait_ge(s_kse, i + 1)
                        cols = slice(i * 512, (i + 1) * 512)
                        V.tensor_tensor(KS[64:64 + NS, cols], PB[4 + i][0:NS, :], full(KS[0:NS, cols]),
                                        ALU.subtract).then_inc(s_ksl, 1)
                    dve.wait_ge(s_ksl, 2)
                if 1 <= c <= H:
                    dve.wait_ge(s_rve, 2 * c)
                    b = (c - 1) % 2
                    V.tensor_tensor(V3[32:32 + NS, b, :], PB[3][0:NS, 0:IC], full(V3[0:NS, b, :]), ALU.subtract)\
                        .then_inc(s_v3l, 1)
                if c < H:
                    prepare(C_ODD + 8 + c + 2)
                if c >= 2:
                    h = c - 2
                    dve.wait_ge(s_state[h % 4], 32 + 16 * (h // 4 + 1))
                    for g in range(4):
                        u = 4 * h + g
                        dve.wait_ge(s_out, u + 1)
                        s = ST[h % 4][:, g * 512:(g + 1) * 512]
                        V.scalar_tensor_tensor(out=s, in0=s, scalar=GAMMA[h], in1=PB[4 + u % 3][:, :],
                                               op0=ALU.mult, op1=ALU.add).then_inc(s_new, 1)
                if 1 <= c <= H:
                    spread_k(c - 1)
                if c < H:
                    prepare(C_ODD + 8 + c + 3)
            dve.wait_ge(s_decay, 16)
            for h in range(H):
                dve.wait_ge(s_sc, h + 1)
                if h >= 2:
                    dve.wait_ge(s_o, 2 * (h - 1))
                V.tensor_tensor(SC[:, h % 2, 0:SEQ], PB[h % 2][:, 0:SEQ], DT[:, h, :], ALU.mult)
                V.tensor_tensor(SC[:, h % 2, SEQ:ZW], PB[h % 2][:, SEQ:ZW], DT[:, h, 0:P], ALU.mult)\
                    .then_inc(s_sce, 1)
                dve.wait_ge(s_rp, h + 1)
                if h >= 2:
                    dve.wait_ge(s_rpo[h % 2], 16 * (h // 2))
                V.tensor_copy(RP[:, h % 2, :], PB[2 + h % 2][:, EV:2 * EV]).then_inc(s_rpe, 1)

            for i in (2, 3):
                dve.wait_ge(s_sto[i], 16 * H // 4)
            dve.wait_ge(s_ose, H)
            V.tensor_copy(O[:, :, SEQ:T], OS[:, :, :].rearrange("p h (j b) -> p (h j) b", b=NS)).then_inc(s_osc, 1)
            dve.wait_ge(s_osc, 1)

            def centre(h):
                dve.wait_ge(s_om, h + 1)
                if h >= 2:
                    dve.wait_ge(s_on, 2 * (h - 1))
                V.tensor_tensor(OD[:, h % 2], O[:, 2 * h:2 * h + 2, :],
                                PB[h % 2][:, 0:T].rearrange("p (o n) -> p o n", o=1).to_broadcast([P, 2, T]),
                                ALU.subtract).then_inc(s_od, 1)

            centre(0)
            for h in range(H):
                dve.wait_ge(s_od, h + 1)
                dve.wait_ge(s_ort, h + 1)
                link(V.reciprocal(RS[:, h % 2, :], RS[:, h % 2, :]))
                for j in range(2):
                    n = 2 * h + j
                    V.scalar_tensor_tensor(out=O[:, n, :], in0=OD[:, h % 2, j, :],
                                           scalar=param_("gn_g")[:, n:n + 1], in1=RS[:, h % 2, :],
                                           op0=ALU.mult, op1=ALU.mult).then_inc(s_on, 1)
                if h + 1 < H:
                    centre(h + 1)
                for j in range(2):
                    n = 2 * h + j
                    dve.wait_ge(s_on, n + 1)
                    dve.wait_ge(s_gs, n + 1)
                    V.scalar_tensor_tensor(out=O[:, n, :], in0=O[:, n, :], scalar=param_("gn_b")[:, n:n + 1],
                                           in1=R2[:, n % 2, :], op0=ALU.add, op1=ALU.mult).then_inc(s_y, 1)
                prepare(C_ODD + 16 + h + 3)
                for j in range(2):
                    n = 2 * h + j
                    dve.wait_ge(s_yh, n + 1)
                    V.tensor_tensor(YL[:, n, :], O[:, n, :], full(YH[:, n, :]), ALU.subtract).then_inc(s_yl, 1)
            add_down(2)

            norm_dve(3, "g3", C_MOE - 1)
            dve.wait_ge(s_down, NDOWN)
            V.memset(LG[:], 0.0)
            dve.wait_ge(s_lf, 1)
            V.tensor_copy(LF[0:E, :], PB[0][0:E, 0:T]).then_inc(s_lfe, 1)
            dve.wait_ge(s_lg, 1)
            V.tensor_copy(LG[:, 0:2, :], PB[1][:, P:P + 2 * E].rearrange("p (t e) -> p t e", e=E))
            link(V.tensor_copy(LG[0:NS, 2, :], PB[1][0:NS, P + 2 * E:P + NT * E]))
            for t in range(NT):
                last = V.max(MX[:, t, :], LG[:, t, :])
            link(last)
            for t in range(NT):
                last = V.max_index(MI[:, t, :], MX[:, t, :], LG[:, t, :])
            link(last)
            V.tensor_tensor(MX[:, :, 2], MX[:, :, 1], MX[:, :, 0], ALU.subtract).then_inc(s_lgx, 1)
            link(V.tensor_copy(MIF[:], MI[:]))
            io8 = const_("iota8").rearrange("p (o e) -> p o e", o=1).to_broadcast([P, NT, E])
            V.tensor_tensor(S1[:], io8, MIF[:, :, 0:1].to_broadcast([P, NT, E]), ALU.is_equal)
            link(V.tensor_tensor(LT[:, 0:NT, :], io8, MIF[:, :, 1:2].to_broadcast([P, NT, E]), ALU.is_equal))
            link(V.tensor_tensor(SE[:], LT[:, 0:NT, :], S1[:], ALU.add))
            V.tensor_tensor(SE[:, 2, :], SE[:, 2, :], C[:, CONST["rows"][0]:CONST["rows"][0] + 1]
                            .to_broadcast([P, E]), ALU.mult).then_inc(s_sel, 1)
            dve.wait_ge(s_e2, 1)
            link(V.tensor_scalar(GE[:, :, 1], GE[:, :, 0], 1.0, None, ALU.add))
            link(V.reciprocal(GE[:, :, 2], GE[:, :, 1]))
            link(V.tensor_tensor(GE[:, :, 3], GE[:, :, 2], GE[:, :, 0], ALU.mult))
            GT = M1[:, 0:NT, :]
            G2 = M2[:, 0:NT, :]
            V.tensor_tensor(GT, S1[:], GE[:, :, 2:3].to_broadcast([P, NT, E]), ALU.mult)
            link(V.tensor_tensor(G2, LT[:, 0:NT, :], GE[:, :, 3:4].to_broadcast([P, NT, E]), ALU.mult))
            link(V.tensor_tensor(LG[:], GT, G2, ALU.add))

            def low_x(i):
                t, half = i // 2, i % 2
                cols = slice(half * 512, (half + 1) * 512)
                dve.wait_ge(s_hx, i + 1)
                V.tensor_tensor(HXL[0:TOK[t], t, cols], PB[2 + i][0:TOK[t], :], full(HXH[0:TOK[t], t, cols]),
                                ALU.subtract).then_inc(s_hxl, 1)

            low_x(0)
            low_x(1)
            dve.wait_ge(s_sel, 1)
            dve.wait_ge(s_rk, 1)
            rank = PB[1][:, 0:NT * E].rearrange("p (t e) -> p t e", e=E)
            count = PB[1][:, 32:32 + NT * E].rearrange("p (t e) -> p e t", e=E)
            V.scalar_tensor_tensor(out=RK[:], in0=rank, scalar=1000.0, in1=SE[:], op0=ALU.add, op1=ALU.mult)
            link(V.tensor_reduce(TI[:, 5, :], count, AX.X, ALU.add))
            V.tensor_scalar(RK[:], RK[:], -1000.0, None, ALU.add)
            V.tensor_scalar(TI[:, 0, :], TI[:, 5, :], 128.5, None, ALU.is_gt)
            link(V.tensor_scalar(TI[:, 1, :], TI[:, 5, :], 256.5, None, ALU.is_gt))
            link(V.scalar_tensor_tensor(out=TI[:, 2, :], in0=TI[:, 0, :], scalar=1.0, in1=TI[:, 1, :],
                                        op0=ALU.add, op1=ALU.add))
            V.tensor_reduce(EI[:, TI_N:TI_N + 1], TI[:, 2, :], AX.X, ALU.add)
            link(V.tensor_tensor(LT[:], const_("lt8").rearrange("p (a b) -> p a b", b=E),
                                 TI[:, 2:3, :].to_broadcast([P, E, E]), ALU.mult))
            link(V.tensor_reduce(TI[:, 3, :], LT[:], AX.X, ALU.add))
            item = const_("item").rearrange("p (i e) -> p i e", e=E)
            V.tensor_tensor(TI[:, 4, :], TI[:, 3, :], TI[:, 2, :], ALU.add)
            V.tensor_tensor(M3[:], item, TI[:, 3:4, :].to_broadcast([P, TI_N, E]), ALU.subtract)
            link(V.tensor_tensor(M1[:], item, TI[:, 3:4, :].to_broadcast([P, TI_N, E]), ALU.is_ge))
            link(V.tensor_tensor(M2[:], item, TI[:, 4:5, :].to_broadcast([P, TI_N, E]), ALU.is_lt))
            link(V.tensor_tensor(M1[:], M1[:], M2[:], ALU.mult))
            each_tile = M1[:].rearrange("p (o i) e -> p o i e", o=1).to_broadcast([P, NT, TI_N, E])
            link(V.tensor_tensor(M2[:], const_("expert").rearrange("p (i e) -> p i e", e=E), M1[:], ALU.mult))
            V.tensor_reduce(EI[:, 0:TI_N], M2[:], AX.X, ALU.add)
            link(V.tensor_tensor(M3[:], M3[:], M1[:], ALU.mult))
            V.tensor_copy(EII[:], EI[:, :]).then_inc(s_items, 1)
            V.tensor_reduce(BA[:, :], M3[:], AX.X, ALU.add)
            for src, m in ((RK, M4), (LG, M5)):
                m = m[:].rearrange("p t (i e) -> p t i e", e=E)
                last = V.tensor_tensor(m, each_tile, src[:].rearrange("p t (o e) -> p t o e", o=1)
                                       .to_broadcast([P, NT, TI_N, E]), ALU.mult)
            link(last)
            for m, dst in ((M4, CR), (M5, CG)):
                last = V.tensor_reduce(dst[:].rearrange("p i t -> p t i"),
                                       m[:].rearrange("p t (i e) -> p t i e", e=E), AX.X, ALU.add)
            link(last)
            link(V.scalar_tensor_tensor(out=CR[:], in0=BA[:].rearrange("p (i o) -> p i o", o=1)
                                        .to_broadcast([P, TI_N, NT]), scalar=-128.0, in1=CR[:],
                                        op0=ALU.mult, op1=ALU.add))
            dve.wait_ge(s_items, 1)
            for i in range(2, 2 * NT):
                low_x(i)
            n_items = dve.value_load(EII[0:1, TI_N:TI_N + 1], min_val=E, max_val=MAXI)
            slot = const_("slot")

            def low_moe(it, c):
                q = C_MOE + c
                dve.wait_ge(s_hi, it * MCH + (q + 1))
                V.tensor_tensor(WL[:, q % WRING, :], chunk(q), full(WH[:, q % WRING, :]), ALU.subtract)\
                    .then_inc(s_lo, 1)

            base = steps[0]

            def one_hot(it):
                if not isinstance(it, int):
                    dve.wait_ge(s_oh, it)
                V.tensor_copy(CU[:, 0:1, :], CR[:, bass.ds(it, 1), :]).then_inc(s_dch, 1)
                V.tensor_copy(CU[:, 1:2, :], CG[:, bass.ds(it, 1), :]).then_inc(s_dch, 1)
                dve.wait_ge(s_dch, it * 2 + (base + 2))
                for t in range(NT):
                    V.tensor_scalar(OH[:, t, :], slot, CU[:, 0, t:t + 1], None, ALU.is_equal)
                    last = V.tensor_scalar(OG[:, t, :], slot, CU[:, 0, t:t + 1], CU[:, 1, t:t + 1], ALU.is_equal,
                                           ALU.mult)
                last.then_inc(s_oh, 1)

            one_hot(0)
            V.memset(YE[:, 0:512], 0.0).then_inc(s_yee, 1)
            V.memset(YE[:, 512:D], 0.0).then_inc(s_yee, 1)
            V.memset(OT[:, :], 0.0).then_inc(s_ot, 1)
            for c in range(WRING):
                low_moe(0, c)
            with dve.Fori(0, n_items) as it:
                def turned(f):
                    dve.wait_ge(s_ate, it * MSTEPS + f + 1)
                    V.tensor_tensor(ATL[:, f % 2, :], PB[6 + f % 2][:, 0:2 * P], full(ATH[:, f % 2, :]),
                                    ALU.subtract).then_inc(s_atl, 1)

                done = WRING
                for f in range(MSTEPS):
                    for kind in ("gate", "up"):
                        n = min(PLACE[(kind, f)] + WRING, MCH - 1)
                        for c in range(done, n + 1):
                            low_moe(it, c)
                        done = max(done, n + 1)
                    dve.wait_ge(s_si, it * MSTEPS + f + 1)
                    if f >= 2:
                        dve.wait_ge(s_at, it * MSTEPS + f - 1)
                    V.tensor_tensor(AC[:, f % 2, :], SI[:, f % 2, :], PB[2 + f % 2][:, IC:2 * IC], ALU.mult)\
                        .then_inc(s_ac, 1)
                    if f <= 1:
                        for k in range(4 * f, 4 * f + 4):
                            dve.wait_ge(s_sca, it * DK + k + 1)
                            V.tensor_tensor(XT[:, k, :], XT[:, k, :], PB[SCATTER[k % 4]][:, 0:T], ALU.add)\
                                .then_inc(s_add, 1)
                    if f == 1:
                        dve.wait_ge(s_oht, it + 1)
                        V.tensor_copy(OT[:, :], PB[7][:, 0:T]).then_inc(s_ot, 1)
                    if f == 6:
                        one_hot(it + 1)
                    if f >= 1:
                        turned(f - 1)
                    if f >= 2:
                        n = min(PLACE[("down", f - 2)] + WRING, MCH - 1)
                        for c in range(done, n + 1):
                            low_moe(it, c)
                        done = max(done, n + 1)
                turned(MSTEPS - 1)
                with dve.If(it < n_items - 1):
                    for c in range(WRING):
                        low_moe(it + 1, c)
            for k in range(DK):
                dve.wait_ge(s_sca, n_items * DK + k + 1)
                V.tensor_tensor(XT[:, k, :], XT[:, k, :], PB[SCATTER[k % 4]][:, 0:T], ALU.add).then_inc(s_add, 1)


def tables():
    C = np.zeros((P, NCONST), np.float32)
    p = np.arange(P)

    def put(name, a):
        at, n = CONST[name]
        C[:, at:at + n] = np.broadcast_to(np.asarray(a, np.float64), (P, n))

    put("ident", np.eye(P))
    put("negtri", -(p[:, None] > p[None, :]).astype(float))
    put("negones", -1.0)
    put("below", (p[:, None] < p[None, :]).astype(float))
    put("ones", 1.0)
    put("mean_d", 1.0 / D)
    put("mean_ch", 1.0 / CH)
    put("mean_hd", (p[:, None] // HD == p[None, :] // HD) / HD)
    put("mean_ev", 1.0 / EV)
    half = P // 2
    inv = np.float32(10000.0) ** (-np.linspace(0.0, 1.0, half, dtype=np.float32))
    pos = np.concatenate([np.arange(SEQ), np.full(NS, PAST)]).astype(np.float32)
    ang = (pos[None, :] * inv[:, None]).astype(np.float32)
    cos, sin = np.cos(ang), np.sin(ang)
    scale = np.float32(P) ** np.float32(-0.5)
    put("cos", np.concatenate([np.concatenate([cos, cos]), np.concatenate([cos, cos]) * scale], axis=1))
    put("sin", np.concatenate([np.concatenate([sin, -sin]), np.concatenate([sin, -sin]) * scale], axis=1))
    put("slot", p)
    gamma = np.array(GAMMA)
    put("kdecay", np.stack([gamma[h] ** (SEQ - 1 - (m * P + p)) for h in range(H) for m in range(2)], axis=1))
    e = np.arange(E)
    put("iota8", e)
    put("lt8", (e[None, :] < e[:, None]).astype(float).ravel())
    put("item", np.repeat(np.arange(TI_N), E))
    put("expert", np.tile(e, TI_N))
    put("eps", EPS)
    put("rows", (p < NS).astype(float)[:, None])
    put("sample", (p[:, None] % 32 == np.arange(NS)[None, :]).astype(float))
    key, query = np.meshgrid(np.arange(SEQ), np.arange(SEQ), indexing="ij")
    diff = query - key
    table = []
    for h in range(H):
        d = np.where(diff >= 0, gamma[h] ** np.maximum(diff, 0), 0.0)
        table.append(d[0:P])
    return C, np.concatenate(table, axis=1).astype(np.float32)


_OUTS = [(1, SEQ, D), (NS, 1, D), (1, 1, SEQ, H, HD), (1, 1, SEQ, H, HD), (1, NS, 1, H, HD), (1, NS, 1, H, HD),
         (1, 1, W - 1, CH), (1, NS, W - 1, CH), (1, 1, H, P, EV), (1, NS, H, P, EV)]
_INS = ["x_prompt", "x_sample", "cache_sb_k", "cache_sb_v", "cache_conv", "state_ret", "page_table"]
_WEIGHTS = ["w_in_even", "w_out_even", "ffn_w_gate", "ffn_w_up", "ffn_w_down", "w_in_odd", "w_out_odd",
            "moe_w_gate", "moe_w_up", "moe_w_down"]


def kernel(**inputs):
    import concourse.bacc as bacc
    from concourse.bass_utils import run_bass_kernel_spmd

    a = {k: np.asarray(v) for k, v in inputs.items()}
    const, decay = tables()

    def tiles(x):
        return x.reshape(-1, P).T

    param = np.concatenate([
        tiles(a["norm_mix_even"][0]), tiles(a["norm_ffn_even"][0]), tiles(a["norm_mix_odd"][0]),
        tiles(a["norm_ffn_odd"][0]), a["conv_w"][0].reshape(W, CT, P).transpose(2, 1, 0).reshape(P, CT * W),
        tiles(a["conv_b"][0]), tiles(a["conv_ln_g"][0]), tiles(a["conv_ln_b"][0]),
        np.tile(a["sb_q_norm"][0], 2)[:, None], np.tile(a["sb_k_norm"][0], 2)[:, None],
        np.broadcast_to(a["sb_bias"][0], (P, H)), tiles(a["ret_gn_g"][0]), tiles(a["ret_gn_b"][0]),
        a["router_w"][0].reshape(DK, P, E).transpose(1, 0, 2).reshape(P, DK * E)], axis=1)
    arrays = {n: a[n] for n in _INS}
    arrays.update(const=const, decay=decay, param=param)
    arrays.update({n: a[n] for n in _WEIGHTS})
    nc = bacc.Bacc("TRN2", target_bir_lowering=False, num_devices=1)
    feed, args = {}, []
    for name, x in arrays.items():
        x = np.ascontiguousarray(x)
        feed[f"in_{name}"] = x
        args.append(nc.dram_tensor(f"in_{name}", x.shape, mybir.dt.from_np(x.dtype), kind="ExternalInput").ap())
    names = ["y_prompt", "y_sample", "k_prompt", "v_prompt", "k_sample", "v_sample", "conv_prompt", "conv_sample",
             "ret_prompt", "ret_sample"]
    for name, shape in zip(names, _OUTS):
        args.append(nc.dram_tensor(f"out_{name}", shape, F32, kind="ExternalOutput").ap())
    build(nc, *args)
    r = run_bass_kernel_spmd(nc, [feed], core_ids=[0])
    return tuple(r.results[0][f"out_{name}"] for name in names)
```
